# Optimizing a Trainium2 kernel written in Bass

```python
import jax, jax.numpy as jnp
from jax import lax
import numpy as np

D_MODEL = 1024
BATCH = 1
SEQ = 256
DEPTH = 1

GRID_W = 64
CTX_LEN = 256
RET_HEADS = 4
RET_DK = 128
RET_DV = 128
RET_CHUNK = 128
WIN_HEADS = 8
WIN_KV_HEADS = 2
WIN_HEAD_DIM = 64
WINDOW = 128
WIN_BLOCK = 128
NA_HEADS = 8
NA_HEAD_DIM = 64
NA_ROWS_MAX = 8
NA_COLS = 16
N_EXPERTS = 16
EXPERT_HIDDEN = 1024
CAPACITY_FACTOR = 2
N_BRANCHES = 3
N_MOD = 6
ROPE_BASE = 10000.0
EPS = 1e-6
NEG_INF = -1e30
RET_QK = RET_HEADS * RET_DK
RET_V = RET_HEADS * RET_DV
WIN_Q = WIN_HEADS * WIN_HEAD_DIM
WIN_KV = WIN_KV_HEADS * WIN_HEAD_DIM
NA_W = NA_HEADS * NA_HEAD_DIM
IN_SPLITS = (('q_r', RET_QK), ('k_r', RET_QK), ('v_r', RET_V), ('g_r', RET_V),
             ('q_w', WIN_Q), ('k_w', WIN_KV), ('v_w', WIN_KV),
             ('q_n', NA_W), ('k_n', NA_W), ('v_n', NA_W),
             ('gates', N_BRANCHES * D_MODEL))
IN_COLS = 2 * RET_QK + 2 * RET_V + WIN_Q + 2 * WIN_KV + 3 * NA_W + N_BRANCHES * D_MODEL
KV_NAMES = ('k_r', 'v_r', 'k_w', 'v_w', 'k_n', 'v_n')


def rms_norm(x, g):
    xf = x.astype(jnp.float32)
    y = xf * lax.rsqrt(jnp.mean(xf * xf, axis=-1, keepdims=True) + EPS)
    return (y * g.astype(jnp.float32)).astype(x.dtype)

def modulate(h, shift, scale):
    return h * (1 + scale[:, None, :]) + shift[:, None, :]

def column_layout():
    layout, off = {}, 0
    for name, size in IN_SPLITS:
        layout[name] = (off, size)
        off += size
    return layout

def split_columns(p):
    return {n: p[..., o:o + s] for n, (o, s) in column_layout().items()}

def heads(t, n_heads):
    return t.reshape(t.shape[0], t.shape[1], n_heads, -1)

def axial_rope(x):
    n, d = x.shape[1], x.shape[-1]
    nf = d // 4
    t = jnp.arange(n)
    row = (t // GRID_W).astype(jnp.float32)
    col = (t % GRID_W).astype(jnp.float32)
    inv = ROPE_BASE ** (-jnp.arange(nf, dtype=jnp.float32) / nf)
    ang = jnp.concatenate([row[:, None] * inv, col[:, None] * inv], axis=-1)
    cos = jnp.cos(ang)[None, :, None, :]
    sin = jnp.sin(ang)[None, :, None, :]
    xf = x.astype(jnp.float32)
    x1, x2 = xf[..., :d // 2], xf[..., d // 2:]
    return jnp.concatenate([x1 * cos - x2 * sin, x1 * sin + x2 * cos], axis=-1).astype(x.dtype)

def retention_final_state(k, v, log_gamma):
    n = k.shape[2]
    w = jnp.exp((n - 1 - jnp.arange(n, dtype=jnp.float32))[None, :] * log_gamma[:, None])
    return jnp.einsum('bhnd,bhne->bhde', k * w[None, :, :, None], v)

def retention_chunkwise(q, k, v, log_gamma, state0, include_diag):
    b, h, n, dk = q.shape
    dv = v.shape[-1]
    ch = RET_CHUNK
    nc = n // ch
    qc = q.reshape(b, h, nc, ch, dk)
    kc = k.reshape(b, h, nc, ch, dk)
    vc = v.reshape(b, h, nc, ch, dv)
    i = jnp.arange(ch, dtype=jnp.float32)
    diff = i[:, None] - i[None, :]
    lg = log_gamma[:, None, None]
    dmat = jnp.where(diff >= (0.0 if include_diag else 1.0), jnp.exp(jnp.maximum(diff, 0.0) * lg), 0.0)
    inner = jnp.einsum('bhnid,bhnjd->bhnij', qc, kc) * dmat[None, :, None]
    inner = jnp.einsum('bhnij,bhnje->bhnie', inner, vc)
    zeta = jnp.exp((ch - 1 - i)[None, :] * log_gamma[:, None])
    s = jnp.einsum('bhnjd,bhnje->nbhde', kc * zeta[None, :, None, :, None], vc)
    chunk_decay = jnp.exp(ch * log_gamma)[None, :, None, None]

    def step(r, s_n):
        return chunk_decay * r + s_n, r

    _, r_prev = lax.scan(step, state0, s)
    xi = jnp.exp((i + 1)[None, :] * log_gamma[:, None])
    cross = jnp.einsum('bhnid,nbhde->bhnie', qc, r_prev) * xi[None, :, None, :, None]
    return (inner + cross).reshape(b, h, n, dv)

def bidirectional_retention(q, k, v, lg_f, lg_b, state_f, state_b):
    flip = lambda t: jnp.flip(t, axis=2)
    fwd = retention_chunkwise(q, k, v, lg_f, state_f, True)
    bwd = retention_chunkwise(flip(q), flip(k), flip(v), lg_b, state_b, False)
    return fwd + flip(bwd)

def retention_readout(y, g, gn_gain):
    mu = jnp.mean(y, axis=-1, keepdims=True)
    var = jnp.mean(jnp.square(y - mu), axis=-1, keepdims=True)
    y = (y - mu) * lax.rsqrt(var + EPS)
    y = jnp.swapaxes(y, 1, 2).reshape(y.shape[0], y.shape[2], -1) * gn_gain.astype(jnp.float32)
    return (y * jax.nn.silu(g.astype(jnp.float32))).astype(g.dtype)

def retention_mixer(px, pc, decay_logit, gn_gain, need_ctx):
    lg_f = jax.nn.log_sigmoid(decay_logit[0].astype(jnp.float32))
    lg_b = jax.nn.log_sigmoid(decay_logit[1].astype(jnp.float32))
    to_bhnd = lambda t: jnp.swapaxes(t, 1, 2).astype(jnp.float32)
    k_scale = RET_DK ** -0.5
    qx = to_bhnd(axial_rope(heads(px['q_r'], RET_HEADS)))
    kx = to_bhnd(axial_rope(heads(px['k_r'], RET_HEADS))) * k_scale
    vx = to_bhnd(heads(px['v_r'], RET_HEADS))
    kc = to_bhnd(heads(pc['k_r'], RET_HEADS)) * k_scale
    vc = to_bhnd(heads(pc['v_r'], RET_HEADS))
    flip = lambda t: jnp.flip(t, axis=2)
    state_f = retention_final_state(kc, vc, lg_f)
    state_b = retention_final_state(flip(kc), flip(vc), lg_b)
    yx = retention_readout(bidirectional_retention(qx, kx, vx, lg_f, lg_b, state_f, state_b), px['g_r'], gn_gain)
    yc = None
    if need_ctx:
        qc = to_bhnd(heads(pc['q_r'], RET_HEADS))
        zero = jnp.zeros(state_f.shape, jnp.float32)
        yc = retention_readout(bidirectional_retention(qc, kc, vc, lg_f, lg_b, zero, zero), pc['g_r'], gn_gain)
    return yx, yc

def context_self_attention(q, k, v, sink):
    b, l, hq, d = q.shape
    hkv = k.shape[2]
    g = hq // hkv
    qg = q.reshape(b, l, hkv, g, d)
    s = jnp.einsum('bqhgd,bkhd->bhgqk', qg, k).astype(jnp.float32) * d ** -0.5
    if sink is not None:
        s_sink = jnp.broadcast_to(sink.astype(jnp.float32).reshape(1, hkv, g, 1, 1), s.shape[:-1] + (1,))
        s = jnp.concatenate([s, s_sink], axis=-1)
    p = jax.nn.softmax(s, axis=-1)[..., :l].astype(v.dtype)
    return jnp.einsum('bhgqk,bkhd->bqhgd', p, v).reshape(b, l, hq * d)

def banded_window_attention(q, k, v, kc, vc, sink):
    b, n, hq, d = q.shape
    hkv = k.shape[2]
    g = hq // hkv
    l = kc.shape[1]
    nb = n // WIN_BLOCK
    pad = ((0, 0), (WIN_BLOCK, WIN_BLOCK), (0, 0), (0, 0))

    def band(t):
        tb = jnp.pad(t, pad).reshape(b, nb + 2, WIN_BLOCK, hkv, d)
        return jnp.concatenate([tb[:, :-2], tb[:, 1:-1], tb[:, 2:]], axis=2)

    kb, vb = band(k), band(v)
    qb = q.reshape(b, nb, WIN_BLOCK, hkv, g, d)
    scale = d ** -0.5
    s_loc = jnp.einsum('bnqhgd,bnkhd->bnhgqk', qb, kb).astype(jnp.float32) * scale
    s_ctx = jnp.einsum('bnqhgd,blhd->bnhgql', qb, kc).astype(jnp.float32) * scale
    qpos = jnp.arange(WIN_BLOCK)[:, None]
    kpos = jnp.arange(3 * WIN_BLOCK)[None, :] - WIN_BLOCK
    kabs = jnp.arange(nb)[:, None, None] * WIN_BLOCK + kpos[None]
    valid = (jnp.abs(kpos - qpos) <= WINDOW)[None] & (kabs >= 0) & (kabs < n)
    s_loc = jnp.where(valid[None, :, None, None], s_loc, NEG_INF)
    s_sink = jnp.broadcast_to(sink.astype(jnp.float32).reshape(1, 1, hkv, g, 1, 1), s_ctx.shape[:-1] + (1,))
    p = jax.nn.softmax(jnp.concatenate([s_loc, s_ctx, s_sink], axis=-1), axis=-1)
    kl = 3 * WIN_BLOCK
    p_loc = p[..., :kl].astype(v.dtype)
    p_ctx = p[..., kl:kl + l].astype(v.dtype)
    out = jnp.einsum('bnhgqk,bnkhd->bnqhgd', p_loc, vb) + jnp.einsum('bnhgql,blhd->bnqhgd', p_ctx, vc)
    return out.reshape(b, n, hq * d)

def window_mixer(px, pc, sink, need_ctx):
    q = axial_rope(heads(px['q_w'], WIN_HEADS))
    k = axial_rope(heads(px['k_w'], WIN_KV_HEADS))
    v = heads(px['v_w'], WIN_KV_HEADS)
    kc = heads(pc['k_w'], WIN_KV_HEADS)
    vc = heads(pc['v_w'], WIN_KV_HEADS)
    yx = banded_window_attention(q, k, v, kc, vc, sink)
    yc = context_self_attention(heads(pc['q_w'], WIN_HEADS), kc, vc, sink) if need_ctx else None
    return yx, yc

def neighbourhood_attention(q, k, v, kc, vc, rpb):
    b, n, h, d = q.shape
    rows = n // GRID_W
    kr = min(NA_ROWS_MAX, rows)
    r = jnp.arange(rows)
    row_idx = jnp.clip(r - kr // 2, 0, rows - kr)[:, None] + jnp.arange(kr)[None, :]
    cq = jnp.arange(GRID_W)
    col_start = jnp.clip(cq - NA_COLS // 2, 0, GRID_W - NA_COLS)
    col_valid = (cq[None, :] >= col_start[:, None]) & (cq[None, :] < col_start[:, None] + NA_COLS)
    ri = row_idx - r[:, None] + NA_ROWS_MAX - 1
    ci = jnp.clip(cq[None, :] - cq[:, None], -(NA_COLS - 1), NA_COLS - 1) + NA_COLS - 1
    bias = rpb.astype(jnp.float32)[:, ri[:, None, :, None], ci[None, :, None, :]]
    qg = q.reshape(b, rows, GRID_W, h, d)
    k_rows = k.reshape(b, rows, GRID_W, h, d)[:, row_idx]
    v_rows = v.reshape(b, rows, GRID_W, h, d)[:, row_idx]
    scale = d ** -0.5
    s_loc = jnp.einsum('brchd,brkwhd->bhrckw', qg, k_rows).astype(jnp.float32) * scale + bias[None]
    s_loc = jnp.where(col_valid[:, None, :], s_loc, NEG_INF).reshape(b, h, rows, GRID_W, kr * GRID_W)
    s_ctx = jnp.einsum('brchd,blhd->bhrcl', qg, kc).astype(jnp.float32) * scale
    p = jax.nn.softmax(jnp.concatenate([s_loc, s_ctx], axis=-1), axis=-1)
    nl = kr * GRID_W
    p_loc = p[..., :nl].reshape(b, h, rows, GRID_W, kr, GRID_W).astype(v.dtype)
    p_ctx = p[..., nl:].astype(v.dtype)
    out = jnp.einsum('bhrckw,brkwhd->brchd', p_loc, v_rows) + jnp.einsum('bhrcl,blhd->brchd', p_ctx, vc)
    return out.reshape(b, n, h * d)

def na_mixer(px, pc, rpb, need_ctx):
    q = heads(px['q_n'], NA_HEADS)
    k = heads(px['k_n'], NA_HEADS)
    v = heads(px['v_n'], NA_HEADS)
    kc = heads(pc['k_n'], NA_HEADS)
    vc = heads(pc['v_n'], NA_HEADS)
    yx = neighbourhood_attention(q, k, v, kc, vc, rpb)
    yc = context_self_attention(heads(pc['q_n'], NA_HEADS), kc, vc, None) if need_ctx else None
    return yx, yc

def gated_merge(gates, ya, yb, yc, w_ret, w_win, w_na, w_out):
    ga, gb, gc = jnp.split(jax.nn.sigmoid(gates), N_BRANCHES, axis=-1)
    return (ga * (ya @ w_ret) + gb * (yb @ w_win) + gc * (yc @ w_na)) @ w_out

def hybrid_mixer(hx, hc, w_in, decay_logit, gn_gain, w_ret, sink, w_win, rpb, w_na, w_out, need_ctx):
    px = split_columns(hx @ w_in)
    if need_ctx:
        pc = split_columns(hc @ w_in)
    else:
        lay = column_layout()
        pc = {nm: hc @ w_in[:, lay[nm][0]:lay[nm][0] + lay[nm][1]] for nm in KV_NAMES}
    ya, yca = retention_mixer(px, pc, decay_logit, gn_gain, need_ctx)
    yb, ycb = window_mixer(px, pc, sink, need_ctx)
    yc, ycc = na_mixer(px, pc, rpb, need_ctx)
    mx = gated_merge(px['gates'], ya, yb, yc, w_ret, w_win, w_na, w_out)
    mc = gated_merge(pc['gates'], yca, ycb, ycc, w_ret, w_win, w_na, w_out) if need_ctx else None
    return mx, mc

def expert_choice_ffn(h, w_router, w_gate, w_up, w_down):
    b, n, d = h.shape
    cap = CAPACITY_FACTOR * n // N_EXPERTS
    aff = jax.nn.softmax((h @ w_router).astype(jnp.float32), axis=-1)
    gate, idx = lax.top_k(jnp.swapaxes(aff, 1, 2), cap)
    bidx = jnp.arange(b)[:, None, None]
    xe = h[bidx, idx]
    hid = jax.nn.silu(jnp.einsum('becd,edf->becf', xe, w_gate)) * jnp.einsum('becd,edf->becf', xe, w_up)
    ye = jnp.einsum('becf,efd->becd', hid, w_down) * gate[..., None].astype(h.dtype)
    return jnp.zeros_like(h).at[bidx, idx].add(ye)

def first_inputs(seed: int = 0) -> dict:
    key = jax.random.key(seed)
    ks = jax.random.split(key, 24)
    f32 = jnp.float32
    d = D_MODEL
    nrm = lambda k, shape, s: jax.random.normal(k, shape, f32) * s
    gamma0 = 1.0 - 2.0 ** (-5.0 - np.arange(RET_HEADS))
    logit0 = jnp.asarray(np.log(gamma0 / (1.0 - gamma0)).astype(np.float32))
    return {
        'x': nrm(ks[0], (BATCH, SEQ, d), 1.0),
        'c': nrm(ks[1], (BATCH, d), 1.0),
        'ctx': nrm(ks[2], (BATCH, CTX_LEN, d), 1.0),
        'c_ctx': nrm(ks[3], (d,), 1.0),
        'w_mod': nrm(ks[4], (DEPTH, d, N_MOD * d), 0.5 * d ** -0.5),
        'b_mod': nrm(ks[5], (DEPTH, N_MOD * d), 0.02),
        'g_mix': 1.0 + nrm(ks[6], (DEPTH, d), 0.02),
        'g_ffn': 1.0 + nrm(ks[7], (DEPTH, d), 0.02),
        'w_in': nrm(ks[8], (DEPTH, d, IN_COLS), d ** -0.5),
        'ret_decay_logit': logit0[None, None, :] + nrm(ks[9], (DEPTH, 2, RET_HEADS), 0.1),
        'ret_gn': 1.0 + nrm(ks[10], (DEPTH, RET_V), 0.02),
        'w_ret': nrm(ks[11], (DEPTH, RET_V, d), RET_V ** -0.5),
        'win_sink': nrm(ks[12], (DEPTH, WIN_HEADS), 1.0),
        'w_win': nrm(ks[13], (DEPTH, WIN_Q, d), WIN_Q ** -0.5),
        'na_rpb': nrm(ks[14], (DEPTH, NA_HEADS, 2 * NA_ROWS_MAX - 1, 2 * NA_COLS - 1), 0.1),
        'w_na': nrm(ks[15], (DEPTH, NA_W, d), NA_W ** -0.5),
        'w_out': nrm(ks[16], (DEPTH, d, d), d ** -0.5),
        'w_router': nrm(ks[17], (DEPTH, d, N_EXPERTS), d ** -0.5),
        'w_exp_gate': nrm(ks[18], (DEPTH, N_EXPERTS, d, EXPERT_HIDDEN), d ** -0.5),
        'w_exp_up': nrm(ks[19], (DEPTH, N_EXPERTS, d, EXPERT_HIDDEN), d ** -0.5),
        'w_exp_down': nrm(ks[20], (DEPTH, N_EXPERTS, EXPERT_HIDDEN, d), EXPERT_HIDDEN ** -0.5),
        'g_final': 1.0 + nrm(ks[21], (d,), 0.02),
    }

def first_block(x, c, ctx, c_ctx, w_mod, b_mod, g_mix, g_ffn, w_in, ret_decay_logit, ret_gn, w_ret,
              win_sink, w_win, na_rpb, w_na, w_out, w_router, w_exp_gate, w_exp_up, w_exp_down, g_final):
    d = x.shape[-1]
    sc = jax.nn.silu(c)
    scc = jax.nn.silu(c_ctx)[None]
    for layer in range(DEPTH):
        need_ctx = layer < DEPTH - 1
        mod_x = (sc @ w_mod[layer] + b_mod[layer]).reshape(-1, N_MOD, d)
        n_mod_c = N_MOD if need_ctx else 2
        mod_c = (scc @ w_mod[layer][:, :n_mod_c * d] + b_mod[layer][:n_mod_c * d]).reshape(1, n_mod_c, d)
        hx = modulate(rms_norm(x, g_mix[layer]), mod_x[:, 0], mod_x[:, 1])
        hc = modulate(rms_norm(ctx, g_mix[layer]), mod_c[:, 0], mod_c[:, 1])
        mx, mc = hybrid_mixer(hx, hc, w_in[layer], ret_decay_logit[layer], ret_gn[layer], w_ret[layer],
                              win_sink[layer], w_win[layer], na_rpb[layer], w_na[layer], w_out[layer], need_ctx)
        x = x + mod_x[:, 2, None] * mx
        hx = modulate(rms_norm(x, g_ffn[layer]), mod_x[:, 3], mod_x[:, 4])
        x = x + mod_x[:, 5, None] * expert_choice_ffn(hx, w_router[layer], w_exp_gate[layer],
                                                      w_exp_up[layer], w_exp_down[layer])
        if need_ctx:
            ctx = ctx + mod_c[:, 2, None] * mc
            hc = modulate(rms_norm(ctx, g_ffn[layer]), mod_c[:, 3], mod_c[:, 4])
            ctx = ctx + mod_c[:, 5, None] * expert_choice_ffn(hc, w_router[layer], w_exp_gate[layer],
                                                              w_exp_up[layer], w_exp_down[layer])
    return rms_norm(x, g_final)


DEPTH_2 = 2

N_MIXERS = 2
N_NSA_LAYERS = (DEPTH_2 + 1) // 2
N_RG_LAYERS = DEPTH_2 // 2

NSA_HEADS = 16
NSA_GROUPS = 4
NSA_HPG = NSA_HEADS // NSA_GROUPS
HEAD_DIM = 64
CMP_STRIDE = 16
CMP_BLOCK = 2 * CMP_STRIDE
CMP_HIDDEN = 256
SEL_BLOCK = 64
SEL_TOP_N = 8
WINDOW_2 = 512
Q_BLOCK = 128
N_BRANCH = 3
Q_DIM = NSA_HEADS * HEAD_DIM
KV_DIM = NSA_GROUPS * HEAD_DIM
NSA_IN = Q_DIM + 6 * KV_DIM + N_BRANCH * NSA_HEADS

RNN_WIDTH = 1408
RNN_BLOCKS = 16
RNN_BLOCK_W = RNN_WIDTH // RNN_BLOCKS
CONV_WIDTH = 4
RG_C = 8.0

FFN_HIDDEN = ((8 * D_MODEL // 3 + 255) // 256) * 256


def rms_norm_2(x, g):
    xf = x.astype(jnp.float32)
    y = xf * lax.rsqrt(jnp.mean(xf * xf, axis=-1, keepdims=True) + EPS)
    return (y * g.astype(jnp.float32)).astype(x.dtype)

def masked_softmax(s, mask):
    s = jnp.where(mask, s.astype(jnp.float32), -jnp.inf)
    m = jnp.max(s, axis=-1, keepdims=True)
    m = jnp.where(jnp.isfinite(m), m, 0.0)
    p = jnp.exp(s - m)
    return p / jnp.maximum(jnp.sum(p, axis=-1, keepdims=True), jnp.finfo(jnp.float32).tiny)

def cmp_to_sel_map(seq):
    n_c = seq // CMP_STRIDE - 1
    n_s = seq // SEL_BLOCK
    tok = np.arange(seq)
    start = np.arange(n_c) * CMP_STRIDE
    cover_c = (tok[None, :] >= start[:, None]) & (tok[None, :] < start[:, None] + CMP_BLOCK)
    cover_s = (tok[:, None] // SEL_BLOCK) == np.arange(n_s)[None, :]
    m = cover_c.astype(np.float32) @ cover_s.astype(np.float32) / np.float32(CMP_BLOCK)
    return jnp.asarray(m, dtype=jnp.float32)

def compress(t, pos, w1, w2):
    B, S, G, DH = t.shape
    ch = t.reshape(B, S // CMP_STRIDE, CMP_STRIDE, G, DH)
    blocks = jnp.concatenate([ch[:, :-1], ch[:, 1:]], axis=2) + pos[:, None, :]
    flat = jnp.transpose(blocks, (0, 1, 3, 2, 4)).reshape(B, S // CMP_STRIDE - 1, G, CMP_BLOCK * DH)
    return jax.nn.silu(flat @ w1) @ w2

def nsa_mixer(h, w_in, w_out, cmp_pos, cmp_w1, cmp_w2, q_gain, k_gain):
    B, S, _ = h.shape
    G, HPG, DH = NSA_GROUPS, NSA_HPG, HEAD_DIM
    n_c = S // CMP_STRIDE - 1
    n_s = S // SEL_BLOCK
    n_qb = S // Q_BLOCK
    top_k = min(SEL_TOP_N, n_s)
    scale = HEAD_DIM ** -0.5

    proj = h @ w_in
    splits = [Q_DIM + j * KV_DIM for j in range(7)]
    q, k_c, v_c, k_s, v_s, k_w, v_w, g = jnp.split(proj, splits, axis=-1)

    q = rms_norm_2(q.reshape(B, S, NSA_HEADS, DH), q_gain).reshape(B, S, G, HPG, DH)
    kv = lambda t: t.reshape(B, S, G, DH)
    k_c = rms_norm_2(compress(kv(k_c), cmp_pos[0], cmp_w1[0], cmp_w2[0]), k_gain[0])
    v_c = compress(kv(v_c), cmp_pos[1], cmp_w1[1], cmp_w2[1])
    k_s = rms_norm_2(kv(k_s), k_gain[1])
    v_s = kv(v_s)
    k_w = rms_norm_2(kv(k_w), k_gain[2])
    v_w = kv(v_w)
    gates = jax.nn.sigmoid(g.astype(jnp.float32)).reshape(B, S, G, HPG, N_BRANCH)

    to_blocks = lambda t: jnp.transpose(t.reshape(B, n_s, SEL_BLOCK, G, DH), (0, 3, 1, 2, 4))
    k_sb, v_sb = to_blocks(k_s), to_blocks(v_s)
    pad = ((0, 0), (WINDOW_2, 0), (0, 0), (0, 0))
    k_wp, v_wp = jnp.pad(k_w, pad), jnp.pad(v_w, pad)
    sel_map = cmp_to_sel_map(S)
    cmp_end = jnp.arange(n_c) * CMP_STRIDE + CMP_BLOCK - 1
    blk = jnp.arange(n_s)
    gather = jax.vmap(jax.vmap(lambda blocks, ix: blocks[ix]))

    def block_fn(args):
        qb, gb, i = args
        t = i * Q_BLOCK + jnp.arange(Q_BLOCK)
        s = jnp.einsum('bqgnd,bcgd->bgnqc', qb, k_c) * scale
        p_c = masked_softmax(s, cmp_end[None, :] <= t[:, None])
        o_c = jnp.einsum('bgnqc,bcgd->bqgnd', p_c.astype(v_c.dtype), v_c)
        imp = jnp.einsum('bgnqc,cs->bgqs', p_c, sel_map)
        cur = (t // SEL_BLOCK)[:, None]
        imp = jnp.where(blk[None, :] <= cur, imp, -jnp.inf)
        forced = (blk[None, :] == 0) | (blk[None, :] == cur) | (blk[None, :] == cur - 1)
        imp = jnp.where(forced, jnp.inf, imp)
        _, idx = lax.top_k(imp, top_k)
        k_sel = gather(k_sb, idx).reshape(B, G, Q_BLOCK, top_k * SEL_BLOCK, DH)
        v_sel = gather(v_sb, idx).reshape(B, G, Q_BLOCK, top_k * SEL_BLOCK, DH)
        kpos = (idx[..., None] * SEL_BLOCK + jnp.arange(SEL_BLOCK)).reshape(B, G, Q_BLOCK, top_k * SEL_BLOCK)
        mask_s = (kpos <= t[None, None, :, None])[:, :, None]
        s = jnp.einsum('bqgnd,bgqjd->bgnqj', qb, k_sel) * scale
        p = masked_softmax(s, mask_s)
        o_s = jnp.einsum('bgnqj,bgqjd->bqgnd', p.astype(v_sel.dtype), v_sel)
        kw = lax.dynamic_slice_in_dim(k_wp, i * Q_BLOCK, WINDOW_2 + Q_BLOCK, axis=1)
        vw = lax.dynamic_slice_in_dim(v_wp, i * Q_BLOCK, WINDOW_2 + Q_BLOCK, axis=1)
        wpos = i * Q_BLOCK - WINDOW_2 + jnp.arange(WINDOW_2 + Q_BLOCK)
        mask_w = (wpos[None, :] <= t[:, None]) & (wpos[None, :] > t[:, None] - WINDOW_2) & (wpos[None, :] >= 0)
        s = jnp.einsum('bqgnd,bkgd->bgnqk', qb, kw) * scale
        p = masked_softmax(s, mask_w)
        o_w = jnp.einsum('bgnqk,bkgd->bqgnd', p.astype(vw.dtype), vw)
        o = gb[..., 0:1] * o_c + gb[..., 1:2] * o_s + gb[..., 2:3] * o_w
        return o.astype(qb.dtype)

    q_blocks = jnp.moveaxis(q.reshape(B, n_qb, Q_BLOCK, G, HPG, DH), 1, 0)
    g_blocks = jnp.moveaxis(gates.reshape(B, n_qb, Q_BLOCK, G, HPG, N_BRANCH), 1, 0)
    o = lax.map(block_fn, (q_blocks, g_blocks, jnp.arange(n_qb)))
    o = jnp.moveaxis(o, 0, 1).reshape(B, S, Q_DIM)
    return o @ w_out

def lin_rec(left, right):
    a_l, b_l = left
    a_r, b_r = right
    return a_l * a_r, a_r * b_l + b_r

def rglru_mixer(h, w_in, conv_w, conv_b, w_a, b_a, w_x, b_x, lam, w_out):
    B, S, _ = h.shape
    gate, u = jnp.split(h @ w_in, 2, axis=-1)
    u = lax.conv_general_dilated(u, conv_w[:, None, :].astype(u.dtype), window_strides=(1,),
                                 padding=[(CONV_WIDTH - 1, 0)],
                                 dimension_numbers=('NWC', 'WIO', 'NWC'),
                                 feature_group_count=RNN_WIDTH) + conv_b
    ub = u.reshape(B, S, RNN_BLOCKS, RNN_BLOCK_W)
    r = jax.nn.sigmoid(jnp.einsum('bsnd,nde->bsne', ub, w_a) + b_a).reshape(B, S, RNN_WIDTH)
    i_g = jax.nn.sigmoid(jnp.einsum('bsnd,nde->bsne', ub, w_x) + b_x).reshape(B, S, RNN_WIDTH)
    log_a = -RG_C * jax.nn.softplus(-lam.astype(jnp.float32)) * r.astype(jnp.float32)
    a = jnp.exp(log_a)
    b = jnp.sqrt(-jnp.expm1(2.0 * log_a)) * (i_g * u).astype(jnp.float32)
    _, hs = lax.associative_scan(lin_rec, (a, b), axis=1)
    y = hs.astype(h.dtype) * jax.nn.gelu(gate)
    return y @ w_out

def swiglu(h, w_in, w_out):
    g, u = jnp.split(h @ w_in, 2, axis=-1)
    return (jax.nn.silu(g) * u) @ w_out

def second_inputs(seed: int = 0) -> dict:
    key = jax.random.key(seed)
    ks = jax.random.split(key, 24)
    nrm = lambda k, shape, s: jax.random.normal(k, shape, jnp.float32) * s
    D, NN, NR = D_MODEL, N_NSA_LAYERS, N_RG_LAYERS
    a0 = jax.random.uniform(ks[20], (NR, RNN_WIDTH), jnp.float32, 0.9, 0.999)
    s0 = a0 ** (1.0 / RG_C)
    return {
        "x": nrm(ks[0], (BATCH, SEQ, D), 1.0),
        "c": nrm(ks[1], (BATCH, D), 1.0),
        "ada_w": nrm(ks[2], (DEPTH_2, D, 6 * D), 0.5 * D ** -0.5),
        "ada_b": nrm(ks[3], (DEPTH_2, 6 * D), 0.02),
        "norm1_g": 1.0 + nrm(ks[4], (DEPTH_2, D), 0.1),
        "norm2_g": 1.0 + nrm(ks[5], (DEPTH_2, D), 0.1),
        "nsa_w_in": nrm(ks[6], (NN, D, NSA_IN), D ** -0.5),
        "nsa_w_out": nrm(ks[7], (NN, Q_DIM, D), Q_DIM ** -0.5),
        "nsa_cmp_pos": nrm(ks[8], (NN, 2, CMP_BLOCK, HEAD_DIM), 0.1),
        "nsa_cmp_w1": nrm(ks[9], (NN, 2, CMP_BLOCK * HEAD_DIM, CMP_HIDDEN), (CMP_BLOCK * HEAD_DIM) ** -0.5),
        "nsa_cmp_w2": nrm(ks[10], (NN, 2, CMP_HIDDEN, HEAD_DIM), CMP_HIDDEN ** -0.5),
        "nsa_q_gain": 1.0 + nrm(ks[11], (NN, HEAD_DIM), 0.1),
        "nsa_k_gain": 1.0 + nrm(ks[12], (NN, N_BRANCH, HEAD_DIM), 0.1),
        "rg_w_in": nrm(ks[13], (NR, D, 2 * RNN_WIDTH), D ** -0.5),
        "rg_conv_w": nrm(ks[14], (NR, CONV_WIDTH, RNN_WIDTH), CONV_WIDTH ** -0.5),
        "rg_conv_b": nrm(ks[15], (NR, RNN_WIDTH), 0.02),
        "rg_w_a": nrm(ks[16], (NR, RNN_BLOCKS, RNN_BLOCK_W, RNN_BLOCK_W), RNN_BLOCK_W ** -0.5),
        "rg_b_a": nrm(ks[17], (NR, RNN_BLOCKS, RNN_BLOCK_W), 0.02),
        "rg_w_x": nrm(ks[18], (NR, RNN_BLOCKS, RNN_BLOCK_W, RNN_BLOCK_W), RNN_BLOCK_W ** -0.5),
        "rg_b_x": nrm(ks[19], (NR, RNN_BLOCKS, RNN_BLOCK_W), 0.02),
        "rg_lam": jnp.log(s0) - jnp.log1p(-s0),
        "rg_w_out": nrm(ks[21], (NR, RNN_WIDTH, D), RNN_WIDTH ** -0.5),
        "ffn_w_in": nrm(ks[22], (DEPTH_2, D, 2 * FFN_HIDDEN), D ** -0.5),
        "ffn_w_out": nrm(ks[23], (DEPTH_2, FFN_HIDDEN, D), FFN_HIDDEN ** -0.5),
    }

def second_block(x, c, ada_w, ada_b, norm1_g, norm2_g, nsa_w_in, nsa_w_out, nsa_cmp_pos,
              nsa_cmp_w1, nsa_cmp_w2, nsa_q_gain, nsa_k_gain, rg_w_in, rg_conv_w, rg_conv_b,
              rg_w_a, rg_b_a, rg_w_x, rg_b_x, rg_lam, rg_w_out, ffn_w_in, ffn_w_out):
    cond = jax.nn.silu(c)
    for layer in range(DEPTH_2):
        mod = (cond @ ada_w[layer] + ada_b[layer])[:, None, :]
        sh1, sc1, g1, sh2, sc2, g2 = jnp.split(mod, 6, axis=-1)
        hh = rms_norm_2(x, norm1_g[layer]) * (1.0 + sc1) + sh1
        j = layer // N_MIXERS
        if layer % N_MIXERS == 0:
            mix = nsa_mixer(hh, nsa_w_in[j], nsa_w_out[j], nsa_cmp_pos[j], nsa_cmp_w1[j],
                            nsa_cmp_w2[j], nsa_q_gain[j], nsa_k_gain[j])
        else:
            mix = rglru_mixer(hh, rg_w_in[j], rg_conv_w[j], rg_conv_b[j], rg_w_a[j], rg_b_a[j],
                              rg_w_x[j], rg_b_x[j], rg_lam[j], rg_w_out[j])
        x = x + g1 * mix
        hh = rms_norm_2(x, norm2_g[layer]) * (1.0 + sc2) + sh2
        x = x + g2 * swiglu(hh, ffn_w_in[layer], ffn_w_out[layer])
    return x


def setup_inputs(seed=0):
    out = dict(first_inputs(seed))
    for name, value in second_inputs(seed + 1).items():
        if name != "x":
            out[name + "_2"] = value
    return out


def reference(
    x, c, ctx, c_ctx, w_mod, b_mod, g_mix, g_ffn, w_in, ret_decay_logit, ret_gn, w_ret,
    win_sink, w_win, na_rpb, w_na, w_out, w_router, w_exp_gate, w_exp_up, w_exp_down, g_final,
    c_2, ada_w_2, ada_b_2, norm1_g_2, norm2_g_2, nsa_w_in_2, nsa_w_out_2, nsa_cmp_pos_2,
    nsa_cmp_w1_2, nsa_cmp_w2_2, nsa_q_gain_2, nsa_k_gain_2, rg_w_in_2, rg_conv_w_2, rg_conv_b_2,
    rg_w_a_2, rg_b_a_2, rg_w_x_2, rg_b_x_2, rg_lam_2, rg_w_out_2, ffn_w_in_2, ffn_w_out_2,
):
    x = first_block(
        x, c, ctx, c_ctx, w_mod, b_mod, g_mix, g_ffn, w_in, ret_decay_logit, ret_gn, w_ret,
        win_sink, w_win, na_rpb, w_na, w_out, w_router, w_exp_gate, w_exp_up, w_exp_down,
        g_final,
    )
    return second_block(
        x, c_2, ada_w_2, ada_b_2, norm1_g_2, norm2_g_2, nsa_w_in_2, nsa_w_out_2, nsa_cmp_pos_2,
        nsa_cmp_w1_2, nsa_cmp_w2_2, nsa_q_gain_2, nsa_k_gain_2, rg_w_in_2, rg_conv_w_2,
        rg_conv_b_2, rg_w_a_2, rg_b_a_2, rg_w_x_2, rg_b_x_2, rg_lam_2, rg_w_out_2, ffn_w_in_2,
        ffn_w_out_2,
    )


_drawn_inputs = setup_inputs


def setup_inputs(seed=0):
    import zlib

    import numpy as np

    out = dict(_drawn_inputs(seed))
    spreads = {}
    factors = {'b_mod': 3.349,
     'g_mix': 8.0,
     'g_ffn': 7.318,
     'ret_gn': 8.0,
     'win_sink': 8.0,
     'na_rpb': 8.0,
     'nsa_cmp_pos_2': 5.109,
     'nsa_q_gain_2': 8.0,
     'nsa_k_gain_2': 8.0,
     'rg_conv_b_2': 3.7,
     'rg_b_a_2': 64.0,
     'rg_b_x_2': 24.299}
    for name, (base, spread) in spreads.items():
        noise = np.random.default_rng([zlib.crc32(name.encode()), seed]).standard_normal(out[name].shape)
        drawn = base * np.exp(spread * noise) if base else spread * noise
        out[name] = __import__('jax').numpy.asarray(drawn.astype(out[name].dtype))
    for name, factor in factors.items():
        out[name] = (out[name] * factor).astype(out[name].dtype)
    return out
```

```python
from contextlib import ExitStack

import concourse.bass as bass
from concourse import mybir

F32 = mybir.dt.float32
U32 = mybir.dt.uint32
ALU = mybir.AluOpType
ACT = mybir.ActivationFunctionType
AX = mybir.AxisListType.X

P = 128
D = 1024
T = 256
KT = D // P
EPS = 1e-6
NEG = -1e30
TINY = 1.1754944e-38
N_MOD = 6
EXPERTS, CAP = 16, 32
R_HEADS = 4
FFN_T = 22
RNN_T = 11
N_CMP = 15
NSA_HEADS = 16
CHUNK = 2048
SLOTS_A, SLOTS = 6, 12
MOD_FIRST, MOD_LAST = (0, 8, 24), (7, 23, 71)

COLS = {}
CONSTS = {}
DECAY = {}


def lay(table, items):
    at = 0
    for name, width in items:
        table[name] = (at, width)
        at += width
    return at


N_COLS = lay(COLS, [("c_both", 16), ("c_2", 8), ("b_mod", 48), ("ada_b", 96), ("g_mix", 8), ("g_ffn", 8),
                    ("g_final", 8), ("norm1", 16), ("norm2", 16), ("ret_gn", 4), ("decays", 8), ("lam", 11),
                    ("sink", 8), ("q_gain", 1), ("k_gain", 3), ("pos", 32), ("conv_w", 44), ("conv_b", 11),
                    ("b_a", 11), ("b_x", 11)])
N_CONSTS = lay(CONSTS, [("ident", 128), ("ones", 128), ("half_ones", 128), ("rot128", 128), ("rot64", 128),
                        ("cos128", 256), ("sin128", 256), ("cos64", 256), ("sin64", 256), ("win_mask", 512),
                        ("na_mask", 256), ("causal", 128), ("cmp_add", 30), ("cmp_keep", 30), ("own", 512),
                        ("token", 2)])
N_DECAY = lay(DECAY, [("ahead", 512), ("behind", 512), ("ctx_f", 512), ("ctx_b", 512)])


def plan_steps():
    s = [("sum_sq", 0), ("decay",)]
    s += [("mod", i) for i in range(8)] + [("mod_out", 0), ("apply", 0)]
    fill = [("mod", i) for i in range(8, 24)] + [("mod_out", 1)] + [("mod", i) for i in range(24, 72)]
    fill += [("mod_out", 2)]

    def with_fill(steps, n):
        for x in steps:
            s.append(x)
            for _ in range(n):
                if fill:
                    s.append(fill.pop(0))

    with_fill([("kr", 0), ("kr", 1), ("qr", 0), ("qr", 1), ("vr", 0), ("rot", "kr", 0), ("vr", 1),
               ("rot", "kr", 1), ("gr", 0), ("rot", "qr", 0), ("gr", 1), ("rot", "qr", 1), ("kvw",),
               ("qw", 0), ("qw", 1), ("rot", "kw", 0), ("kn", 0), ("rot", "qw", 0), ("kn", 1),
               ("rot", "qw", 1)], 1)
    s += [("ret_s", 0, 0), ("ret_s", 0, 1), ("vn", 0), ("ret_s", 1, 0), ("ret_s", 1, 1), ("ret_o", 0), ("vn", 1),
          ("ret_s", 2, 0), ("ret_s", 2, 1), ("ret_o", 1), ("qn", 0), ("ret_s", 3, 0), ("ret_s", 3, 1),
          ("ret_o", 2), ("qn", 1), ("ret_o", 3), ("na_bias",), ("gate", 0), ("ret_mean", 0), ("ret_mean", 1),
          ("gate", 1), ("ret_var", 0), ("ret_var", 1)]
    gates = [("gate", i) for i in range(2, 12)]
    units = 32
    for i in range(units + 4):
        if i < units:
            s.append(("att_s", i))
        if gates:
            s.append(gates.pop(0))
        if fill:
            s.append(fill.pop(0))
        if 0 <= i - 2 < units:
            s.append(("att_t", i - 2))
        if 0 <= i - 3 < units and (i - 3) % 2:
            s.append(("att_o", (i - 3) // 2))
        if i == units:
            s += fill
            fill = []
    s += [("branch", ch, b) for ch in range(2) for b in range(3)]
    s += [("mix_out", c) for c in range(4)]
    s += [("sum_sq", 1), ("apply", 1)]
    s += [("tok_major", t, kq) for t in range(2) for kq in range(2)] + [("router",), ("affinity",), ("pick",)]
    s += [("gather", k) for k in range(KT)] + [("pick_t", t) for t in range(2)]
    s += [("experts",)]
    s += [("ye_t", j, kq) for j in range(4) for kq in range(2)] + [("combine", p) for p in range(4)]
    s += [("sum_sq", 2), ("apply", 2), ("sum_sq", 3), ("apply", 3)]
    s += [("nkv", 0), ("nkv", 1), ("nqk", 0), ("nqk", 1), ("cmp", 0, 0), ("cmp", 0, 1), ("cmp", 1, 0),
          ("cmp", 1, 1), ("cmp_k",), ("cmp_v",), ("nnorm", 0), ("nnorm", 1)]
    s += [("nqk", 2), ("nqk", 3), ("nnorm", 2), ("nqk", 4), ("nnorm", 3), ("nqk", 5), ("nnorm", 4), ("nv", 0),
          ("nnorm", 5), ("nv", 1), ("nnorm", 6), ("ngate",), ("cmp_s",)]
    units = 2 * NSA_HEADS
    for i in range(units + 4):
        if i < units:
            s.append(("nsa_s", i))
        if 0 <= i - 2 < units:
            s.append(("nsa_t", i - 2))
        if 0 <= i - 3 < units and (i - 3) % 2:
            s.append(("nsa_o", (i - 3) // 2))
    s += [("nsa_out", c) for c in range(4)]
    s += [("sum_sq", 4), ("apply", 4)]
    s += [("ffn_in", 0, i) for i in range(FFN_T)] + [("ffn_out", 0, j) for j in range(FFN_T // 2)]
    s += [("ffn_add", 0)]
    s += [("sum_sq", 5), ("apply", 5)]
    s += [("rnn_in", i) for i in range(RNN_T)]
    s += [("rnn_gate", i) for i in range(RNN_T)] + [("rnn_scan",)]
    s += [("rnn_out", j) for j in range((RNN_T + 1) // 2)] + [("rnn_add",)]
    s += [("sum_sq", 6), ("apply", 6)]
    s += [("ffn_in", 1, i) for i in range(FFN_T)] + [("ffn_out", 1, j) for j in range(FFN_T // 2)]
    s += [("ffn_add", 1)]
    return s


def gate_tiles():
    return [(n, w, k) for n in range(RNN_T) for w in range(2) for k in range(max(0, n - 1), min(RNN_T, n + 2))]


STEPS = plan_steps()
GATE_TILES = gate_tiles()
N_GATE_CHUNKS = -(-len(GATE_TILES) // 16)


def chunk_keys():
    one = {"mod", "kr", "qr", "vr", "gr", "kvw", "qw", "kn", "vn", "qn", "gate", "branch", "mix_out", "nkv", "nv",
           "cmp", "nsa_out", "ffn_in", "ffn_out", "rnn_in", "rnn_out"}
    keys, seen = [], 0
    for x in STEPS:
        if x[0] in one or (x[0] == "nqk"):
            keys.append(x)
        if x[0] == "experts":
            keys += [("expert", e, c) for e in range(EXPERTS) for c in range(12)]
        if x[0] == "rnn_gate":
            last = max(i for i, g in enumerate(GATE_TILES) if g[0] == x[1]) // 16
            while seen <= last:
                keys.append(("gates", seen))
                seen += 1
    return keys


CHUNKS = chunk_keys()
CHUNK_NO = {k: i for i, k in enumerate(CHUNKS)}
FIRST_EXPERT = CHUNK_NO[("expert", 0, 0)]
FIRST_SECOND = FIRST_EXPERT + 12 * EXPERTS


def slot_of(c):
    return c % SLOTS_A if c < FIRST_EXPERT else (c - FIRST_EXPERT) % SLOTS


def landed_count(c):
    if c < FIRST_EXPERT:
        return c // SLOTS_A + 1
    s = slot_of(c)
    before = len(range(s, FIRST_EXPERT, SLOTS_A)) if s < SLOTS_A else 0
    return before + (c - FIRST_EXPERT) // SLOTS + 1


class Job:
    pass


def plan_jobs():
    jobs, last, emptied = {}, {}, {"act": 0, "dve": 0}
    turn = [0]

    def add(name, engine, bank=None, counted=True):
        j = Job()
        j.counted = counted
        if bank is None:
            bank = turn[0] % 7
            turn[0] += 1
        j.bank, j.engine = bank, engine
        emptied[engine] += 1
        j.emptied = emptied[engine]
        j.before = last.get(bank)
        last[bank] = j
        jobs[name] = j

    ffn_turn = [0]
    for x in STEPS:
        k = x[0]
        if k == "mod_out":
            add(x, "dve", 7, counted=False)
        if k == "sum_sq":
            add(x, "dve")
        elif k in ("kr", "kn"):
            for i in range(2):
                add(x + (i,), "act" if k == "kr" else "dve")
        elif k in ("qr", "gr", "qw", "qn", "gate"):
            add(x, "act")
        elif k in ("vr", "vn"):
            for i in range(2):
                add(x + (i,), "dve")
        elif k == "kvw":
            add(("kvw", "k"), "act")
            add(("kvw", "v"), "dve")
        elif k in ("rot", "ret_s", "ret_mean", "ret_var", "mix_out", "combine", "nqk", "nnorm", "nv", "cmp_k",
                   "cmp_v", "nsa_out", "affinity"):
            add(x, "dve")
        elif k in ("ret_o", "att_s", "att_t", "router", "nkv", "ngate", "nsa_s", "nsa_t"):
            add(x, "act")
        elif k in ("att_o", "nsa_o"):
            add(x, "dve")
        elif k == "branch":
            for i in range(2):
                add(x + (i,), "dve")
        elif k in ("tok_major", "ye_t"):
            add(x, "act" if x[2] == 0 else "dve")
        elif k == "gather":
            add(x, "act" if x[1] % 2 else "dve")
        elif k == "pick":
            add(("pick", "idx"), "dve")
            add(("pick", "gate"), "act")
        elif k == "pick_t":
            add(x, "act")
        elif k == "cmp_s":
            for half in range(2):
                add(("cmp_s", half), "dve")
        elif k == "cmp":
            if x[2] == 1:
                add(("cmp", x[1]), "act")
        elif k == "experts":
            jobs["experts"] = {b: last.get(b) for b in range(3)}
            for b in range(3):
                last[b] = None
        elif k in ("ffn_in", "rnn_in"):
            add(x, "dve" if k == "ffn_in" else "act", ffn_turn[0] % 4)
            ffn_turn[0] += 1
        elif k == "rnn_gate":
            add(x, "act", ffn_turn[0] % 4)
            ffn_turn[0] += 1
        elif k in ("ffn_add", "rnn_add"):
            for p in range(4):
                add(x + (p,), "dve", 4 + p)
    return jobs


def build(nc, w, small, out):
    JOBS = {}
    n = 0
    for name, j in plan_jobs().items():
        JOBS[name] = j
        if isinstance(j, Job) and j.counted:
            n += 1
            j.no = n

    ctx = ExitStack()
    with ctx:
        def sb(name, shape, dt=F32):
            return ctx.enter_context(nc.sbuf_tensor(name, shape, dt))

        def sem(name):
            return ctx.enter_context(nc.semaphore(name))

        ring = sb("ring", [P, SLOTS, CHUNK])
        X = sb("X", [P, KT, T])
        H = sb("H", [P, KT, 2 * T])
        SQ = H[:, :, T:2 * T]
        cols = sb("cols", [P, N_COLS])
        consts = sb("consts", [P, N_CONSTS])
        wide = sb("wide", [P, KT, 64])
        silu_c = sb("silu_c", [P, 24])
        mod = sb("mod", [P, 48, 2])
        mod2 = sb("mod2", [P, 96])
        mod_a = sb("mod_a", [P, 7, 8])
        norm_t = sb("norm_t", [P, 2, 2 * T])
        sp = sb("sp", [P, 8, 19])
        stat = sb("stat", [P, 64])
        arena = sb("arena", [P, 16896])

        def col(name, i=0, width=1):
            return cols[:, COLS[name][0] + i:COLS[name][0] + i + width]

        def const(name, rows=P):
            return consts[0:rows, CONSTS[name][0]:CONSTS[name][0] + CONSTS[name][1]]

        def room(at, *shape, rows=P):
            size = 1
            for k in shape:
                size *= k
            v = arena[0:rows, at:at + size]
            if len(shape) == 2:
                v = v.rearrange("p (a b) -> p a b", a=shape[0])
            if len(shape) == 3:
                v = v.rearrange("p (a b c) -> p a b c", a=shape[0], b=shape[1])
            return v

        ident, ones, half_ones = const("ident"), const("ones"), const("half_ones")
        q_r, k_r, v_r, g_r = room(0, 4, T), room(1024, 4, 2 * T), room(3072, 4, 512), room(5120, 4, T)
        q_w, k_w, v_w = room(6144, 4, T), room(7168, 512), room(7680, 4, 128)
        q_n, k_n, v_n = room(8192, 4, T), room(9216, 4, 512), room(11264, 4, 512)
        probs = room(13312, 3, 512)
        probs_t = [room(14848 + 1024 * i, 4, T) for i in range(2)]
        decay_in = room(13312, N_DECAY)
        rope_a, rope_b = room(15872, 2, T), room(16384, 2, T)
        y_r, y_w, y_n = q_r, q_w, q_n
        merged = room(1024, KT, T)
        ctx_in = room(1024, KT, T)
        gates = ring[:, 6:9, :].rearrange("p a b -> p (a b)").rearrange("p (a b) -> p a b", b=T)
        sq_0 = ring[:, 6:8, :].rearrange("p a b -> p (a b)").rearrange("p (a b) -> p a b", b=2 * T)
        decay_m = ring[:, 9:11, :].rearrange("p a b -> p (a b)").rearrange("p (h k q) -> p h k q", h=4, k=4)
        bias_n = ring[:, 9:11, :].rearrange("p a b -> p (a b)").rearrange("p (h k q) -> p h k q", h=8, k=2)
        ret_p = [ring[:, 11, 1024 * i:1024 * i + 1024].rearrange("p (k q) -> p k q", k=4) for i in range(2)]
        ret_sq = ret_p[0]
        h_tok, x_e, y_e = room(0, 2, D), room(2048, KT, 512), room(6144, KT, 512)
        y_tok = room(2048, 4, D)
        hot, hot_t = room(10240, 2, 512), room(11264, 4, T)
        gate_b = room(12288, 512)
        aff, aff_t = room(12800, 2, 16), room(12832, T, rows=16)
        top_v = room(13088, 32, rows=16)
        top_f = room(13120, 32, rows=16)
        top_i = ctx.enter_context(nc.sbuf_tensor("top_i", [16, 32], U32))
        spread_i, spread_g = room(13152, 16, 32, rows=16), room(13664, 16, 32, rows=16)
        x_cur, silu_g, hid = room(14176, KT, 32), room(14432, 256), room(14688, 256)
        qk = room(0, 3104)
        n_sq, n_rs = room(3104, 2, 512), room(4128, 2, 512)
        win_f = [room(5152 + 1024 * i, 4, T) for i in range(2)]
        flat = [room(7200 + 960 * i, 16, 4, 15) for i in range(2)]
        o_n = room(5152, KT, T)
        hid_c = room(9120, 2, 2, 60)
        v_c = room(9360, 4, 64, rows=15)
        v_s = [room(9616 + 512 * i, 2, T) for i in range(2)]
        n_p = room(10640, 3, 512)
        n_pt = [room(12176 + 1024 * i, 2, 2, T) for i in range(2)]
        cmp_p = room(14224, 2, 16, 15)
        cmp_pt = [room(14704 + 256 * i, T, rows=15) for i in range(2)]
        n_gate = room(15216, 2, 48)
        cmp_m = room(15312, 2, 16)
        w2c = room(15344, 4, 64).rearrange("p (a b) n -> p a b n", a=2)
        ffn_h = room(0, FFN_T, T)
        ffn_g = room(5632, 2, T)
        gelu_g, u_in, u_c = room(0, RNN_T, T), room(2816, RNN_T, T + 3), room(5665, RNN_T, T)
        rec, inp = room(8481, RNN_T, T), room(11297, RNN_T, T)
        thr, rnn_d = room(2816, RNN_T, T), room(14113, 2, T)

        bank = [ctx.enter_context(nc.psum_tensor(f"bank{i}", [P, 512], F32)) for i in range(8)]
        mods = bank[7]

        landed = [sem(f"landed{i}") for i in range(SLOTS)]
        chunk_used = sem("chunk_used")
        job_done = sem("job_done")
        emptied = {"act": sem("act_emptied"), "dve": sem("dve_emptied")}
        x_landed, ctx_landed, cols_landed = sem("x_landed"), sem("ctx_landed"), sem("cols_landed")
        consts_landed, decay_landed, wide_landed = sem("consts_landed"), sem("decay_landed"), sem("wide_landed")
        bias_landed, bias_ready, w2_landed = sem("bias_landed"), sem("bias_ready"), sem("w2_landed")
        dve_step, act_step = sem("dve_step"), sem("act_step")
        silu_ready, mod_done, sq_x, sq_ctx = sem("silu_ready"), sem("mod_done"), sem("sq_x"), sem("sq_ctx")
        sq_ready, std_ready, h_scaled, h_ready = sem("sq_ready"), sem("std_ready"), sem("h_scaled"), sem("h_ready")
        x_final = sem("x_final")
        sp_arg, sp_exp, sp_ready = sem("sp_arg"), sem("sp_exp"), sem("sp_ready")
        decay_arg, decay_exp, decay_ready = sem("decay_arg"), sem("decay_exp"), sem("decay_ready")
        roped = sem("roped")
        ret_sq_ready, ret_std, ret_ready = sem("ret_sq_ready"), sem("ret_std"), sem("ret_ready")
        max_ready, sink_ready, probs_ready = sem("max_ready"), sem("sink_ready"), sem("probs_ready")
        merged_ready = sem("merged_ready")
        aff_max, aff_ready, spread_ready = sem("aff_max"), sem("aff_ready"), sem("spread_ready")
        x_cur_free, x_cur_ready, gate_done, up_done = (sem("x_cur_free"), sem("x_cur_ready"), sem("gate_done"),
                                                       sem("up_done"))
        silu_g_ready, hid_ready, down_done, ye_taken = (sem("silu_g_ready"), sem("hid_ready"), sem("down_done"),
                                                        sem("ye_taken"))
        flat_ready, n_sq_ready, n_std, n_normed = sem("flat_ready"), sem("n_sq_ready"), sem("n_std"), sem("n_normed")
        cmp_arg, cmp_exp, cmp_ready = sem("cmp_arg"), sem("cmp_exp"), sem("cmp_ready")
        n_max, n_ready = sem("n_max"), sem("n_ready")
        ffn_silu, conv_ready, rnn_tanh, rnn_sqrt_in, rnn_sqrt, rnn_ready = (
            sem("ffn_silu"), sem("conv_ready"), sem("rnn_tanh"), sem("rnn_sqrt_in"), sem("rnn_sqrt"),
            sem("rnn_ready"))
        out_landed = sem("out_landed")

        def att_unit(u):
            return u >= 16, u // 2 % 8, u % 2

        def att_head(kind, hd):
            return (hd // 2, hd % 2)

        def nsa_head(h):
            g = h // 4
            return g // 2 * 4 + h % 4, g % 2, g // 2

        X_JOBS = {1: [("mix_out", c) for c in range(4)], 2: [("combine", p) for p in range(4)],
                  4: [("nsa_out", c) for c in range(4)], 5: [("ffn_add", 0, p) for p in range(4)],
                  6: [("rnn_add", p) for p in range(4)]}
        NORM_GAIN = {0: ("g_mix", 0), 1: ("g_ffn", 0), 3: ("norm1", 0), 4: ("norm2", 0), 5: ("norm1", 8),
                     6: ("norm2", 8)}
        SHIFT2 = {3: 0, 4: 24, 5: 48, 6: 72}
        H_COUNT = {0: 16, 1: 24, 3: 32, 4: 40, 5: 48, 6: 56}

        def shift_of(ni, k):
            if ni == 0:
                return mod[:, k, 0:1]
            if ni == 1:
                return mod[:, 24 + k, 0:1]
            return mod2[:, SHIFT2[ni] + k:SHIFT2[ni] + k + 1]

        block = ctx.enter_context(nc.Block())

        @block.sync
        def _(sp_eng):
            eng = sp_eng
            rounds_a = FIRST_EXPERT // SLOTS_A
            first = w[0:rounds_a * SLOTS_A].rearrange("(r s) p f -> r s p f", s=SLOTS_A)
            for s in range(SLOTS_A):
                eng.dma_start(ring[:, s, :], first[0, s]).then_inc(landed[s], 16)
            with eng.Fori(1, rounds_a) as r:
                for s in range(SLOTS_A):
                    eng.wait_ge(chunk_used, r * SLOTS_A + (s + 1 - SLOTS_A))
                    eng.dma_start(ring[:, s, :], first[r, s]).then_inc(landed[s], 16)
            for c in range(rounds_a * SLOTS_A, FIRST_EXPERT):
                eng.wait_ge(chunk_used, c - SLOTS_A + 1)
                eng.dma_start(ring[:, slot_of(c), :], w[c]).then_inc(landed[slot_of(c)], 16)
            experts = w[FIRST_EXPERT:FIRST_SECOND].rearrange("(e s) p f -> e s p f", s=SLOTS)
            for s in range(SLOTS):
                if s < SLOTS_A:
                    eng.wait_ge(chunk_used, max(c for c in range(FIRST_EXPERT) if c % SLOTS_A == s) + 1)
                elif s == SLOTS_A:
                    eng.wait_ge(merged_ready, 4)
                eng.dma_start(ring[:, s, :], experts[0, s]).then_inc(landed[s], 16)
            with eng.Fori(1, EXPERTS) as e:
                for s in range(SLOTS):
                    eng.wait_ge(chunk_used, e * SLOTS + (FIRST_EXPERT + s + 1 - SLOTS))
                    eng.dma_start(ring[:, s, :], experts[e, s]).then_inc(landed[s], 16)
            rest = len(CHUNKS) - FIRST_SECOND
            rounds_b = rest // SLOTS
            second = w[FIRST_SECOND:FIRST_SECOND + rounds_b * SLOTS].rearrange("(r s) p f -> r s p f", s=SLOTS)
            with eng.Fori(0, rounds_b) as r:
                for s in range(SLOTS):
                    eng.wait_ge(chunk_used, r * SLOTS + (FIRST_SECOND + s + 1 - SLOTS))
                    eng.dma_start(ring[:, s, :], second[r, s]).then_inc(landed[s], 16)
            for c in range(FIRST_SECOND + rounds_b * SLOTS, len(CHUNKS)):
                eng.wait_ge(chunk_used, c - SLOTS + 1)
                eng.dma_start(ring[:, slot_of(c), :], w[c]).then_inc(landed[slot_of(c)], 16)
            for p in range(4):
                eng.wait_ge(emptied["dve"], JOBS[("ffn_add", 1, p)].emptied)
                eng.dma_start(out[:, 2 * p:2 * p + 2, :], X[:, 2 * p:2 * p + 2, :]).then_inc(out_landed, 16)
            eng.wait_ge(out_landed, 64)

        @block.gpsimd
        def _(eng):
            eng.dma_start(cols[:, :], small["cols"]).then_inc(cols_landed, 16)
            eng.dma_start(consts[:, :], small["consts"]).then_inc(consts_landed, 16)
            eng.dma_start(decay_in, small["decay"]).then_inc(decay_landed, 16)
            eng.dma_start(wide[:, :, :], small["wide"]).then_inc(wide_landed, 16)
            eng.wait_ge(emptied["dve"], JOBS[("ret_s", 3, 1)].emptied)
            eng.dma_start(bias_n.rearrange("p h k q -> p (h k q)"), small["bias"]).then_inc(bias_landed, 16)
            eng.wait_ge(bias_landed, 16)
            eng.wait_ge(consts_landed, 16)
            mask = const("na_mask").unsqueeze(1).to_broadcast([P, 16, T])
            flat_bias = bias_n.rearrange("p h k q -> p (h k) q")
            nc.gpsimd.tensor_tensor(flat_bias, flat_bias, mask, ALU.add).then_inc(bias_ready, 1)
            eng.wait_ge(merged_ready, 4)
            eng.dma_start(w2c, small["w2c"]).then_inc(w2_landed, 16)

        @block.tensor
        def _(pe):
            owed = [0]

            def mm(o, lhsT, rhs, start, stop, ends=None, grouped=False):
                i = nc.tensor.matmul(o, lhsT, rhs, start=start, stop=stop, skip_group_check=grouped)
                return settle(i, ends)

            def tr(o, in_, ends=None, rows=P):
                i = nc.tensor.transpose(o, in_, ident[0:rows, 0:rows])
                return settle(i, ends)

            def settle(i, ends):
                if ends is not None:
                    i.then_inc(ends, 1)
                elif owed[0]:
                    i.then_inc(chunk_used, owed[0])
                    owed[0] = 0
                return i

            def chunk(key):
                c = CHUNK_NO[key]
                pe.wait_ge(landed[slot_of(c)], 16 * landed_count(c))
                return ring[:, slot_of(c), :].rearrange("p (k n) -> p k n", k=8)

            def begin(name):
                j = JOBS[name]
                if j.before is not None:
                    pe.wait_ge(emptied[j.before.engine], j.before.emptied)
                return bank[j.bank]

            def in_sbuf(name):
                pe.wait_ge(emptied[JOBS[name].engine], JOBS[name].emptied)

            def h_is(ni):
                pe.wait_ge(h_ready, H_COUNT[ni])

            def tiles(x, n, act, name=None):
                ck = chunk(x)
                b = begin(name or x)
                for j in range(2):
                    for k in range(KT):
                        mm(b[:, j * n:(j + 1) * n], ck[:, k, j * P:(j + 1) * P], act(k), k == 0, k == KT - 1,
                           job_done if j == 1 and k == KT - 1 else None)
                owed[0] += 1

            def hx(k):
                return H[:, k, 0:T]

            def hxc(k):
                return H[:, k, :]

            def key_tiles(x):
                ck = chunk(x)
                for j in range(2):
                    b = begin(x + (j,))
                    for k in range(KT):
                        mm(b[:, :], ck[:, k, j * P:(j + 1) * P], hxc(k), k == 0, k == KT - 1,
                           job_done if k == KT - 1 else None)
                owed[0] += 1

            def value_tiles(x, names, tokens):
                ck = chunk(x)
                for i, name in enumerate(names):
                    b = begin(name)
                    for j in range(2):
                        t = 2 * i + j
                        for k in range(KT):
                            mm(b[:, j * T:(j + 1) * T], H[:, k, t * P:(t + 1) * P], ck[:, k, :], k == 0, k == KT - 1,
                               job_done if j == 1 and k == KT - 1 else None)
                owed[0] += 1

            def step_sum_sq(ni):
                if ni == 0:
                    pe.wait_ge(consts_landed, 16)
                    pe.wait_ge(sq_x, 1)
                    pe.wait_ge(sq_ctx, 1)
                b = begin(("sum_sq", ni))
                for k in range(KT):
                    if ni and k % 2 == 0:
                        pe.wait_ge(sq_ready, 4 * (ni - 1) + k // 2 + 1)
                    if ni == 0:
                        mm(b[:, :], ones, sq_0[:, k, :], k == 0, k == KT - 1, job_done if k == KT - 1 else None)
                    else:
                        mm(b[:, 0:T], ones, SQ[:, k, :], k == 0, k == KT - 1, job_done if k == KT - 1 else None)

            def step_mod(i):
                ck = chunk(("mod", i))
                if i == 0:
                    pe.wait_ge(silu_ready, 1)
                if i in MOD_FIRST:
                    begin(("mod_out", MOD_FIRST.index(i)))
                ends = i in MOD_LAST
                for j in range(2):
                    n = 2 * i + j
                    for k in range(KT):
                        if n < 48:
                            o, v = mods[:, 2 * n:2 * n + 2], silu_c[:, 2 * k:2 * k + 2]
                        else:
                            o, v = mods[:, 48 + n:49 + n], silu_c[:, 16 + k:17 + k]
                        mm(o, ck[:, k, j * P:(j + 1) * P], v, k == 0, k == KT - 1,
                           mod_done if ends and j == 1 and k == KT - 1 else None)
                owed[0] += 1

            def step_kr(c):
                if c == 0:
                    h_is(0)
                key_tiles(("kr", c))

            def step_rot(what, p):
                if what == "kr":
                    in_sbuf(("kr", p, 1))
                    m, v, n = const("rot128"), k_r[:, 2 * p:2 * p + 2, 0:T], 512
                elif what == "qr":
                    in_sbuf(("qr", p))
                    m, v, n = const("rot128"), q_r[:, 2 * p:2 * p + 2, :], 512
                elif what == "kw":
                    in_sbuf(("kvw", "k"))
                    m, v, n = const("rot64"), k_w[:, 0:T], 256
                else:
                    in_sbuf(("qw", p))
                    m, v, n = const("rot64"), q_w[:, 2 * p:2 * p + 2, :], 512
                mm(begin(("rot", what, p))[:, 0:n], m, v, True, True, job_done)

            def step_vr(c):
                value_tiles(("vr", c), [("vr", c, 0), ("vr", c, 1)], 4)

            def step_vn(c):
                value_tiles(("vn", c), [("vn", c, 0), ("vn", c, 1)], 4)

            def step_kvw():
                ck = chunk(("kvw",))
                b = begin(("kvw", "k"))
                for k in range(KT):
                    mm(b[:, :], ck[:, k, 0:P], hxc(k), k == 0, k == KT - 1, job_done if k == KT - 1 else None)
                b = begin(("kvw", "v"))
                for t in range(4):
                    for k in range(KT):
                        mm(b[:, t * P:(t + 1) * P], H[:, k, t * P:(t + 1) * P], ck[:, k, P:2 * P], k == 0,
                           k == KT - 1, job_done if t == 3 and k == KT - 1 else None)
                owed[0] += 1

            def step_ret_s(h, kp):
                if h == 0 and kp == 0:
                    pe.wait_ge(roped, 4)
                b = begin(("ret_s", h, kp))
                for j in range(2):
                    mm(b[:, j * T:(j + 1) * T], k_r[:, h, (2 * kp + j) * P:(2 * kp + j + 1) * P], q_r[:, h, :], True,
                       True, job_done if j else None)

            def step_ret_o(h):
                in_sbuf(("ret_s", h, 1))
                b = begin(("ret_o", h))
                for kt in range(4):
                    mm(b[:, 0:T], v_r[:, kt, h * P:(h + 1) * P], ret_p[h % 2][:, kt, :], kt == 0, kt == 3,
                       job_done if kt == 3 else None)

            def step_ret_mean(p):
                in_sbuf(("ret_o", 2 * p + 1))
                mm(begin(("ret_mean", p))[:, :], ones, y_r[:, 2 * p:2 * p + 2, :], True, True, job_done)

            def step_ret_var(p):
                pe.wait_ge(ret_sq_ready, p + 1)
                mm(begin(("ret_var", p))[:, :], ones, ret_sq[:, 2 * p:2 * p + 2, :], True, True, job_done)

            def step_att_s(u):
                na, hd, qt = att_unit(u)
                if u == 0:
                    pe.wait_ge(roped, 7)
                if u == 16:
                    in_sbuf(("qn", 1))
                    in_sbuf(("kn", 1, 1))
                t, half = att_head(na, hd)
                rows = slice(64 * half, 64 * half + 64)
                q = (q_n if na else q_w)[rows, t, qt * P:(qt + 1) * P]
                keys = k_n[rows, t, :] if na else k_w[rows, :]
                mm(begin(("att_s", u))[:, :], q, keys, True, True, job_done)

            def step_att_t(u):
                pe.wait_ge(probs_ready, u + 1)
                b = begin(("att_t", u))
                for kt in range(4):
                    tr(b[:, kt * P:(kt + 1) * P], probs[:, u % 3, kt * P:(kt + 1) * P], job_done if kt == 3 else None)

            def step_att_o(i):
                na, hd, _ = att_unit(2 * i)
                in_sbuf(("att_t", 2 * i + 1))
                if i == 0:
                    in_sbuf(("kvw", "v"))
                if i == 8:
                    in_sbuf(("vn", 1, 1))
                t, half = att_head(na, hd)
                b = begin(("att_o", i))
                for kt in range(4):
                    v = v_n[:, kt, hd * 64:hd * 64 + 64] if na else v_w[:, kt, half * 64:half * 64 + 64]
                    mm(b[64 * half:64 * half + 64, 0:T], v, probs_t[i % 2][:, kt, :], kt == 0, kt == 3,
                       job_done if kt == 3 else None)

            def step_branch(ch, br):
                ck = chunk(("branch", ch, br)).rearrange("p k n -> p (k n)").rearrange("p (k n) -> p k n", k=4)
                y = (y_r, y_w, y_n)[br]
                if br == 0:
                    pe.wait_ge(ret_ready, 2)
                else:
                    in_sbuf(("att_o", 7 if br == 1 else 15))
                for p in range(2):
                    b = begin(("branch", ch, br, p))
                    for j in range(2):
                        for k in range(4):
                            mm(b[:, j * T:(j + 1) * T], ck[:, k, (2 * p + j) * P:(2 * p + j + 1) * P], y[:, k, :],
                               k == 0, k == 3, job_done if j == 1 and k == 3 else None)
                owed[0] += 1

            def step_mix_out(c):
                pe.wait_ge(merged_ready, 4)
                tiles(("mix_out", c), T, lambda k: merged[:, k, :])

            def step_tok_major(t, kq):
                h_is(1)
                b = begin(("tok_major", t, kq))
                for j in range(4):
                    tr(b[:, j * P:(j + 1) * P], H[:, 4 * kq + j, t * P:(t + 1) * P], job_done if j == 3 else None)

            def step_router():
                pe.wait_ge(wide_landed, 16)
                b = begin(("router",))
                for t in range(2):
                    for k in range(KT):
                        mm(b[:, t * 16:t * 16 + 16], H[:, k, t * P:(t + 1) * P], wide[:, k, 0:16], k == 0, k == KT - 1,
                           job_done if t == 1 and k == KT - 1 else None)

            def step_affinity():
                pe.wait_ge(aff_ready, 1)
                b = begin(("affinity",))
                for t in range(2):
                    tr(b[0:16, t * P:(t + 1) * P], aff[:, t, :], job_done if t else None)

            def step_pick():
                pe.wait_ge(spread_ready, 1)
                mm(begin(("pick", "idx"))[:, :], ones[0:16, :], spread_i, True, True, job_done)
                mm(begin(("pick", "gate"))[:, :], ones[0:16, :], spread_g, True, True, job_done)

            def step_gather(k):
                if k == 0:
                    for t in range(2):
                        for kq in range(2):
                            in_sbuf(("tok_major", t, kq))
                    in_sbuf(("pick", "idx"))
                b = begin(("gather", k))
                for t in range(2):
                    mm(b[:, :], h_tok[:, t, k * P:(k + 1) * P], hot[:, t, :], t == 0, t == 1, job_done if t else None)

            def step_pick_t(t):
                b = begin(("pick_t", t))
                for j in range(4):
                    tr(b[:, j * P:(j + 1) * P], hot[:, t, j * P:(j + 1) * P], job_done if j == 3 else None)

            def step_experts():
                for b in range(3):
                    j = JOBS["experts"][b]
                    pe.wait_ge(emptied[j.engine], j.emptied)
                if owed[0]:
                    pe.sem_inc(chunk_used, owed[0])
                    owed[0] = 0
                before = [landed_count(FIRST_EXPERT + s) - 1 for s in range(SLOTS)]
                with pe.Fori(0, EXPERTS) as e:
                    pe.wait_ge(x_cur_ready, e + 1)
                    for part, (b, ends, act) in enumerate(((0, gate_done, x_cur), (1, up_done, x_cur),
                                                           (2, down_done, None))):
                        if part == 2:
                            pe.wait_ge(hid_ready, e + 1)
                            pe.wait_ge(ye_taken, e + 1)
                        for c in range(4):
                            s = 4 * part + c
                            pe.wait_ge(landed[s], e * 16 + 16 * (before[s] + 1))
                            ck = ring[:, s, :].rearrange("p (k n) -> p k n", k=8)
                            for j in range(2):
                                n = 2 * c + j
                                for k in range(KT):
                                    v = x_cur[:, k, :] if part < 2 else hid[:, k * CAP:(k + 1) * CAP]
                                    i = nc.tensor.matmul(bank[b][:, n * CAP:(n + 1) * CAP], ck[:, k, j * P:(j + 1) * P],
                                                         v, start=k == 0, stop=k == KT - 1)
                                    if c and j == 0 and k == 0:
                                        i.then_inc(chunk_used, 1)
                        i.then_inc(ends, 1)
                        pe.wait_ge(ends, e + 1)
                        pe.sem_inc(chunk_used, 1)
                pe.wait_ge(ye_taken, EXPERTS + 1)

            def step_ye_t(j, kq):
                b = begin(("ye_t", j, kq))
                for i in range(4):
                    tr(b[:, i * P:(i + 1) * P], y_e[:, 4 * kq + i, j * P:(j + 1) * P], job_done if i == 3 else None)

            def step_combine(p):
                if p == 0:
                    in_sbuf(("ye_t", 3, 0))
                    in_sbuf(("ye_t", 3, 1))
                b = begin(("combine", p))
                for i in range(2):
                    n = 2 * p + i
                    for j in range(4):
                        mm(b[:, i * T:(i + 1) * T], y_tok[:, j, n * P:(n + 1) * P], hot_t[:, j, :], j == 0, j == 3,
                           job_done if i == 1 and j == 3 else None)

            def step_nkv(kv):
                h_is(3)
                tiles(("nkv", kv), T, hx)

            def step_nnorm(i):
                pe.wait_ge(n_sq_ready, i + 1)
                n = 512 if i < 6 else 30
                mm(begin(("nnorm", i))[:, 0:n], half_ones, n_sq[:, i % 2, 0:n], True, True, job_done)

            def step_nv(i):
                value_tiles(("nv", i), [("nv", i)], 2)

            def step_ngate():
                b = begin(("ngate",))
                for t in range(2):
                    for k in range(KT):
                        mm(b[:, t * 48:t * 48 + 48], H[:, k, t * P:(t + 1) * P], wide[:, k, 16:64], k == 0, k == KT - 1,
                           job_done if t == 1 and k == KT - 1 else None)

            cmp_bank = [None]

            def step_cmp(kv, part):
                ck = chunk(("cmp", kv, part))
                if part == 0:
                    pe.wait_ge(flat_ready, kv + 1)
                    cmp_bank[0] = begin(("cmp", kv))
                for ht in range(2):
                    for j in range(8):
                        f = flat[kv][:, 8 * part + j, :, :]
                        mm(cmp_bank[0][:, ht * 60:ht * 60 + 60], ck[:, j, ht * P:(ht + 1) * P], f,
                           part == 0 and ht == 0 and j == 0, part == 1 and j == 7,
                           job_done if part == 1 and ht == 1 and j == 7 else None, grouped=True)
                owed[0] += 1

            def step_cmp_k():
                pe.wait_ge(w2_landed, 16)
                in_sbuf(("cmp", 0))
                b = begin(("cmp_k",))
                for par in range(2):
                    for ht in range(2):
                        v = hid_c[:, 0, ht, :].rearrange("p (g c) -> p g c", g=4)[:, par::2, :]
                        mm(b[64 * par:64 * par + 64, 0:30], w2c[:, 0, ht, :], v, ht == 0, ht == 1,
                           job_done if par and ht else None)

            def step_cmp_v():
                in_sbuf(("cmp", 1))
                b = begin(("cmp_v",))
                for g in range(4):
                    for ht in range(2):
                        mm(b[0:N_CMP, g * 64:g * 64 + 64], hid_c[:, 1, ht, g * N_CMP:(g + 1) * N_CMP], w2c[:, 1, ht, :],
                           ht == 0, ht == 1, job_done if g == 3 and ht else None)

            def step_cmp_s():
                pe.wait_ge(n_normed, 7)
                for half in range(2):
                    b = begin(("cmp_s", half))
                    rows = slice(64 * half, 64 * half + 64)
                    for qt in range(2):
                        for qi in range(8):
                            gp, at = qi // 4, (qt * 8 + qi) * N_CMP
                            mm(b[:, at:at + N_CMP], qk[rows, 1024 + qi * T + qt * P:1024 + qi * T + (qt + 1) * P],
                               qk[rows, 3072 + gp * N_CMP:3072 + (gp + 1) * N_CMP], True, True,
                               job_done if qt == 1 and qi == 7 else None)

            def step_nsa_s(u):
                h, qt = u // 2, u % 2
                qi, half, gp = nsa_head(h)
                rows = slice(64 * half, 64 * half + 64)
                nk = P * (qt + 1)
                b = begin(("nsa_s", u))
                for br in range(2):
                    mm(b[:, br * nk:(br + 1) * nk], qk[rows, 1024 + qi * T + qt * P:1024 + qi * T + (qt + 1) * P],
                       qk[rows, br * 512 + gp * T:br * 512 + gp * T + nk], True, True, job_done if br else None)

            def step_nsa_t(u):
                h, qt = u // 2, u % 2
                pe.wait_ge(n_ready, u + 1)
                if u == 0:
                    pe.wait_ge(cmp_ready, 1)
                nk = P * (qt + 1)
                b = begin(("nsa_t", u))
                if qt == 0:
                    for q in range(2):
                        tr(b[0:N_CMP, 256 + q * P:256 + (q + 1) * P], cmp_p[:, q, h, :])
                for kt in range(qt + 1):
                    for br in range(2):
                        at = (2 * kt + br) * P
                        tr(b[:, at:at + P], n_p[:, u % 3, br * nk + kt * P:br * nk + (kt + 1) * P],
                           job_done if kt == qt and br else None)

            def step_nsa_o(h):
                qi, half, gp = nsa_head(h)
                g = h // 4
                in_sbuf(("nsa_t", 2 * h + 1))
                b = begin(("nsa_o", h))[64 * half:64 * half + 64, 0:T]
                pt = n_pt[h % 2]
                mm(b, v_c[:, g, :], cmp_pt[h % 2], True, False)
                for br in range(2):
                    mm(b, v_s[br][:, 0, g * 64:g * 64 + 64], pt[:, 0, br, :], False, False)
                for br in range(2):
                    mm(b[:, P:T], v_s[br][:, 1, g * 64:g * 64 + 64], pt[:, 1, br, P:T], False, br == 1,
                       job_done if br else None)

            def step_nsa_out(c):
                if c == 0:
                    in_sbuf(("nsa_o", NSA_HEADS - 1))
                tiles(("nsa_out", c), T, lambda k: o_n[:, k, :])

            def step_ffn_in(l, i):
                h_is(4 if l == 0 else 6)
                tiles(("ffn_in", l, i), T, hx)

            def rows_out(key, j, n_k, act, adds):
                ck = chunk(key).rearrange("p k n -> p (k n)").rearrange("p (k n) -> p k n", k=2)
                if j == 0:
                    for p in range(4):
                        begin(adds[p])
                for kk in range(2):
                    k = 2 * j + kk
                    if k == n_k:
                        break
                    for n in range(KT):
                        o = bank[4 + n // 2][:, n % 2 * T:n % 2 * T + T]
                        mm(o, ck[:, kk, n * P:(n + 1) * P], act(k), k == 0 and n % 2 == 0, k == n_k - 1,
                           job_done if k == n_k - 1 and n % 2 else None, grouped=True)
                owed[0] += 1

            def step_ffn_out(l, j):
                in_sbuf(("ffn_in", l, 2 * j + 1))
                rows_out(("ffn_out", l, j), j, FFN_T, lambda k: ffn_h[:, k, :], [("ffn_add", l, p) for p in range(4)])

            def step_rnn_in(i):
                h_is(5)
                tiles(("rnn_in", i), T, hx)

            seen = [-1]

            def step_rnn_gate(n):
                pe.wait_ge(conv_ready, min(n + 2, RNN_T))
                b = begin(("rnn_gate", n))
                mine = [(i, x) for i, x in enumerate(GATE_TILES) if x[0] == n]
                for i, (_, wh, k) in mine:
                    if i // 16 != seen[0]:
                        if seen[0] >= 0:
                            owed[0] += 1
                        seen[0] = i // 16
                    ck = chunk(("gates", i // 16)).rearrange("p k n -> p (k n)")
                    ks = [x[2] for _, x in mine if x[1] == wh]
                    mm(b[:, wh * T:(wh + 1) * T], ck[:, i % 16 * P:(i % 16 + 1) * P], u_c[:, k, :], k == ks[0],
                       k == ks[-1], job_done if (i, (n, wh, k)) == mine[-1] else None)
                if n == RNN_T - 1:
                    owed[0] += 1

            def step_rnn_out(j):
                pe.wait_ge(rnn_ready, min(2 * j + 2, RNN_T))
                rows_out(("rnn_out", j), j, RNN_T, lambda k: gelu_g[:, k, :], [("rnn_add", p) for p in range(4)])

            def whole(name):
                return lambda *a: tiles((name,) + a, T, hx)

            parts = {"sum_sq": step_sum_sq, "mod": step_mod, "kr": step_kr, "rot": step_rot, "qr": whole("qr"),
                     "vr": step_vr, "gr": whole("gr"), "kvw": step_kvw, "qw": whole("qw"),
                     "kn": lambda c: key_tiles(("kn", c)), "vn": step_vn, "qn": whole("qn"), "gate": whole("gate"),
                     "ret_s": step_ret_s, "ret_o": step_ret_o, "ret_mean": step_ret_mean, "ret_var": step_ret_var,
                     "att_s": step_att_s, "att_t": step_att_t, "att_o": step_att_o, "branch": step_branch,
                     "mix_out": step_mix_out, "tok_major": step_tok_major, "router": step_router,
                     "affinity": step_affinity, "pick": step_pick, "gather": step_gather, "pick_t": step_pick_t,
                     "experts": step_experts, "ye_t": step_ye_t, "combine": step_combine, "nkv": step_nkv,
                     "nqk": whole("nqk"), "nnorm": step_nnorm, "nv": step_nv, "ngate": step_ngate, "cmp": step_cmp,
                     "cmp_k": step_cmp_k, "cmp_v": step_cmp_v, "cmp_s": step_cmp_s, "nsa_s": step_nsa_s,
                     "nsa_t": step_nsa_t, "nsa_o": step_nsa_o, "nsa_out": step_nsa_out, "ffn_in": step_ffn_in,
                     "ffn_out": step_ffn_out, "rnn_in": step_rnn_in, "rnn_gate": step_rnn_gate,
                     "rnn_out": step_rnn_out}
            for name, *args in STEPS:
                if name in parts:
                    parts[name](*args)

        @block.scalar
        def _(act):
            f = nc.scalar.activation

            def job(name):
                act.wait_ge(job_done, JOBS[name].no)
                return bank[JOBS[name].bank]

            def takes(i, name):
                assert JOBS[name].engine == "act"
                i.then_inc(emptied["act"], 1)

            def two(b, n=T):
                return b[:, 0:2 * n].rearrange("p (a b) -> p a b", a=2)

            act.dma_start(X[:, :, :], small["x"]).then_inc(x_landed, 16)
            act.dma_start(ctx_in, small["ctx"]).then_inc(ctx_landed, 16)

            def step_sum_sq(ni):
                if ni == 0:
                    act.wait_ge(cols_landed, 16)
                    f(silu_c[:, :], cols[:, 0:24], ACT.Silu).then_inc(silu_ready, 1)
                    act.wait_ge(x_landed, 16)
                    f(sq_0[:, :, 0:T], X[:, :, :], ACT.Square).then_inc(sq_x, 1)
                else:
                    for p in range(4):
                        if ni in X_JOBS:
                            act.wait_ge(emptied["dve"], JOBS[X_JOBS[ni][p]].emptied)
                        else:
                            act.wait_ge(x_final, 2 * p + 2)
                        f(SQ[:, 2 * p:2 * p + 2, :], X[:, 2 * p:2 * p + 2, :], ACT.Square).then_inc(sq_ready, 1)
                n = 2 * T if ni == 0 else T
                act.wait_ge(emptied["dve"], JOBS[("sum_sq", ni)].emptied)
                f(norm_t[:, 1, 0:n], norm_t[:, 0, 0:n], ACT.Sqrt).then_inc(std_ready, 1)

            def step_apply(ni):
                if ni == 2:
                    return
                done = H_COUNT[ni] - (16 if ni == 0 else 8)
                for k in range(KT):
                    act.wait_ge(h_scaled, done + (2 * k + 1 if ni == 0 else k + 1))
                    f(H[:, k, 0:T], H[:, k, 0:T], ACT.Identity, bias=shift_of(ni, k)).then_inc(h_ready, 1)
                    if ni == 0:
                        act.wait_ge(h_scaled, 2 * k + 2)
                        f(H[:, k, T:2 * T], H[:, k, T:2 * T], ACT.Identity, bias=mod[:, k, 1:2]).then_inc(h_ready, 1)

            def step_decay():
                act.wait_ge(sp_arg, 1)
                f(sp[:, 1, :], sp[:, 0, :], ACT.Exp, scale=-1.0).then_inc(sp_exp, 1)
                act.wait_ge(decay_landed, 16)
                for h in range(R_HEADS):
                    act.wait_ge(decay_arg, h + 1)
                    f(decay_m[:, h, 0:2, :], decay_m[:, h, 0:2, :], ACT.Exp, scale=-1.0)
                    f(decay_m[:, h, 2:4, :], decay_in[:, 1024:1536].rearrange("p (a b) -> p a b", a=2), ACT.Exp,
                      scale=sp[:, 7, h:h + 1])
                    if h >= 2:
                        act.wait_ge(decay_ready, h - 1)
                    f(ret_p[h % 2][:, 0:2, :], decay_in[:, 1536:2048].rearrange("p (a b) -> p a b", a=2), ACT.Exp,
                      scale=sp[:, 7, 4 + h:5 + h]).then_inc(decay_exp, 1)

            def step_kr(c):
                for j in range(2):
                    takes(f(k_r[:, 2 * c + j, :], job(("kr", c, j))[:, :], ACT.Copy), ("kr", c, j))

            def evac(name, dst, func=ACT.Copy, scale=1.0):
                def run(c):
                    takes(f(dst[:, 2 * c:2 * c + 2, :], two(job((name, c))), func, scale=scale), (name, c))
                return run

            def step_kvw():
                takes(f(k_w, job(("kvw", "k"))[:, :], ACT.Copy), ("kvw", "k"))

            def step_ret_o(h):
                takes(f(y_r[:, h, :], job(("ret_o", h))[:, 0:T], ACT.Copy), ("ret_o", h))

            def step_ret_mean(p):
                act.wait_ge(emptied["dve"], JOBS[("ret_mean", p)].emptied)
                f(ret_sq[:, 2 * p:2 * p + 2, :], y_r[:, 2 * p:2 * p + 2, :], ACT.Square).then_inc(ret_sq_ready, 1)

            def step_ret_var(p):
                act.wait_ge(emptied["dve"], JOBS[("ret_var", p)].emptied)
                f(rope_b if p else rope_a, rope_b if p else rope_a, ACT.Sqrt).then_inc(ret_std, 1)

            def step_att_s(u):
                na, hd, _ = att_unit(u)
                b = job(("att_s", u))
                act.wait_ge(max_ready, u + 1)
                if u >= 3:
                    act.wait_ge(job_done, JOBS[("att_t", u - 3)].no)
                s = 8 * (u % 4)
                i = f(probs[:, u % 3, :], b[:, :], ACT.Exp, bias=stat[:, s:s + 1], accum_out=stat[:, s + 1:s + 2])
                takes(i, ("att_s", u))
                if not na:
                    f(stat[:, s + 2:s + 3], col("sink", hd), ACT.Exp, bias=stat[:, s:s + 1]).then_inc(sink_ready, 1)

            def step_att_t(u):
                b = job(("att_t", u))
                i, qt = u // 2, u % 2
                if i >= 2:
                    act.wait_ge(job_done, JOBS[("att_o", i - 2)].no)
                takes(f(probs_t[i % 2][:, :, qt * P:(qt + 1) * P], b[:, :].rearrange("p (a b) -> p a b", a=4),
                        ACT.Copy), ("att_t", u))

            def step_tok_major(t, kq):
                if kq == 0:
                    takes(f(h_tok[:, t, 0:512], job(("tok_major", t, kq))[:, :], ACT.Copy), ("tok_major", t, kq))

            def step_router():
                b = job(("router",))
                act.wait_ge(aff_max, 1)
                for t in range(2):
                    i = f(aff[:, t, :], b[:, t * 16:t * 16 + 16], ACT.Exp, bias=stat[:, t:t + 1],
                          accum_out=stat[:, 2 + t:3 + t])
                takes(i, ("router",))

            def step_pick():
                takes(f(gate_b, job(("pick", "gate"))[:, :], ACT.Copy), ("pick", "gate"))

            def step_gather(k):
                if k % 2:
                    takes(f(x_e[:, k, :], job(("gather", k))[:, :], ACT.Copy), ("gather", k))

            def step_pick_t(t):
                takes(f(hot_t[:, :, t * P:(t + 1) * P], job(("pick_t", t))[:, :].rearrange("p (a b) -> p a b", a=4),
                        ACT.Copy), ("pick_t", t))

            def step_experts():
                with act.Fori(0, EXPERTS) as e:
                    act.wait_ge(gate_done, e + 1)
                    f(silu_g, bank[0][:, 0:256], ACT.Silu).then_inc(silu_g_ready, 1)

            def step_ye_t(j, kq):
                if kq == 0:
                    takes(f(y_tok[:, j, 0:512], job(("ye_t", j, kq))[:, :], ACT.Copy), ("ye_t", j, kq))

            def step_nkv(kv):
                b = two(job(("nkv", kv)))
                v = win_f[kv].rearrange("p (gp par) t -> p gp par t", par=2)
                f(v[0:64, :, 0, :], b[0:64, :, :], ACT.Copy)
                f(v[0:64, :, 1, :], b[64:128, :, :], ACT.Copy)
                f(v[64:128, :, 0, 0:T - 1], b[0:64, :, 1:T], ACT.Copy)
                takes(f(v[64:128, :, 1, 0:T - 1], b[64:128, :, 1:T], ACT.Copy), ("nkv", kv))

            def square_part(i, n):
                f(n_sq[:, i % 2, 0:n], qk[:, i * 512:i * 512 + n], ACT.Square).then_inc(n_sq_ready, 1)

            def step_nqk(i):
                act.wait_ge(emptied["dve"], JOBS[("nqk", i)].emptied)
                square_part(i, 512)

            def step_nnorm(i):
                n = 512 if i < 6 else 30
                if i == 4:
                    pass
                if i == 6:
                    act.wait_ge(emptied["dve"], JOBS[("cmp_k",)].emptied)
                    square_part(6, 30)
                act.wait_ge(emptied["dve"], JOBS[("nnorm", i)].emptied)
                f(n_rs[:, i % 2, 0:n], n_rs[:, i % 2, 0:n], ACT.Sqrt).then_inc(n_std, 1)

            def step_ngate():
                takes(f(n_gate.rearrange("p t n -> p (t n)"), job(("ngate",))[:, 0:96], ACT.Sigmoid), ("ngate",))

            def step_cmp(kv, part):
                if part == 1:
                    takes(f(hid_c[:, kv, :, :], job(("cmp", kv))[:, 0:120].rearrange("p (a b) -> p a b", a=2),
                            ACT.Silu), ("cmp", kv))

            def step_cmp_s():
                act.wait_ge(cmp_arg, 1)
                v = cmp_p.rearrange("p t h c -> p (t h c)")
                f(v, v, ACT.Exp).then_inc(cmp_exp, 1)

            def step_nsa_s(u):
                qt = u % 2
                nk = P * (qt + 1)
                b = job(("nsa_s", u))
                act.wait_ge(n_max, u + 1)
                if u >= 3:
                    act.wait_ge(job_done, JOBS[("nsa_t", u - 3)].no)
                s = 8 * (u % 4)
                for br in range(2):
                    i = f(n_p[:, u % 3, br * nk:(br + 1) * nk], b[:, br * nk:(br + 1) * nk], ACT.Exp,
                          bias=stat[:, s + br:s + br + 1], accum_out=stat[:, s + 2 + br:s + 3 + br])
                takes(i, ("nsa_s", u))

            def step_nsa_t(u):
                h, qt = u // 2, u % 2
                b = job(("nsa_t", u))
                if h >= 2:
                    act.wait_ge(job_done, JOBS[("nsa_o", h - 2)].no)
                pt = n_pt[h % 2]
                if qt == 0:
                    f(cmp_pt[h % 2], b[0:N_CMP, 256:512], ACT.Copy)
                    i = f(pt[:, 0, :, 0:P], b[:, 0:256].rearrange("p (a b) -> p a b", a=2), ACT.Copy)
                else:
                    i = f(pt[:, :, :, P:T], b[:, :].rearrange("p (k a b) -> p k a b", k=2, a=2), ACT.Copy)
                takes(i, ("nsa_t", u))

            def step_ffn_in(l, i):
                b = job(("ffn_in", l, i))
                if i >= 2:
                    act.wait_ge(emptied["dve"], JOBS[("ffn_in", l, i - 2)].emptied)
                f(ffn_g[:, i % 2, :], b[:, 0:T], ACT.Silu).then_inc(ffn_silu, 1)

            def step_rnn_in(i):
                b = job(("rnn_in", i))
                f(gelu_g[:, i, :], b[:, 0:T], ACT.Gelu_apprx_tanh)
                takes(f(u_in[:, i, 3:T + 3], b[:, T:2 * T], ACT.Copy), ("rnn_in", i))

            def step_rnn_gate(n):
                b = job(("rnn_gate", n))
                f(rec[:, n, :], b[:, 0:T], ACT.Sigmoid, bias=col("b_a", n)).then_inc(act_step, 1)
                takes(f(inp[:, n, :], b[:, T:2 * T], ACT.Sigmoid, bias=col("b_x", n)), ("rnn_gate", n))

            def step_rnn_scan():
                act.wait_ge(conv_ready, RNN_T)
                act.wait_ge(act_step, RNN_T)
                for i in range(RNN_T):
                    f(thr[:, i, :], rec[:, i, :], ACT.Tanh, scale=sp[:, 6, 8 + i:9 + i]).then_inc(act_step, 1)
                for i in range(RNN_T):
                    act.wait_ge(act_step, RNN_T + i + 1)
                    f(rec[:, i, :], rec[:, i, :], ACT.Exp, scale=sp[:, 7, 8 + i:9 + i]).then_inc(rnn_tanh, 1)
                for i in range(RNN_T):
                    act.wait_ge(rnn_sqrt_in, i + 1)
                    f(thr[:, i, :], thr[:, i, :], ACT.Sqrt).then_inc(rnn_sqrt, 1)

            parts = {"sum_sq": step_sum_sq, "apply": step_apply, "decay": step_decay, "kr": step_kr,
                     "qr": evac("qr", q_r), "gr": evac("gr", g_r, ACT.Silu), "kvw": step_kvw,
                     "qw": evac("qw", q_w, scale=0.125), "qn": evac("qn", q_n, scale=0.125),
                     "gate": evac("gate", gates, ACT.Sigmoid), "ret_o": step_ret_o, "ret_mean": step_ret_mean,
                     "ret_var": step_ret_var, "att_s": step_att_s, "att_t": step_att_t, "tok_major": step_tok_major,
                     "router": step_router, "pick": step_pick, "gather": step_gather, "pick_t": step_pick_t,
                     "experts": step_experts, "ye_t": step_ye_t, "nkv": step_nkv, "nqk": step_nqk,
                     "nnorm": step_nnorm, "ngate": step_ngate, "cmp": step_cmp, "cmp_s": step_cmp_s,
                     "nsa_s": step_nsa_s, "nsa_t": step_nsa_t, "ffn_in": step_ffn_in, "rnn_in": step_rnn_in,
                     "rnn_gate": step_rnn_gate, "rnn_scan": step_rnn_scan}
            for name, *args in STEPS:
                if name in parts:
                    parts[name](*args)

        @block.vector
        def _(dve):
            v = nc.vector
            steps = [0]

            def link(i):
                steps[0] += 1
                i.then_inc(dve_step, 1)
                dve.wait_ge(dve_step, steps[0])

            def job(name):
                dve.wait_ge(job_done, JOBS[name].no)
                return bank[JOBS[name].bank]

            def takes(i, name):
                assert JOBS[name].engine == "dve"
                i.then_inc(emptied["dve"], 1)

            def taken(name):
                dve.wait_ge(emptied[JOBS[name].engine], JOBS[name].emptied)

            def two(b, n=T):
                return b[:, 0:2 * n].rearrange("p (a b) -> p a b", a=2)

            def over(a, n):
                return a.unsqueeze(1).to_broadcast([a.shape[0], n, a.shape[1]])

            def each(a, n):
                return a.unsqueeze(2).to_broadcast([a.shape[0], a.shape[1], n])

            def step_sum_sq(ni):
                if ni == 0:
                    dve.wait_ge(ctx_landed, 16)
                    v.tensor_tensor(sq_0[:, :, T:2 * T], ctx_in, ctx_in, ALU.mult).then_inc(sq_ctx, 1)
                n = 2 * T if ni == 0 else T
                b = job(("sum_sq", ni))
                takes(v.tensor_scalar(norm_t[:, 0, 0:n], b[:, 0:n], 1.0 / D, EPS, ALU.mult, ALU.add), ("sum_sq", ni))
                if ni:
                    finish_std(ni)

            def finish_std(ni):
                n = 2 * T if ni == 0 else T
                dve.wait_ge(std_ready, ni + 1)
                link(v.reciprocal(norm_t[:, 0, 0:n], norm_t[:, 1, 0:n]))

            def step_apply(ni):
                if ni == 0:
                    finish_std(0)
                for k in range(KT):
                    if ni == 2:
                        v.scalar_tensor_tensor(X[:, k, :], X[:, k, :], col("g_final", k), norm_t[:, 0, 0:T], ALU.mult,
                                               ALU.mult).then_inc(x_final, 1)
                        continue
                    v.scalar_tensor_tensor(H[:, k, 0:T], X[:, k, :], mod_a[:, ni, k:k + 1], norm_t[:, 0, 0:T], ALU.mult,
                                           ALU.mult).then_inc(h_scaled, 1)
                    if ni == 0:
                        v.scalar_tensor_tensor(H[:, k, T:2 * T], ctx_in[:, k, :], mod_a[:, 2, k:k + 1],
                                               norm_t[:, 0, T:2 * T], ALU.mult, ALU.mult).then_inc(h_scaled, 1)
                if ni == 2:
                    dve.wait_ge(x_final, 8)

            def step_decay():
                dve.wait_ge(cols_landed, 16)
                a = cols[:, COLS["decays"][0]:COLS["decays"][0] + 19]
                link(v.tensor_scalar(sp[:, 2, :], a, -1.0, None, ALU.mult))
                v.tensor_tensor(sp[:, 0, :], a, sp[:, 2, :], ALU.max).then_inc(sp_arg, 1)
                dve.wait_ge(sp_exp, 1)
                link(v.tensor_scalar(sp[:, 3, :], sp[:, 1, :], 2.0, None, ALU.add))
                link(v.reciprocal(sp[:, 3, :], sp[:, 3, :]))
                link(v.tensor_tensor(sp[:, 3, :], sp[:, 3, :], sp[:, 1, :], ALU.mult))
                link(v.tensor_tensor(sp[:, 4, :], sp[:, 3, :], sp[:, 3, :], ALU.mult))
                link(v.tensor_scalar(sp[:, 5, :], sp[:, 4, :], 1.0 / 17, None, ALU.mult))
                for odd in (15, 13, 11, 9, 7, 5, 3):
                    link(v.scalar_tensor_tensor(sp[:, 5, :], sp[:, 5, :], 1.0 / odd, sp[:, 4, :], ALU.add, ALU.mult))
                link(v.scalar_tensor_tensor(sp[:, 5, :], sp[:, 5, :], 1.0, sp[:, 3, :], ALU.add, ALU.mult))
                link(v.tensor_scalar(sp[:, 2, :], sp[:, 2, :], 0.0, None, ALU.max))
                link(v.scalar_tensor_tensor(sp[:, 6, :], sp[:, 5, :], 2.0, sp[:, 2, :], ALU.mult, ALU.add))
                link(v.tensor_scalar(sp[:, 6, 8:19], sp[:, 6, 8:19], 8.0, None, ALU.mult))
                link(v.tensor_scalar(sp[:, 7, :], sp[:, 6, :], -1.0, None, ALU.mult))
                dve.wait_ge(decay_landed, 16)
                for h in range(R_HEADS):
                    d = decay_m[:, h, 0:2, :].rearrange("p a b -> p (a b)")
                    link(v.tensor_scalar(d, decay_in[:, 0:512], sp[:, 6, h:h + 1], None, ALU.mult))
                    v.scalar_tensor_tensor(d, decay_in[:, 512:1024], sp[:, 6, 4 + h:5 + h], d, ALU.mult,
                                           ALU.add).then_inc(decay_arg, 1)
                for h in range(R_HEADS):
                    dve.wait_ge(decay_exp, h + 1)
                    v.tensor_tensor(decay_m[:, h, 2:4, :], decay_m[:, h, 2:4, :], ret_p[h % 2][:, 0:2, :],
                                    ALU.add).then_inc(decay_ready, 1)

            def scale_col(ni, sc, gain):
                v.scalar_tensor_tensor(mod_a[:, ni, :], sc, 1.0, gain, ALU.add, ALU.mult)

            def gain_of(ni):
                name, at = NORM_GAIN[ni]
                return col(name, at, 8)

            def step_mod_out(part):
                dve.wait_ge(mod_done, part + 1)
                if part < 2:
                    a, b = ((0, 16), (16, 48))[part]
                    takes(v.tensor_tensor(mod[:, a:b, :], mods[:, 2 * a:2 * b].rearrange("p (n t) -> p n t", t=2),
                                          each(col("b_mod", a, b - a), 2), ALU.add), ("mod_out", part))
                    taken(("mod_out", part))
                if part == 0:
                    link(v.scalar_tensor_tensor(mod_a[:, 0, :], mod[:, 8:16, 0], 1.0, gain_of(0), ALU.add, ALU.mult))
                    link(v.scalar_tensor_tensor(mod_a[:, 2, :], mod[:, 8:16, 1], 1.0, gain_of(0), ALU.add, ALU.mult))
                elif part == 1:
                    link(v.scalar_tensor_tensor(mod_a[:, 1, :], mod[:, 32:40, 0], 1.0, gain_of(1), ALU.add, ALU.mult))
                else:
                    takes(v.tensor_tensor(mod2[:, :], mods[:, 96:192], col("ada_b", 0, 96), ALU.add), ("mod_out", 2))
                    taken(("mod_out", 2))
                    for ni in (3, 4, 5, 6):
                        at = SHIFT2[ni] + 8
                        link(v.scalar_tensor_tensor(mod_a[:, ni, :], mod2[:, at:at + 8], 1.0, gain_of(ni), ALU.add,
                                                    ALU.mult))

            def rope(name, dst, n, size):
                b = job(name)
                cos, sin = const(f"cos{size}"), const(f"sin{size}")
                if n == 1:
                    c, s, ps = cos, sin, b[:, 0:T]
                    ta, tb = rope_a[:, 0, :], rope_b[:, 0, :]
                else:
                    c, s, ps = over(cos, 2), over(sin, 2), two(b)
                    ta, tb = rope_a, rope_b
                takes(v.tensor_tensor(tb, ps, s, ALU.mult), name)
                link(v.tensor_tensor(ta, dst, c, ALU.mult))
                taken(name)
                v.tensor_tensor(dst, ta, tb, ALU.add).then_inc(roped, 1)
                rope_no[0] += 1
                dve.wait_ge(roped, rope_no[0])

            rope_no = [0]

            def step_rot(what, p):
                dst, n, size = {"kr": (k_r[:, 2 * p:2 * p + 2, 0:T], 2, 128), "qr": (q_r[:, 2 * p:2 * p + 2, :], 2, 128),
                                "kw": (k_w[:, 0:T], 1, 64), "qw": (q_w[:, 2 * p:2 * p + 2, :], 2, 64)}[what]
                if what == "kr" and p == 0:
                    dve.wait_ge(consts_landed, 16)
                rope(("rot", what, p), dst, n, size)

            def values(name, dst):
                def run(c):
                    for i in range(2):
                        takes(v.tensor_copy(dst[:, 2 * i:2 * i + 2, c * T:(c + 1) * T], two(job((name, c, i)))),
                              (name, c, i))
                return run

            def step_kvw():
                takes(v.tensor_copy(v_w, job(("kvw", "v"))[:, :].rearrange("p (a b) -> p a b", a=4)), ("kvw", "v"))

            def step_kn(c):
                for j in range(2):
                    takes(v.tensor_copy(k_n[:, 2 * c + j, :], job(("kn", c, j))[:, :]), ("kn", c, j))

            def step_ret_s(h, kp):
                b = job(("ret_s", h, kp))
                if h >= 2 and kp == 0:
                    dve.wait_ge(job_done, JOBS[("ret_o", h - 2)].no)
                takes(v.scalar_tensor_tensor(ret_p[h % 2][:, 2 * kp:2 * kp + 2, :], two(b), float(P) ** -0.5,
                                             decay_m[:, h, 2 * kp:2 * kp + 2, :], ALU.mult, ALU.mult), ("ret_s", h, kp))

            def step_ret_mean(p):
                y = y_r[:, 2 * p:2 * p + 2, :]
                takes(v.scalar_tensor_tensor(y, two(job(("ret_mean", p))), -1.0 / P, y, ALU.mult, ALU.add),
                      ("ret_mean", p))

            def step_ret_var(p):
                t = rope_b if p else rope_a
                b = job(("ret_var", p))
                takes(v.tensor_scalar(t, two(b), 1.0 / P, EPS, ALU.mult, ALU.add), ("ret_var", p))
                dve.wait_ge(ret_std, p + 1)
                link(v.reciprocal(t, t))
                y = y_r[:, 2 * p:2 * p + 2, :]
                link(v.tensor_tensor(y, y, t, ALU.mult))
                for h in (2 * p, 2 * p + 1):
                    i = v.scalar_tensor_tensor(y_r[:, h, :], y_r[:, h, :], col("ret_gn", h), g_r[:, h, :], ALU.mult,
                                               ALU.mult)
                i.then_inc(ret_ready, 1)

            def step_att_s(u):
                na, hd, qt = att_unit(u)
                b = job(("att_s", u))
                if u == 16:
                    dve.wait_ge(bias_ready, 1)
                if na:
                    m = bias_n[:, hd, qt, :]
                else:
                    m = const("win_mask")[:, qt * T:(qt + 1) * T]
                link(v.tensor_tensor(b[:, 0:T], b[:, 0:T], m, ALU.add))
                s = 8 * (u % 4)
                if na:
                    v.tensor_reduce(stat[:, s:s + 1], b[:, :], AX, ALU.max, negate=True).then_inc(max_ready, 1)
                else:
                    link(v.tensor_reduce(stat[:, s + 3:s + 4], b[:, :], AX, ALU.max))
                    v.tensor_scalar(stat[:, s:s + 1], stat[:, s + 3:s + 4], col("sink", hd), -1.0, ALU.max,
                                    ALU.mult).then_inc(max_ready, 1)

            def step_att_t(u):
                na = att_unit(u)[0]
                s = 8 * (u % 4)
                taken(("att_s", u))
                if not na:
                    dve.wait_ge(sink_ready, u + 1)
                    link(v.tensor_tensor(stat[:, s + 1:s + 2], stat[:, s + 1:s + 2], stat[:, s + 2:s + 3], ALU.add))
                link(v.reciprocal(stat[:, s + 4:s + 5], stat[:, s + 1:s + 2]))
                v.tensor_scalar(probs[:, u % 3, :], probs[:, u % 3, :], stat[:, s + 4:s + 5], None,
                                ALU.mult).then_inc(probs_ready, 1)

            def step_att_o(i):
                na, hd, _ = att_unit(2 * i)
                t, half = att_head(na, hd)
                rows = slice(64 * half, 64 * half + 64)
                takes(v.tensor_copy((y_n if na else y_w)[rows, t, :], job(("att_o", i))[rows, 0:T]), ("att_o", i))

            def step_branch(ch, br):
                if ch == 0 and br == 0:
                    taken(("gate", 11))
                for p in range(2):
                    name = ("branch", ch, br, p)
                    at = 4 * ch + 2 * p
                    g = gates[:, 8 * br + at:8 * br + at + 2, :]
                    takes(v.tensor_tensor(g, g, two(job(name)), ALU.mult), name)
                if br == 2:
                    taken(name)
                    for p in range(2):
                        at = 4 * ch + 2 * p
                        m = merged[:, at:at + 2, :]
                        link(v.tensor_tensor(m, gates[:, at:at + 2, :], gates[:, 8 + at:10 + at, :], ALU.add))
                        v.tensor_tensor(m, m, gates[:, 16 + at:18 + at, :], ALU.add).then_inc(merged_ready, 1)

            def add_to_x(name, gain, at):
                b = job(name)
                for j in range(2):
                    i = v.scalar_tensor_tensor(X[:, at + j, :], b[:, j * T:(j + 1) * T], gain(at + j), X[:, at + j, :],
                                               ALU.mult, ALU.add)
                takes(i, name)
                taken(name)

            def step_mix_out(c):
                add_to_x(("mix_out", c), lambda n: mod[:, 16 + n, 0:1], 2 * c)

            def step_tok_major(t, kq):
                if kq == 1:
                    takes(v.tensor_copy(h_tok[:, t, 512:1024], job(("tok_major", t, kq))[:, :]), ("tok_major", t, kq))

            def step_router():
                b = job(("router",))
                v.tensor_reduce(stat[:, 0:2], b[:, 0:32].rearrange("p (t e) -> p t e", t=2), AX, ALU.max,
                                negate=True).then_inc(aff_max, 1)
                taken(("router",))
                link(v.reciprocal(stat[:, 4:6], stat[:, 2:4]))
                v.tensor_tensor(aff, aff, each(stat[:, 4:6], 16), ALU.mult).then_inc(aff_ready, 1)

            def step_affinity():
                takes(v.tensor_copy(aff_t, job(("affinity",))[0:16, 0:T]), ("affinity",))
                taken(("affinity",))
                for r in range(4):
                    link(v.max(top_v[:, 8 * r:8 * r + 8], aff_t))
                    link(v.max_index(top_i[:, 8 * r:8 * r + 8], top_v[:, 8 * r:8 * r + 8], aff_t))
                    if r < 3:
                        link(v.match_replace(aff_t, top_v[:, 8 * r:8 * r + 8], aff_t, -1.0))
                link(v.tensor_copy(top_f, top_i[:, :]))
                own = const("own", 16).rearrange("p (e c) -> p e c", e=16)
                link(v.tensor_tensor(spread_i, own, over(top_f, 16), ALU.mult))
                v.tensor_tensor(spread_g, own, over(top_v, 16), ALU.mult).then_inc(spread_ready, 1)

            def step_pick():
                b = job(("pick", "idx"))
                for t in range(2):
                    i = v.tensor_scalar(hot[:, t, :], b[:, :], const("token")[:, t:t + 1], None, ALU.is_equal)
                takes(i, ("pick", "idx"))

            def step_gather(k):
                if k % 2 == 0:
                    takes(v.tensor_copy(x_e[:, k, :], job(("gather", k))[:, :]), ("gather", k))

            def step_experts():
                taken(("gather", 7))
                taken(("pick", "gate"))
                taken(("gather", 6))
                xe = x_e.rearrange("p k (e c) -> p k e c", e=EXPERTS)
                ye = y_e.rearrange("p k (e c) -> p k e c", e=EXPERTS)
                gb = gate_b.rearrange("p (e c) -> p e c", e=EXPERTS)
                link(v.tensor_copy(stat[:, 63:64], gate_b[:, 0:1]))
                dve.sem_inc(ye_taken, 1)
                with dve.Fori(0, EXPERTS) as e:
                    v.tensor_copy(x_cur, xe[:, :, e, :]).then_inc(x_cur_ready, 1)
                    dve.wait_ge(silu_g_ready, e + 1)
                    dve.wait_ge(up_done, e + 1)
                    v.tensor_tensor(hid, silu_g, bank[1][:, 0:256], ALU.mult).then_inc(hid_ready, 1)
                    dve.wait_ge(down_done, e + 1)
                    v.tensor_tensor(ye[:, :, e, :], bank[2][:, 0:256].rearrange("p (k c) -> p k c", k=KT),
                                    over(gb[:, e, :], KT), ALU.mult).then_inc(ye_taken, 1)

            def step_ye_t(j, kq):
                if kq == 1:
                    takes(v.tensor_copy(y_tok[:, j, 512:1024], job(("ye_t", j, kq))[:, :]), ("ye_t", j, kq))

            def step_combine(p):
                add_to_x(("combine", p), lambda n: mod[:, 40 + n, 0:1], 2 * p)

            def step_nkv(kv):
                taken(("nkv", kv))
                f4 = win_f[kv]
                for half in range(2):
                    rows = slice(64 * half, 64 * half + 64)
                    for g in range(4):
                        src = f4[rows, g, 0:240].rearrange("p (c j l) -> p j c l", c=15, l=2)[:, :, :, 0]
                        pos = col("pos", 16 * kv, 16)[rows]
                        i = v.tensor_tensor(flat[kv][rows, 0:8, g, :], src, each(pos[:, 0:8], 15), ALU.add)
                        src = f4[rows, g, 16:256].rearrange("p (c j l) -> p j c l", c=15, l=2)[:, :, :, 0]
                        i = v.tensor_tensor(flat[kv][rows, 8:16, g, :], src, each(pos[:, 8:16], 15), ALU.add)
                i.then_inc(flat_ready, 1)

            def step_nqk(i):
                takes(v.tensor_copy(qk[:, i * 512:(i + 1) * 512], job(("nqk", i))[:, :]), ("nqk", i))

            def step_nnorm(i):
                n = 512 if i < 6 else 30
                b = job(("nnorm", i))
                rs = n_rs[:, i % 2, 0:n]
                takes(v.tensor_scalar(rs, b[:, 0:n], 1.0 / 64, EPS, ALU.mult, ALU.add), ("nnorm", i))
                dve.wait_ge(n_std, i + 1)
                link(v.reciprocal(rs, rs))
                gain = (col("k_gain", 1), col("k_gain", 2))[i] if i < 2 else (
                    stat[:, 40:41] if i < 6 else col("k_gain", 0))
                if i == 2:
                    link(v.tensor_scalar(stat[:, 40:41], col("q_gain"), 0.125, None, ALU.mult))
                z = qk[:, i * 512:i * 512 + n]
                v.scalar_tensor_tensor(z, z, gain, rs, ALU.mult, ALU.mult).then_inc(n_normed, 1)

            def step_nv(i):
                takes(v.tensor_copy(v_s[i], two(job(("nv", i)))), ("nv", i))

            def step_cmp_k():
                takes(v.tensor_copy(qk[:, 3072:3102], job(("cmp_k",))[:, 0:30]), ("cmp_k",))

            def step_cmp_v():
                takes(v.tensor_copy(v_c, job(("cmp_v",))[0:N_CMP, 0:256].rearrange("p (a b) -> p a b", a=4)), ("cmp_v",))

            def step_cmp_s():
                add = const("cmp_add").rearrange("p (t c) -> p t c", t=2)
                keep = const("cmp_keep").rearrange("p (t c) -> p t c", t=2)
                for half in range(2):
                    ps = job(("cmp_s", half))[:, 0:240].rearrange("p (t q c) -> p t q c", t=2, q=8)
                    for t in range(2):
                        for gp in range(2):
                            h = 4 * (2 * gp + half)
                            i = v.tensor_tensor(cmp_p[:, t, h:h + 4, :], ps[:, t, 4 * gp:4 * gp + 4, :],
                                                over(add[:, t, :], 4), ALU.add)
                    takes(i, ("cmp_s", half))
                taken(("cmp_s", 1))
                link(v.tensor_reduce(cmp_m, cmp_p, AX, ALU.max))
                for t in range(2):
                    i = v.tensor_tensor(cmp_p[:, t, :, :], cmp_p[:, t, :, :], each(cmp_m[:, t, :], 15), ALU.subtract)
                i.then_inc(cmp_arg, 1)
                dve.wait_ge(cmp_exp, 1)
                for t in range(2):
                    link(v.tensor_tensor(cmp_p[:, t, :, :], cmp_p[:, t, :, :], over(keep[:, t, :], 16), ALU.mult))
                link(v.tensor_reduce(cmp_m, cmp_p, AX, ALU.add))
                link(v.tensor_scalar(cmp_m, cmp_m, TINY, None, ALU.max))
                link(v.reciprocal(cmp_m, cmp_m))
                taken(("ngate",))
                g = n_gate.rearrange("p t (h b) -> p t h b", b=3)
                link(v.tensor_tensor(cmp_m, cmp_m, g[:, :, :, 0], ALU.mult))
                for t in range(2):
                    i = v.tensor_tensor(cmp_p[:, t, :, :], cmp_p[:, t, :, :], each(cmp_m[:, t, :], 15), ALU.mult)
                i.then_inc(cmp_ready, 1)

            def step_nsa_s(u):
                qt = u % 2
                nk = P * (qt + 1)
                b = two(job(("nsa_s", u)), nk)
                diag = b[:, :, qt * P:(qt + 1) * P]
                link(v.tensor_tensor(diag, diag, over(const("causal"), 2), ALU.add))
                s = 8 * (u % 4)
                v.tensor_reduce(stat[:, s:s + 2], b, AX, ALU.max, negate=True).then_inc(n_max, 1)

            def step_nsa_t(u):
                h, qt = u // 2, u % 2
                nk = P * (qt + 1)
                s = 8 * (u % 4)
                taken(("nsa_s", u))
                link(v.reciprocal(stat[:, s + 4:s + 6], stat[:, s + 2:s + 4]))
                link(v.tensor_tensor(stat[:, s + 4:s + 6], stat[:, s + 4:s + 6], n_gate[:, qt, 3 * h + 1:3 * h + 3],
                                     ALU.mult))
                z = n_p[:, u % 3, 0:2 * nk].rearrange("p (a b) -> p a b", a=2)
                v.tensor_tensor(z, z, each(stat[:, s + 4:s + 6], nk), ALU.mult).then_inc(n_ready, 1)

            def step_nsa_o(h):
                qi, half, _ = nsa_head(h)
                rows = slice(64 * half, 64 * half + 64)
                takes(v.tensor_copy(o_n[rows, qi, :], job(("nsa_o", h))[rows, 0:T]), ("nsa_o", h))

            def step_nsa_out(c):
                add_to_x(("nsa_out", c), lambda n: mod2[:, 16 + n:17 + n], 2 * c)

            def step_ffn_in(l, i):
                b = job(("ffn_in", l, i))
                dve.wait_ge(ffn_silu, FFN_T * l + i + 1)
                takes(v.tensor_tensor(ffn_h[:, i, :], ffn_g[:, i % 2, :], b[:, T:2 * T], ALU.mult), ("ffn_in", l, i))

            def step_ffn_add(l):
                for p in range(4):
                    add_to_x(("ffn_add", l, p), lambda n: mod2[:, 48 * l + 40 + n:48 * l + 41 + n], 2 * p)

            def step_rnn_in(i):
                if i == 0:
                    link(v.memset(u_in[:, :, 0:3], 0.0))
                taken(("rnn_in", i))
                link(v.tensor_scalar(u_c[:, i, :], u_in[:, i, 0:T], col("conv_w", i), col("conv_b", i), ALU.mult,
                                     ALU.add))
                for k in range(1, 4):
                    j = v.scalar_tensor_tensor(u_c[:, i, :], u_in[:, i, k:k + T], col("conv_w", 11 * k + i), u_c[:, i, :],
                                               ALU.mult, ALU.add)
                    if k < 3:
                        link(j)
                j.then_inc(conv_ready, 1)

            def step_rnn_scan():
                for i in range(RNN_T):
                    dve.wait_ge(rnn_tanh, i + 1)
                    link(v.tensor_scalar(rnn_d[:, i % 2, :], thr[:, i, :], 1.0, None, ALU.add))
                    link(v.reciprocal(rnn_d[:, i % 2, :], rnn_d[:, i % 2, :]))
                    v.scalar_tensor_tensor(thr[:, i, :], thr[:, i, :], 2.0, rnn_d[:, i % 2, :], ALU.mult,
                                           ALU.mult).then_inc(rnn_sqrt_in, 1)
                    link(v.tensor_tensor(inp[:, i, :], inp[:, i, :], u_c[:, i, :], ALU.mult))
                for i in range(RNN_T):
                    dve.wait_ge(rnn_sqrt, i + 1)
                    link(v.tensor_tensor(inp[:, i, :], inp[:, i, :], thr[:, i, :], ALU.mult))
                    link(v.tensor_tensor_scan(u_c[:, i, :], rec[:, i, :], inp[:, i, :], 0.0, ALU.mult, ALU.add))
                    v.tensor_tensor(gelu_g[:, i, :], gelu_g[:, i, :], u_c[:, i, :], ALU.mult).then_inc(rnn_ready, 1)

            def step_rnn_add():
                for p in range(4):
                    add_to_x(("rnn_add", p), lambda n: mod2[:, 48 + 16 + n:48 + 17 + n], 2 * p)

            parts = {"sum_sq": step_sum_sq, "apply": step_apply, "decay": step_decay, "mod_out": step_mod_out,
                     "rot": step_rot, "vr": values("vr", v_r), "vn": values("vn", v_n), "kvw": step_kvw, "kn": step_kn,
                     "ret_s": step_ret_s, "ret_mean": step_ret_mean, "ret_var": step_ret_var, "att_s": step_att_s,
                     "att_t": step_att_t, "att_o": step_att_o, "branch": step_branch, "mix_out": step_mix_out,
                     "tok_major": step_tok_major, "router": step_router, "affinity": step_affinity, "pick": step_pick,
                     "gather": step_gather, "experts": step_experts, "ye_t": step_ye_t, "combine": step_combine,
                     "nkv": step_nkv, "nqk": step_nqk, "nnorm": step_nnorm, "nv": step_nv, "cmp_k": step_cmp_k,
                     "cmp_v": step_cmp_v, "cmp_s": step_cmp_s, "nsa_s": step_nsa_s, "nsa_t": step_nsa_t,
                     "nsa_o": step_nsa_o, "nsa_out": step_nsa_out, "ffn_in": step_ffn_in, "ffn_add": step_ffn_add,
                     "rnn_in": step_rnn_in, "rnn_scan": step_rnn_scan, "rnn_add": step_rnn_add}
            for name, *args in STEPS:
                if name in parts:
                    parts[name](*args)


W_IN = {"qr": 0, "kr": 512, "vr": 1024, "gr": 1536, "qw": 2048, "kw": 2560, "vw": 2688, "qn": 2816, "kn": 3328,
        "vn": 3840, "gate": 4352}
WIN_ORDER = [0, 4, 1, 5, 2, 6, 3, 7]
NSA_ORDER = [4 * (2 * gp + half) + t for gp in range(2) for t in range(4) for half in range(2)]


def weight_stream(np, i):
    w = np.zeros((len(CHUNKS), P, CHUNK), np.float32)
    head = [h * 64 + d for h in WIN_ORDER for d in range(64)]
    nsa_head = [h * 64 + d for h in NSA_ORDER for d in range(64)]
    w_in, nsa_in = i["w_in"][0], i["nsa_w_in_2"][0]
    rg = np.zeros((2, RNN_T * P, RNN_T * P), np.float32)
    for g, name in enumerate(("rg_w_a_2", "rg_w_x_2")):
        for b in range(16):
            rg[g, 88 * b:88 * b + 88, 88 * b:88 * b + 88] = i[name][0][b]

    def cut(m, k):
        return m.reshape(k, P, -1).transpose(1, 0, 2).reshape(P, -1)

    for c, (name, *a) in enumerate(CHUNKS):
        if name == "mod":
            n = 256 * a[0]
            m = i["w_mod"][0] if n < 6144 else i["ada_w_2"][n // 6144 - 1]
            w[c] = cut(m[:, n % 6144:n % 6144 + 256], 8)
        elif name == "kvw":
            w[c] = cut(w_in[:, W_IN["kw"]:W_IN["kw"] + 256], 8)
        elif name == "qw":
            w[c] = cut(w_in[:, W_IN["qw"]:W_IN["qw"] + 512][:, head][:, 256 * a[0]:256 * a[0] + 256], 8)
        elif name in W_IN:
            n = W_IN[name] + 256 * a[0]
            w[c] = cut(w_in[:, n:n + 256], 8)
        elif name == "branch":
            m = (i["w_ret"][0], i["w_win"][0][head], i["w_na"][0])[a[1]]
            w[c] = cut(m[:, 512 * a[0]:512 * a[0] + 512], 4)
        elif name == "mix_out":
            w[c] = cut(i["w_out"][0][:, 256 * a[0]:256 * a[0] + 256], 8)
        elif name == "expert":
            m = i[("w_exp_gate", "w_exp_up", "w_exp_down")[a[1] // 4]][0][a[0]]
            w[c] = cut(m[:, a[1] % 4 * 256:a[1] % 4 * 256 + 256], 8)
        elif name == "nkv":
            w[c] = cut(nsa_in[:, 1024 + 256 * a[0]:1280 + 256 * a[0]], 8)
        elif name == "nqk":
            m = nsa_in[:, 0:1024][:, nsa_head]
            cols = (nsa_in[:, 1536:1792], nsa_in[:, 2048:2304])[a[0]] if a[0] < 2 else \
                m[:, 256 * (a[0] - 2):256 * (a[0] - 1)]
            w[c] = cut(cols, 8)
        elif name == "nv":
            w[c] = cut(nsa_in[:, 1792 + 512 * a[0]:2048 + 512 * a[0]], 8)
        elif name == "cmp":
            w[c] = cut(i["nsa_cmp_w1_2"][0][a[0]][1024 * a[1]:1024 * a[1] + 1024], 8)
        elif name == "nsa_out":
            w[c] = cut(i["nsa_w_out_2"][0][nsa_head][:, 256 * a[0]:256 * a[0] + 256], 8)
        elif name in ("ffn_in", "rnn_in"):
            m = i["ffn_w_in_2"][a[0]] if name == "ffn_in" else i["rg_w_in_2"][0]
            half, n = m.shape[1] // 2, P * a[-1]
            w[c] = cut(np.concatenate([m[:, n:n + P], m[:, half + n:half + n + P]], axis=1), 8)
        elif name == "ffn_out":
            w[c] = cut(i["ffn_w_out_2"][a[0]][256 * a[1]:256 * a[1] + 256], 2)
        elif name == "rnn_out":
            m = i["rg_w_out_2"][0][256 * a[0]:256 * a[0] + 256]
            w[c, :, 0:m.shape[0] // P * D] = cut(m, m.shape[0] // P)
        elif name == "gates":
            for j, (n, g, k) in enumerate(GATE_TILES[16 * a[0]:16 * a[0] + 16]):
                w[c, :, j * P:(j + 1) * P] = rg[g, k * P:(k + 1) * P, n * P:(n + 1) * P]
    return w


def column_pack(np, i):
    def tiles(x):
        return x.reshape(-1, P).T

    def every(x):
        return np.broadcast_to(x.reshape(1, -1), (P, x.size))

    def twice(x):
        return np.concatenate([x, x], axis=-1).reshape(-1, P).T

    both = np.stack([i["c"][0].reshape(8, P), i["c_ctx"].reshape(8, P)], axis=1).reshape(16, P).T
    parts = {"c_both": both, "c_2": tiles(i["c_2"][0]), "b_mod": tiles(i["b_mod"][0]),
             "ada_b": tiles(i["ada_b_2"].reshape(-1)), "g_mix": tiles(i["g_mix"][0]), "g_ffn": tiles(i["g_ffn"][0]),
             "g_final": tiles(i["g_final"]), "norm1": tiles(i["norm1_g_2"].reshape(-1)),
             "norm2": tiles(i["norm2_g_2"].reshape(-1)), "ret_gn": tiles(i["ret_gn"][0]),
             "decays": every(i["ret_decay_logit"][0].reshape(-1)), "lam": tiles(i["rg_lam_2"][0]),
             "sink": every(i["win_sink"][0][WIN_ORDER]), "q_gain": twice(i["nsa_q_gain_2"][0]),
             "k_gain": twice(i["nsa_k_gain_2"][0]), "pos": tiles(i["nsa_cmp_pos_2"][0].reshape(-1)),
             "conv_w": tiles(i["rg_conv_w_2"][0].reshape(-1)), "conv_b": tiles(i["rg_conv_b_2"][0]),
             "b_a": tiles(i["rg_b_a_2"][0].reshape(-1)), "b_x": tiles(i["rg_b_x_2"][0].reshape(-1))}
    return np.ascontiguousarray(np.concatenate([parts[k] for k in COLS], axis=1))


def constant_pack(np):
    f = np.float32
    p, t = np.arange(P), np.arange(T)

    def rope(size):
        nf = size // 4
        inv = f(10000.0) ** (-np.arange(nf, dtype=f) / f(nf))
        ang = np.concatenate([(t // 64).astype(f)[:, None] * inv, (t % 64).astype(f)[:, None] * inv], axis=1)
        a = np.tile(ang.T, (P // (size // 2), 1))
        m = np.zeros((P, P), f)
        for base in range(0, P, size):
            for d in range(size // 2):
                m[base + d + size // 2, base + d] = -1
                m[base + d, base + d + size // 2] = 1
        return m, np.cos(a).astype(f), np.sin(a).astype(f)

    rot128, cos128, sin128 = rope(128)
    rot64, cos64, sin64 = rope(64)
    q2 = p[:, None, None] + P * np.arange(2)[None, :, None]
    k = t[None, None, :]
    win = np.where(np.abs(k - q2) <= 128, 0, NEG).reshape(P, -1)
    cq, ck = p % 64, t % 64
    start = np.clip(cq - 8, 0, 48)
    na = np.where((ck[None] >= start[:, None]) & (ck[None] < start[:, None] + 16), 0, NEG)
    ends = np.arange(N_CMP) * 16 + 31
    seen = ends[None, None, :] <= q2
    parts = {"ident": np.eye(P), "ones": np.ones((P, P)), "half_ones": np.kron(np.eye(2), np.ones((64, 64))),
             "rot128": rot128, "rot64": rot64, "cos128": cos128, "sin128": sin128, "cos64": cos64, "sin64": sin64,
             "win_mask": win, "na_mask": na, "causal": np.where(p[None] <= p[:, None], 0, NEG),
             "cmp_add": np.where(seen, 0, NEG).reshape(P, -1), "cmp_keep": seen.reshape(P, -1),
             "own": np.kron(np.eye(P)[:, 0:16], np.ones((1, 32))), "token": p[:, None] + P * np.arange(2)[None]}
    consts = np.concatenate([parts[n].astype(f) for n in CONSTS], axis=1)
    key = (p[:, None, None] + P * np.arange(2)[None, :, None])
    decay = np.concatenate([x.reshape(P, -1) for x in (np.maximum(k - key, 0), np.maximum(key - k, 0), k + T - key,
                                                       T - k + key)], axis=1)
    return consts, decay.astype(f)


def kernel(**inputs):
    import numpy as np
    import concourse.bacc as bacc
    from concourse.bass_utils import run_bass_kernel_spmd

    i = {k: np.asarray(x) for k, x in inputs.items()}
    consts, decay = constant_pack(np)

    def feature_major(x):
        return np.ascontiguousarray(x.T.reshape(8, P, T).transpose(1, 0, 2))

    rows = np.arange(4)
    ri = rows[None, :] - rows[:, None] + 7
    cc = np.arange(64)
    ci = np.clip(cc[None, :] - cc[:, None], -15, 15) + 15
    bias = i["na_rpb"][0][:, ri[:, None, :, None], ci[None, :, None, :]].reshape(8, 2, P, T)
    wide = np.concatenate([i["w_router"][0], i["nsa_w_in_2"][0][:, 2560:2608]], axis=1)
    arrays = {
        "w": weight_stream(np, i), "cols": column_pack(np, i), "consts": consts, "decay": decay,
        "x": feature_major(i["x"][0]), "ctx": feature_major(i["ctx"][0]),
        "bias": np.ascontiguousarray(bias.transpose(2, 0, 1, 3).reshape(P, -1)),
        "wide": np.ascontiguousarray(wide.reshape(8, P, 64).transpose(1, 0, 2)),
        "w2c": np.ascontiguousarray(i["nsa_cmp_w2_2"][0].reshape(2, 2, P, 64).transpose(2, 0, 1, 3)),
    }
    nc = bacc.Bacc("TRN2", target_bir_lowering=False, num_devices=1)
    aps = {n: nc.dram_tensor(f"in_{n}", a.shape, F32, kind="ExternalInput").ap() for n, a in arrays.items()}
    out = nc.dram_tensor("out_t", (P, KT, T), F32, kind="ExternalOutput").ap()
    build(nc, aps["w"], aps, out)
    r = run_bass_kernel_spmd(nc, [{f"in_{n}": a for n, a in arrays.items()}], core_ids=[0])
    y = r.results[0]["out_t"]
    return np.ascontiguousarray(y.transpose(2, 1, 0).reshape(1, T, D))
```

```python
from contextlib import ExitStack

import concourse.bass as bass
from concourse import mybir

F32 = mybir.dt.float32
F32R = mybir.dt.float32r
U32 = mybir.dt.uint32
ALU = mybir.AluOpType
ACT = mybir.ActivationFunctionType
AX = mybir.AxisListType.X

P = 128
D = 1024
T = 256
KT = D // P
EPS = 1e-6
NEG = -1e30
TINY = 1.1754944e-38
N_MOD = 6
EXPERTS, CAP = 16, 32
R_HEADS = 4
FFN_T = 22
RNN_T = 11
N_CMP = 15
NSA_HEADS = 16
CHUNK = 2048
SLOTS_A, SLOTS = 6, 12
SLOTS_B, SPLITS = 9, 3
MOD_BLOCKS = 9
LAG = 3
RNN_GROUPS = [range(0, 3), range(3, 7), range(7, RNN_T)]
BUFS = LAG + 1

COLS = {}
CONSTS = {}
DECAY = {}


def lay(table, items):
    at = 0
    for name, width in items:
        table[name] = (at, width)
        at += width
    return at


N_COLS = lay(COLS, [("c_both", 16), ("c_2", 8), ("b_mod", 48), ("ada_b", 96), ("g_mix", 8), ("g_ffn", 8),
                    ("g_final", 8), ("norm1", 16), ("norm2", 16), ("ret_gn", 4), ("decays", 8), ("lam", 11),
                    ("sink", 8), ("q_gain", 1), ("k_gain", 3), ("pos", 32), ("conv_w", 44), ("conv_b", 11),
                    ("b_a", 11), ("b_x", 11)])
N_CONSTS = lay(CONSTS, [("ident", 128), ("ones", 128), ("half_ones", 128), ("rot128", 128), ("rot64", 128),
                        ("cos128", 256), ("sin128", 256), ("cos64", 256), ("sin64", 256), ("win_mask", 512),
                        ("na_mask", 256), ("causal", 128), ("cmp_add", 30), ("cmp_keep", 30), ("own", 512),
                        ("token", 2)])
N_DECAY = lay(DECAY, [("ahead", 512), ("behind", 512), ("ctx_f", 512), ("ctx_b", 512)])


def plan_steps():
    s = [("sum_sq", 0), ("decay",)]
    s += [("mod", 0, k) for k in range(KT)] + [("mod_row", 0), ("mod_out", 0), ("apply", 0)]
    fill = []
    for b in range(1, MOD_BLOCKS):
        fill += [("mod", b, k) for k in range(KT)] + [("mod_row", b), ("mod_out", b)]

    def with_fill(steps, n):
        for x in steps:
            s.append(x)
            for _ in range(n):
                if fill:
                    s.append(fill.pop(0))

    with_fill([("kr", 0), ("kr", 1), ("qr", 0), ("qr", 1), ("vr", 0), ("rot", "kr", 0), ("vr", 1),
               ("rot", "kr", 1), ("gr", 0), ("rot", "qr", 0), ("gr", 1), ("rot", "qr", 1), ("kvw",),
               ("qw", 0), ("qw", 1), ("rot", "kw", 0), ("kn", 0), ("rot", "qw", 0), ("kn", 1),
               ("rot", "qw", 1)], 2)
    s += [("ret_s", 0, 0), ("ret_s", 0, 1), ("vn", 0), ("ret_s", 1, 0), ("ret_s", 1, 1), ("ret_o", 0), ("vn", 1),
          ("ret_s", 2, 0), ("ret_s", 2, 1), ("ret_o", 1), ("qn", 0), ("ret_s", 3, 0), ("ret_s", 3, 1),
          ("ret_o", 2), ("qn", 1), ("ret_o", 3), ("na_bias",), ("gate", 0), ("ret_mean", 0), ("ret_mean", 1),
          ("gate", 1), ("ret_var", 0), ("ret_var", 1)]
    gates = [("gate", i) for i in range(2, 12)]
    units = 32
    for i in range(units + LAG + 2):
        if i < units:
            s.append(("att_s", i))
        if gates:
            s.append(gates.pop(0))
        if fill:
            s.append(fill.pop(0))
        if 0 <= i - LAG + 1 < units:
            s.append(("att_n", i - LAG + 1))
        if 0 <= i - LAG < units:
            s.append(("att_t", i - LAG))
        if 0 <= i - LAG - 1 < units and (i - LAG - 1) % 2:
            s.append(("att_o", (i - LAG - 1) // 2))
        if i == units:
            s += fill
            fill = []
    s += [("branch", ch, b) for ch in range(2) for b in range(3)]
    s += [("mix_out", c) for c in range(4)]
    s += [("sum_sq", 1), ("apply", 1)]
    s += [("tok_major", t, kq) for t in range(2) for kq in range(2)] + [("router",), ("affinity",), ("pick",)]
    s += [("gather", k) for k in range(KT)] + [("pick_t", t) for t in range(2)]
    s += [("experts",)]
    s += [("combine", p) for p in range(4)]
    s += [("sum_sq", 2), ("apply", 2), ("sum_sq", 3), ("apply", 3)]
    s += [("nkv", 0), ("nkv", 1), ("nqk", 0), ("nqk", 1), ("cmp", 0, 0), ("cmp", 0, 1), ("cmp", 1, 0),
          ("cmp", 1, 1), ("cmp_k",), ("cmp_v",), ("nnorm", 0), ("nnorm", 1)]
    s += [("nqk", 2), ("nqk", 3), ("nnorm", 2), ("nqk", 4), ("nnorm", 3), ("nqk", 5), ("nnorm", 4), ("nv", 0),
          ("nnorm", 5), ("nv", 1), ("nnorm", 6), ("ngate",), ("cmp_s",)]
    units = 2 * NSA_HEADS
    for i in range(units + LAG + 2):
        if i < units:
            s.append(("nsa_s", i))
        if 0 <= i - LAG + 1 < units:
            s.append(("nsa_n", i - LAG + 1))
        if 0 <= i - LAG < units:
            s.append(("nsa_t", i - LAG))
        if 0 <= i - LAG - 1 < units and (i - LAG - 1) % 2:
            s.append(("nsa_o", (i - LAG - 1) // 2))
    s += [("nsa_out", c) for c in range(4)]
    s += [("sum_sq", 4), ("apply", 4)]
    s += [("ffn_in", 0, i) for i in range(FFN_T)] + [("ffn_out", 0, j) for j in range(FFN_T // 2)]
    s += [("ffn_add", 0)]
    s += [("sum_sq", 5), ("apply", 5)]
    s += [("rnn_in", i) for i in range(RNN_T)]
    for g, tiles in enumerate(RNN_GROUPS):
        s += [("rnn_gate", i) for i in tiles] + [("rnn_decay", g), ("rnn_scan", g)]
    s += [("rnn_out", j) for j in range((RNN_T + 1) // 2)] + [("rnn_add",)]
    s += [("sum_sq", 6), ("apply", 6)]
    s += [("ffn_in", 1, i) for i in range(FFN_T)] + [("ffn_out", 1, j) for j in range(FFN_T // 2)]
    s += [("ffn_add", 1)]
    return s


def gate_tiles():
    return [(n, w, k) for n in range(RNN_T) for w in range(2) for k in range(max(0, n - 1), min(RNN_T, n + 2))]


SPLIT_STEPS = {"nkv", "nqk", "nv", "nsa_out", "ffn_in", "ffn_out", "rnn_in", "rnn_out"}


def with_splits(steps):
    uses = [x for x in steps if x[0] in SPLIT_STEPS]
    ahead = SPLITS - 1
    s, n = [], 0
    for x in steps:
        if x[0] == "sum_sq" and x[1] == 2:
            s += [("split", u) for u in uses[0:ahead]]
        if x[0] in SPLIT_STEPS:
            if n + ahead < len(uses):
                s.append(("split", uses[n + ahead]))
            n += 1
        s.append(x)
    return s, uses


STEPS, SPLIT_USES = with_splits(plan_steps())
GATE_TILES = gate_tiles()
N_GATE_CHUNKS = -(-len(GATE_TILES) // 16)


def chunk_keys():
    one = {"mod", "kr", "qr", "vr", "gr", "kvw", "qw", "kn", "vn", "qn", "gate", "branch", "mix_out", "nkv", "nv",
           "cmp", "nsa_out", "ffn_in", "ffn_out", "rnn_in", "rnn_out"}
    keys, seen = [], 0
    for x in STEPS:
        if x[0] in one or (x[0] == "nqk"):
            keys.append(x)
        if x[0] == "experts":
            keys += [("expert", e, c) for e in range(EXPERTS) for c in range(12)]
        if x[0] == "rnn_gate":
            last = max(i for i, g in enumerate(GATE_TILES) if g[0] == x[1]) // 16
            while seen <= last:
                keys.append(("gates", seen))
                seen += 1
    return keys


CHUNKS = chunk_keys()
CHUNK_NO = {k: i for i, k in enumerate(CHUNKS)}
FIRST_EXPERT = CHUNK_NO[("expert", 0, 0)]
FIRST_SECOND = FIRST_EXPERT + 12 * EXPERTS


SPLIT_NO = {u: i for i, u in enumerate(SPLIT_USES)}


def slot_of(c):
    if c < FIRST_EXPERT:
        return c % SLOTS_A
    return (c - FIRST_EXPERT) % SLOTS if c < FIRST_SECOND else (c - FIRST_SECOND) % SLOTS_B


def landed_count(c):
    if c < FIRST_EXPERT:
        return c // SLOTS_A + 1
    s = slot_of(c)
    before = len(range(s, FIRST_EXPERT, SLOTS_A)) if s < SLOTS_A else 0
    if c < FIRST_SECOND:
        return before + (c - FIRST_EXPERT) // SLOTS + 1
    return before + EXPERTS + (c - FIRST_SECOND) // SLOTS_B + 1


class Job:
    pass


def plan_jobs():
    jobs, last, emptied = {}, {}, {"act": 0, "dve": 0}
    turn = [0]

    def add(name, engine, bank=None, counted=True):
        j = Job()
        j.counted = counted
        if bank is None:
            bank = turn[0] % 7
            turn[0] += 1
        j.bank, j.engine = bank, engine
        emptied[engine] += 1
        j.emptied = emptied[engine]
        j.before = last.get(bank)
        last[bank] = j
        jobs[name] = j

    ffn_turn = [0]
    for x in STEPS:
        k = x[0]
        if k == "mod_row":
            add(x, "act", 7, counted=False)
        if k == "mod_out":
            add(x, "dve")
        if k == "sum_sq":
            add(x, "dve")
        elif k in ("kr", "kn"):
            for i in range(2):
                add(x + (i,), "act" if k == "kr" else "dve")
        elif k in ("qr", "gr", "qw", "qn", "gate"):
            add(x, "act")
        elif k in ("vr", "vn"):
            for i in range(2):
                add(x + (i,), "dve")
        elif k == "kvw":
            add(("kvw", "k"), "act")
            add(("kvw", "v"), "dve")
        elif k in ("rot", "ret_s", "ret_mean", "ret_var", "mix_out", "combine", "nqk", "nnorm", "nv", "cmp_k",
                   "cmp_v", "nsa_out", "affinity"):
            add(x, "dve")
        elif k in ("ret_o", "att_s", "att_t", "router", "nkv", "ngate", "nsa_s", "nsa_t"):
            add(x, "act")
        elif k in ("att_o", "nsa_o"):
            add(x, "dve")
        elif k == "branch":
            for i in range(2):
                add(x + (i,), "dve")
        elif k == "tok_major":
            add(x, "act" if x[2] == 0 else "dve")
        elif k == "gather":
            add(x, "act" if x[1] % 2 else "dve")
        elif k == "pick":
            add(("pick", "idx"), "dve")
            add(("pick", "gate"), "act")
        elif k == "pick_t":
            add(x, "act")
        elif k == "cmp_s":
            for half in range(2):
                add(("cmp_s", half), "dve")
        elif k == "cmp":
            if x[2] == 1:
                add(("cmp", x[1]), "act")
        elif k == "experts":
            jobs["experts"] = {b: last.get(b) for b in range(3)}
            for b in range(3):
                last[b] = None
        elif k in ("ffn_in", "rnn_in"):
            add(x, "dve" if k == "ffn_in" else "act", ffn_turn[0] % 4)
            ffn_turn[0] += 1
        elif k == "rnn_gate":
            add(x, "act", ffn_turn[0] % 4)
            ffn_turn[0] += 1
        elif k in ("ffn_add", "rnn_add"):
            for p in range(4):
                add(x + (p,), "dve", 4 + p)
    return jobs


def build(nc, w, small, out):
    JOBS = {}
    n = 0
    for name, j in plan_jobs().items():
        JOBS[name] = j
        if isinstance(j, Job) and j.counted:
            n += 1
            j.no = n

    ctx = ExitStack()
    with ctx:
        def sb(name, shape, dt=F32):
            return ctx.enter_context(nc.sbuf_tensor(name, shape, dt))

        def sem(name):
            return ctx.enter_context(nc.semaphore(name))

        twins = {}

        def sb_twin(name, shape):
            at = -(-nc.sbuf_base // 32) * 32
            t = sb(name, shape)
            twins[t.name] = nc.alloc_sbuf_tensor_at(name + "_r", shape, F32R, offset=at)
            return t

        def r(ap):
            return bass.AP(twins[ap.tensor.name], ap.offset, ap.ap)

        ring = sb_twin("ring", [P, SLOTS, CHUNK])
        H = sb_twin("H", [P, KT, 2 * T])
        arena = sb_twin("arena", [P, 16896])
        X = sb("X", [P, KT, T])
        SQ = H[:, :, T:2 * T]
        H_HI, H_LO = H[:, :, T:2 * T], H[:, :, 0:T]
        cols = sb("cols", [P, N_COLS])
        consts = sb("consts", [P, N_CONSTS])
        wide = sb("wide", [P, KT, 64])
        silu_c = sb("silu_c", [P, 48])
        mod = sb("mod", [P, 48, 2])
        mod2 = sb("mod2", [P, 96])
        mod_a = sb("mod_a", [P, 7, 8])
        norm_t = sb("norm_t", [P, 2, 2 * T])
        sp = sb("sp", [P, 8, 19])
        stat = sb("stat", [P, 64])

        def col(name, i=0, width=1):
            return cols[:, COLS[name][0] + i:COLS[name][0] + i + width]

        def const(name, rows=P):
            return consts[0:rows, CONSTS[name][0]:CONSTS[name][0] + CONSTS[name][1]]

        def room(at, *shape, rows=P):
            size = 1
            for k in shape:
                size *= k
            v = arena[0:rows, at:at + size]
            if len(shape) == 2:
                v = v.rearrange("p (a b) -> p a b", a=shape[0])
            if len(shape) == 3:
                v = v.rearrange("p (a b c) -> p a b c", a=shape[0], b=shape[1])
            return v

        ident, ones, half_ones = const("ident"), const("ones"), const("half_ones")
        q_r, k_r, v_r, g_r = room(0, 4, T), room(1024, 4, 2 * T), room(3072, 4, 512), room(5120, 4, T)
        q_w, k_w, v_w = room(6144, 4, T), room(7168, 512), room(7680, 4, 128)
        q_n, k_n, v_n = room(8192, 4, T), room(9216, 4, 512), room(11264, 4, 512)
        probs_t = [room(14848 + 1024 * i, 4, T) for i in range(2)]
        decay_in = room(13312, N_DECAY)
        rope_a, rope_b = room(15872, 2, T), room(16384, 2, T)
        y_r, y_w, y_n = q_r, q_w, q_n
        merged = room(1024, KT, T)
        ctx_in = room(1024, KT, T)
        gates = ring[:, 6:9, :].rearrange("p a b -> p (a b)").rearrange("p (a b) -> p a b", b=T)
        sq_0 = ring[:, 6:8, :].rearrange("p a b -> p (a b)").rearrange("p (a b) -> p a b", b=2 * T)
        decay_m = ring[:, 9:11, :].rearrange("p a b -> p (a b)").rearrange("p (h k q) -> p h k q", h=4, k=4)
        bias_n = ring[:, 9:11, :].rearrange("p a b -> p (a b)").rearrange("p (h k q) -> p h k q", h=8, k=2)
        ret_p = [ring[:, 11, 1024 * i:1024 * i + 1024].rearrange("p (k q) -> p k q", k=4) for i in range(2)]
        ret_sq = ret_p[0]
        probs = ring[:, 11, :].rearrange("p (a b) -> p a b", a=BUFS)
        h_tok, x_e, y_tok = room(0, 2, D), room(2048, KT, (EXPERTS + 1) * CAP), room(6400, 4, D)
        hot, hot_t = room(10496, 2, 512), room(11520, 4, T)
        gate_b = room(12544, 512)
        aff, aff_t = room(13056, 2, 16), room(13088, T, rows=16)
        top_v = room(13344, 32, rows=16)
        top_f = room(13376, 32, rows=16)
        top_i = ctx.enter_context(nc.sbuf_tensor("top_i", [16, 32], U32))
        spread_i, spread_g = room(13408, 16, 32, rows=16), room(13920, 16, 32, rows=16)
        hot_g = room(13408, 2, 512)
        x_cur, silu_g, hid, hid_t = room(14432, KT, CAP), room(14688, 512), room(15200, 512), room(15712, 4, 2 * CAP)
        qk = room(0, 3104)
        n_sq, n_rs = room(3104, 2, 512), room(4128, 2, 512)
        win_f = [room(5152 + 1024 * i, 4, T) for i in range(2)]
        flat = [room(7200 + 960 * i, 16, 4, 15) for i in range(2)]
        o_n, o_lo = room(5152, KT, T), room(7200, KT, T)
        hid_c = room(9120, 2, 2, 60)
        v_c = room(9360, 4, 64, rows=15)
        v_s = [room(9616 + 512 * i, 2, T) for i in range(2)]
        n_p = room(3104, BUFS, 512)
        n_pt = [room(12176 + 1024 * i, 2, 2, T) for i in range(2)]
        cmp_p = room(14224, 2, 16, 15)
        cmp_pt = [room(14704 + 256 * i, T, rows=15) for i in range(2)]
        n_gate = room(15216, 2, 48)
        wide_hi, wide_lo = room(15600, KT, 48), room(15984, KT, 48)
        cmp_m = room(15312, 2, 16)
        w2c = room(15344, 4, 64).rearrange("p (a b) n -> p a b n", a=2)
        ffn_h, ffn_lo = room(0, FFN_T, T), room(5632, FFN_T, T)
        ffn_g, ffn_p = room(11264, 2, T), room(11776, 2, T)
        gelu_g, u_in, u_c = room(0, RNN_T, T), room(2816, RNN_T, T + 3), room(5665, RNN_T, T)
        rec, inp = room(8481, RNN_T, T), room(11297, RNN_T, T)
        thr, rnn_d = room(2816, RNN_T, T), room(14113, 2, T)

        bank = [ctx.enter_context(nc.psum_tensor(f"bank{i}", [P, 512], F32)) for i in range(8)]
        mods = bank[7]

        def mod_rows(b):
            return gates[:, 20:22, :].rearrange("p a b -> p (a b)") if b == 0 else norm_t[:, b % 2, :]

        landed = [sem(f"landed{i}") for i in range(SLOTS)]
        chunk_used = sem("chunk_used")
        job_done = sem("job_done")
        emptied = {"act": sem("act_emptied"), "dve": sem("dve_emptied")}
        x_landed, ctx_landed, cols_landed = sem("x_landed"), sem("ctx_landed"), sem("cols_landed")
        consts_landed, decay_landed, wide_landed = sem("consts_landed"), sem("decay_landed"), sem("wide_landed")
        hi_ready, lo_ready, h_split, wide_split = sem("hi_ready"), sem("lo_ready"), sem("h_split"), sem("wide_split")
        bias_landed, bias_ready, w2_landed = sem("bias_landed"), sem("bias_ready"), sem("w2_landed")
        dve_step, act_step = sem("dve_step"), sem("act_step")
        silu_ready, mod_done, sq_x, sq_ctx = sem("silu_ready"), sem("mod_done"), sem("sq_x"), sem("sq_ctx")
        sq_ready, std_ready, h_scaled, h_ready = sem("sq_ready"), sem("std_ready"), sem("h_scaled"), sem("h_ready")
        x_final = sem("x_final")
        sp_arg, sp_exp, sp_ready = sem("sp_arg"), sem("sp_exp"), sem("sp_ready")
        decay_arg, decay_exp, decay_ready = sem("decay_arg"), sem("decay_exp"), sem("decay_ready")
        roped = sem("roped")
        ret_sq_ready, ret_std, ret_ready = sem("ret_sq_ready"), sem("ret_std"), sem("ret_ready")
        max_ready, sink_ready, probs_ready = sem("max_ready"), sem("sink_ready"), sem("probs_ready")
        merged_ready = sem("merged_ready")
        aff_max, aff_ready, spread_ready = sem("aff_max"), sem("aff_ready"), sem("spread_ready")
        x_cur_ready, gate_up_done, silu_g_ready = sem("x_cur_ready"), sem("gate_up_done"), sem("silu_g_ready")
        hid_ready, hid_turned, hid_t_ready = sem("hid_ready"), sem("hid_turned"), sem("hid_t_ready")
        down_done, ye_taken, hot_g_ready = sem("down_done"), sem("ye_taken"), sem("hot_g_ready")
        flat_ready, n_sq_ready, n_std, n_normed = sem("flat_ready"), sem("n_sq_ready"), sem("n_std"), sem("n_normed")
        cmp_arg, cmp_exp, cmp_ready = sem("cmp_arg"), sem("cmp_exp"), sem("cmp_ready")
        n_max, n_ready = sem("n_max"), sem("n_ready")
        ffn_silu, conv_ready, rnn_tanh, rnn_sqrt_in, rnn_sqrt, rnn_ready = (
            sem("ffn_silu"), sem("conv_ready"), sem("rnn_tanh"), sem("rnn_sqrt_in"), sem("rnn_sqrt"),
            sem("rnn_ready"))
        out_landed = sem("out_landed")

        def att_unit(u):
            return u >= 16, u // 2 % 8, u % 2

        def att_head(kind, hd):
            return (hd // 2, hd % 2)

        def nsa_head(h):
            g = h // 4
            return g // 2 * 4 + h % 4, g % 2, g // 2

        X_JOBS = {1: [("mix_out", c) for c in range(4)], 2: [("combine", p) for p in range(4)],
                  4: [("nsa_out", c) for c in range(4)], 5: [("ffn_add", 0, p) for p in range(4)],
                  6: [("rnn_add", p) for p in range(4)]}
        NORM_GAIN = {0: ("g_mix", 0), 1: ("g_ffn", 0), 3: ("norm1", 0), 4: ("norm2", 0), 5: ("norm1", 8),
                     6: ("norm2", 8)}
        SHIFT2 = {3: 0, 4: 24, 5: 48, 6: 72}
        H_COUNT = {0: 16, 1: 24, 3: 32, 4: 40, 5: 48, 6: 56}

        def split_slots(key):
            return ring[:, SLOTS_B + SPLIT_NO[key] % SPLITS, :], ring[:, slot_of(CHUNK_NO[key]), :]

        def shift_of(ni, k):
            if ni == 0:
                return mod[:, k, 0:1]
            if ni == 1:
                return mod[:, 24 + k, 0:1]
            return mod2[:, SHIFT2[ni] + k:SHIFT2[ni] + k + 1]

        block = ctx.enter_context(nc.Block())

        @block.sync
        def _(sp_eng):
            eng = sp_eng
            rounds_a = FIRST_EXPERT // SLOTS_A
            first = w[0:rounds_a * SLOTS_A].rearrange("(r s) p f -> r s p f", s=SLOTS_A)
            for s in range(SLOTS_A):
                eng.dma_start(ring[:, s, :], first[0, s]).then_inc(landed[s], 16)
            with eng.Fori(1, rounds_a) as r:
                for s in range(SLOTS_A):
                    eng.wait_ge(chunk_used, r * SLOTS_A + (s + 1 - SLOTS_A))
                    eng.dma_start(ring[:, s, :], first[r, s]).then_inc(landed[s], 16)
            for c in range(rounds_a * SLOTS_A, FIRST_EXPERT):
                eng.wait_ge(chunk_used, c - SLOTS_A + 1)
                eng.dma_start(ring[:, slot_of(c), :], w[c]).then_inc(landed[slot_of(c)], 16)
            experts = w[FIRST_EXPERT:FIRST_SECOND].rearrange("(e s) p f -> e s p f", s=SLOTS)
            for s in range(SLOTS):
                if s < SLOTS_A:
                    eng.wait_ge(chunk_used, max(c for c in range(FIRST_EXPERT) if c % SLOTS_A == s) + 1)
                elif s == SLOTS_A:
                    eng.wait_ge(merged_ready, 4)
                eng.dma_start(ring[:, s, :], experts[0, s]).then_inc(landed[s], 16)
            with eng.Fori(1, EXPERTS) as e:
                for s in range(SLOTS):
                    eng.wait_ge(chunk_used, e * SLOTS + (FIRST_EXPERT + s + 1 - SLOTS))
                    eng.dma_start(ring[:, s, :], experts[e, s]).then_inc(landed[s], 16)
            rest = len(CHUNKS) - FIRST_SECOND
            rounds_b = rest // SLOTS_B
            second = w[FIRST_SECOND:FIRST_SECOND + rounds_b * SLOTS_B].rearrange("(r s) p f -> r s p f", s=SLOTS_B)
            for s in range(SLOTS_B):
                eng.wait_ge(chunk_used, FIRST_SECOND - SLOTS + s + 1)
                eng.dma_start(ring[:, s, :], second[0, s]).then_inc(landed[s], 16)
            with eng.Fori(1, rounds_b) as r:
                for s in range(SLOTS_B):
                    eng.wait_ge(chunk_used, r * SLOTS_B + (FIRST_SECOND + s + 1 - SLOTS_B))
                    eng.dma_start(ring[:, s, :], second[r, s]).then_inc(landed[s], 16)
            for c in range(FIRST_SECOND + rounds_b * SLOTS_B, len(CHUNKS)):
                eng.wait_ge(chunk_used, c - SLOTS_B + 1)
                eng.dma_start(ring[:, slot_of(c), :], w[c]).then_inc(landed[slot_of(c)], 16)
            for p in range(4):
                eng.wait_ge(emptied["dve"], JOBS[("ffn_add", 1, p)].emptied)
                eng.dma_start(out[:, 2 * p:2 * p + 2, :], X[:, 2 * p:2 * p + 2, :]).then_inc(out_landed, 16)
            eng.wait_ge(out_landed, 64)

        @block.gpsimd
        def _(eng):
            nc.gpsimd.memset(silu_c[:, 24:48], 0.0).then_inc(silu_ready, 1)
            eng.dma_start(cols[:, :], small["cols"]).then_inc(cols_landed, 16)
            eng.dma_start(consts[:, :], small["consts"]).then_inc(consts_landed, 16)
            eng.dma_start(decay_in, small["decay"]).then_inc(decay_landed, 16)
            eng.dma_start(wide[:, :, :], small["wide"]).then_inc(wide_landed, 16)
            eng.wait_ge(emptied["dve"], JOBS[("ret_s", 3, 1)].emptied)
            eng.dma_start(bias_n.rearrange("p h k q -> p (h k q)"), small["bias"]).then_inc(bias_landed, 16)
            eng.wait_ge(bias_landed, 16)
            eng.wait_ge(consts_landed, 16)
            mask = const("na_mask").unsqueeze(1).to_broadcast([P, 16, T])
            flat_bias = bias_n.rearrange("p h k q -> p (h k) q")
            nc.gpsimd.tensor_tensor(flat_bias, flat_bias, mask, ALU.add).then_inc(bias_ready, 1)
            eng.wait_ge(emptied["dve"], JOBS[("combine", 3)].emptied)
            eng.dma_start(w2c, small["w2c"]).then_inc(w2_landed, 16)

        @block.tensor
        def _(pe):
            owed = [0]

            def mm(o, lhsT, rhs, start, stop, ends=None, grouped=False):
                i = nc.tensor.matmul(o, lhsT, rhs, start=start, stop=stop, skip_group_check=grouped)
                return settle(i, ends)

            def tr(o, in_, ends=None, rows=P):
                i = nc.tensor.transpose(o, in_, ident[0:rows, 0:rows])
                return settle(i, ends)

            def settle(i, ends):
                if ends is not None:
                    i.then_inc(ends, 1)
                elif owed[0]:
                    i.then_inc(chunk_used, owed[0])
                    owed[0] = 0
                return i

            def chunk(key):
                c = CHUNK_NO[key]
                pe.wait_ge(landed[slot_of(c)], 16 * landed_count(c))
                return ring[:, slot_of(c), :].rearrange("p (k n) -> p k n", k=8)

            def begin(name):
                j = JOBS[name]
                if j.before is not None:
                    pe.wait_ge(emptied[j.before.engine], j.before.emptied)
                return bank[j.bank]

            def in_sbuf(name):
                pe.wait_ge(emptied[JOBS[name].engine], JOBS[name].emptied)

            def h_is(ni, k=KT - 1):
                if ni >= 3:
                    pe.wait_ge(h_split, 8 * (ni - 3) + k + 1)
                else:
                    pe.wait_ge(h_ready, H_COUNT[ni])

            def split_chunk(key, n):
                pe.wait_ge(lo_ready, SPLIT_NO[key] + 1)
                return [x.rearrange("p (k n) -> p k n", k=n) for x in split_slots(key)]

            def mm3(o, a, b, start, stop, ends=None, grouped=False):
                a, b = [r(x) for x in a], [r(x) for x in b]
                mm(o, a[0], b[0], start, False, grouped=grouped)
                mm(o, a[0], b[1], False, False, grouped=grouped)
                return mm(o, a[1], b[0], False, stop, ends, grouped)

            def tiles3(x, act, ni=None):
                hi, lo = split_chunk(x, 8)
                b = begin(x)
                for j in range(2):
                    for k in range(KT):
                        if j == 0 and ni is not None:
                            h_is(ni, k)
                        n = slice(j * P, (j + 1) * P)
                        mm3(b[:, j * T:(j + 1) * T], (hi[:, k, n], lo[:, k, n]), act(k), k == 0, k == KT - 1,
                            job_done if j == 1 and k == KT - 1 else None)
                owed[0] += 1

            def h3(k):
                return H_HI[:, k, :], H_LO[:, k, :]

            def tiles(x, n, act, name=None):
                ck = chunk(x)
                b = begin(name or x)
                for j in range(2):
                    for k in range(KT):
                        mm(b[:, j * n:(j + 1) * n], ck[:, k, j * P:(j + 1) * P], act(k), k == 0, k == KT - 1,
                           job_done if j == 1 and k == KT - 1 else None)
                owed[0] += 1

            def hx(k):
                return H[:, k, 0:T]

            def hxc(k):
                return H[:, k, :]

            def key_tiles(x):
                ck = chunk(x)
                for j in range(2):
                    b = begin(x + (j,))
                    for k in range(KT):
                        mm(b[:, :], ck[:, k, j * P:(j + 1) * P], hxc(k), k == 0, k == KT - 1,
                           job_done if k == KT - 1 else None)
                owed[0] += 1

            def value_tiles(x, names, tokens):
                ck = chunk(x)
                for i, name in enumerate(names):
                    b = begin(name)
                    for j in range(2):
                        t = 2 * i + j
                        for k in range(KT):
                            mm(b[:, j * T:(j + 1) * T], H[:, k, t * P:(t + 1) * P], ck[:, k, :], k == 0, k == KT - 1,
                               job_done if j == 1 and k == KT - 1 else None)
                owed[0] += 1

            def step_sum_sq(ni):
                if ni == 0:
                    pe.wait_ge(consts_landed, 16)
                    pe.wait_ge(sq_x, 1)
                    pe.wait_ge(sq_ctx, 1)
                b = begin(("sum_sq", ni))
                for k in range(KT):
                    if ni and k % 2 == 0:
                        pe.wait_ge(sq_ready, 4 * (ni - 1) + k // 2 + 1)
                    if ni == 0:
                        mm(b[:, :], ones, sq_0[:, k, :], k == 0, k == KT - 1, job_done if k == KT - 1 else None)
                    else:
                        mm(b[:, 0:T], ones, SQ[:, k, :], k == 0, k == KT - 1, job_done if k == KT - 1 else None)

            def step_mod(blk, k):
                ck = ring[:, slot_of(CHUNK_NO[("mod", blk, k)]), :]
                chunk(("mod", blk, k))
                if blk == 0 and k == 0:
                    pe.wait_ge(silu_ready, 2)
                if k == 0:
                    begin(("mod_row", blk))
                if blk < 3:
                    v = silu_c[:, 2 * k:2 * k + 32]
                else:
                    v = silu_c[:, 16 + k:17 + k].to_broadcast([P, 32])
                for j in range(4):
                    mm(mods[32 * j:32 * j + 32, :], v, ck[:, 512 * j:512 * j + 512], k == 0, k == KT - 1,
                       mod_done if j == 3 and k == KT - 1 else None)
                owed[0] += 1

            def step_mod_out(blk):
                in_sbuf(("mod_row", blk))
                b = begin(("mod_out", blk))
                for i in range(4):
                    tr(b[:, i * P:(i + 1) * P], mod_rows(blk)[:, i * P:(i + 1) * P], job_done if i == 3 else None)

            def step_kr(c):
                if c == 0:
                    h_is(0)
                key_tiles(("kr", c))

            def step_rot(what, p):
                if what == "kr":
                    in_sbuf(("kr", p, 1))
                    m, v, n = const("rot128"), k_r[:, 2 * p:2 * p + 2, 0:T], 512
                elif what == "qr":
                    in_sbuf(("qr", p))
                    m, v, n = const("rot128"), q_r[:, 2 * p:2 * p + 2, :], 512
                elif what == "kw":
                    in_sbuf(("kvw", "k"))
                    m, v, n = const("rot64"), k_w[:, 0:T], 256
                else:
                    in_sbuf(("qw", p))
                    m, v, n = const("rot64"), q_w[:, 2 * p:2 * p + 2, :], 512
                mm(begin(("rot", what, p))[:, 0:n], m, v, True, True, job_done)

            def step_vr(c):
                value_tiles(("vr", c), [("vr", c, 0), ("vr", c, 1)], 4)

            def step_vn(c):
                value_tiles(("vn", c), [("vn", c, 0), ("vn", c, 1)], 4)

            def step_kvw():
                ck = chunk(("kvw",))
                b = begin(("kvw", "k"))
                for k in range(KT):
                    mm(b[:, :], ck[:, k, 0:P], hxc(k), k == 0, k == KT - 1, job_done if k == KT - 1 else None)
                b = begin(("kvw", "v"))
                for t in range(4):
                    for k in range(KT):
                        mm(b[:, t * P:(t + 1) * P], H[:, k, t * P:(t + 1) * P], ck[:, k, P:2 * P], k == 0,
                           k == KT - 1, job_done if t == 3 and k == KT - 1 else None)
                owed[0] += 1

            def step_ret_s(h, kp):
                if h == 0 and kp == 0:
                    pe.wait_ge(roped, 4)
                b = begin(("ret_s", h, kp))
                for j in range(2):
                    mm(b[:, j * T:(j + 1) * T], k_r[:, h, (2 * kp + j) * P:(2 * kp + j + 1) * P], q_r[:, h, :], True,
                       True, job_done if j else None)

            def step_ret_o(h):
                in_sbuf(("ret_s", h, 1))
                b = begin(("ret_o", h))
                for kt in range(4):
                    mm(b[:, 0:T], v_r[:, kt, h * P:(h + 1) * P], ret_p[h % 2][:, kt, :], kt == 0, kt == 3,
                       job_done if kt == 3 else None)

            def step_ret_mean(p):
                in_sbuf(("ret_o", 2 * p + 1))
                mm(begin(("ret_mean", p))[:, :], ones, y_r[:, 2 * p:2 * p + 2, :], True, True, job_done)

            def step_ret_var(p):
                pe.wait_ge(ret_sq_ready, p + 1)
                mm(begin(("ret_var", p))[:, :], ones, ret_sq[:, 2 * p:2 * p + 2, :], True, True, job_done)

            def step_att_s(u):
                na, hd, qt = att_unit(u)
                if u == 0:
                    pe.wait_ge(roped, 7)
                if u == 16:
                    in_sbuf(("qn", 1))
                    in_sbuf(("kn", 1, 1))
                t, half = att_head(na, hd)
                rows = slice(64 * half, 64 * half + 64)
                q = (q_n if na else q_w)[rows, t, qt * P:(qt + 1) * P]
                keys = k_n[rows, t, :] if na else k_w[rows, :]
                mm(begin(("att_s", u))[:, :], q, keys, True, True, job_done)

            def step_att_t(u):
                pe.wait_ge(probs_ready, u + 1)
                b = begin(("att_t", u))
                for kt in range(4):
                    tr(b[:, kt * P:(kt + 1) * P], probs[:, u % BUFS, kt * P:(kt + 1) * P], job_done if kt == 3 else None)

            def step_att_o(i):
                na, hd, _ = att_unit(2 * i)
                in_sbuf(("att_t", 2 * i + 1))
                if i == 0:
                    in_sbuf(("kvw", "v"))
                if i == 8:
                    in_sbuf(("vn", 1, 1))
                t, half = att_head(na, hd)
                b = begin(("att_o", i))
                for kt in range(4):
                    v = v_n[:, kt, hd * 64:hd * 64 + 64] if na else v_w[:, kt, half * 64:half * 64 + 64]
                    mm(b[64 * half:64 * half + 64, 0:T], v, probs_t[i % 2][:, kt, :], kt == 0, kt == 3,
                       job_done if kt == 3 else None)

            def step_branch(ch, br):
                ck = chunk(("branch", ch, br)).rearrange("p k n -> p (k n)").rearrange("p (k n) -> p k n", k=4)
                y = (y_r, y_w, y_n)[br]
                if br == 0:
                    pe.wait_ge(ret_ready, 2)
                else:
                    in_sbuf(("att_o", 7 if br == 1 else 15))
                for p in range(2):
                    b = begin(("branch", ch, br, p))
                    for j in range(2):
                        for k in range(4):
                            mm(b[:, j * T:(j + 1) * T], ck[:, k, (2 * p + j) * P:(2 * p + j + 1) * P], y[:, k, :],
                               k == 0, k == 3, job_done if j == 1 and k == 3 else None)
                owed[0] += 1

            def step_mix_out(c):
                pe.wait_ge(merged_ready, 4)
                tiles(("mix_out", c), T, lambda k: merged[:, k, :])

            def step_tok_major(t, kq):
                h_is(1)
                b = begin(("tok_major", t, kq))
                for j in range(4):
                    tr(b[:, j * P:(j + 1) * P], H[:, 4 * kq + j, t * P:(t + 1) * P], job_done if j == 3 else None)

            def step_router():
                pe.wait_ge(wide_landed, 16)
                b = begin(("router",))
                for t in range(2):
                    for k in range(KT):
                        mm(b[:, t * 16:t * 16 + 16], H[:, k, t * P:(t + 1) * P], wide[:, k, 0:16], k == 0, k == KT - 1,
                           job_done if t == 1 and k == KT - 1 else None)

            def step_affinity():
                pe.wait_ge(aff_ready, 1)
                b = begin(("affinity",))
                for t in range(2):
                    tr(b[0:16, t * P:(t + 1) * P], aff[:, t, :], job_done if t else None)

            def step_pick():
                pe.wait_ge(spread_ready, 1)
                mm(begin(("pick", "idx"))[:, :], ones[0:16, :], spread_i, True, True, job_done)
                mm(begin(("pick", "gate"))[:, :], ones[0:16, :], spread_g, True, True, job_done)

            def step_gather(k):
                if k == 0:
                    for t in range(2):
                        for kq in range(2):
                            in_sbuf(("tok_major", t, kq))
                    in_sbuf(("pick", "idx"))
                b = begin(("gather", k))
                for t in range(2):
                    mm(b[:, :], h_tok[:, t, k * P:(k + 1) * P], hot[:, t, :], t == 0, t == 1, job_done if t else None)

            def step_pick_t(t):
                pe.wait_ge(hot_g_ready, 1)
                b = begin(("pick_t", t))
                for j in range(4):
                    tr(b[:, j * P:(j + 1) * P], hot_g[:, t, j * P:(j + 1) * P], job_done if j == 3 else None)

            def step_experts():
                for b in range(3):
                    j = JOBS["experts"][b]
                    pe.wait_ge(emptied[j.engine], j.emptied)
                if owed[0]:
                    pe.sem_inc(chunk_used, owed[0])
                    owed[0] = 0
                before = [landed_count(FIRST_EXPERT + s) - 1 for s in range(SLOTS)]
                mm = nc.tensor.matmul
                with pe.Fori(0, EXPERTS // 4) as i:
                    for u in range(4):
                        pe.wait_ge(x_cur_ready, i * 4 + (u + 1))
                        for k in range(KT):
                            pe.wait_ge(landed[k], i * 64 + 16 * (before[k] + u + 1))
                            for j in range(4):
                                last = mm(bank[0][32 * j:32 * j + 32, :], x_cur[:, k, :],
                                          ring[:, k, 512 * j:512 * j + 512], start=k == 0, stop=k == KT - 1)
                            last.then_inc(chunk_used if k < KT - 1 else gate_up_done, 1)
                        pe.wait_ge(hid_ready, i * 4 + (u + 1))
                        pe.sem_inc(chunk_used, 1)
                        for c in range(4):
                            last = nc.tensor.transpose(bank[1][:, c * 64:c * 64 + 64], hid[64:P, c * P:(c + 1) * P],
                                                       ident[64:P, 64:P])
                        last.then_inc(hid_turned, 1)
                        pe.wait_ge(hid_t_ready, i * 4 + (u + 1))
                        pe.wait_ge(ye_taken, i * 4 + (u + 1))
                        for c in range(4):
                            s = KT + c
                            pe.wait_ge(landed[s], i * 64 + 16 * (before[s] + u + 1))
                            ck = ring[:, s, :].rearrange("p (k n) -> p k n", k=2)
                            for kk in range(2):
                                k = 2 * c + kk
                                for j in range(4):
                                    last = mm(bank[2][32 * j:32 * j + 32, 0:T],
                                              hid_t[:, k % 4, k // 4 * CAP:k // 4 * CAP + CAP], ck[:, kk, j * T:j * T + T],
                                              start=k == 0, stop=k == KT - 1)
                                    if kk == 0 and j == 3 and c:
                                        last.then_inc(chunk_used, 1)
                        last.then_inc(down_done, 1)
                        pe.wait_ge(down_done, i * 4 + (u + 1))
                        pe.sem_inc(chunk_used, 1)
                pe.wait_ge(ye_taken, EXPERTS + 1)

            def step_combine(p):
                b = begin(("combine", p))
                if p == 0:
                    in_sbuf(("pick_t", 1))
                for i in range(2):
                    n = 2 * p + i
                    for j in range(4):
                        mm(b[:, i * T:(i + 1) * T], y_tok[:, j, n * P:(n + 1) * P], hot_t[:, j, :], j == 0, j == 3,
                           job_done if i == 1 and j == 3 else None)

            def step_nkv(kv):
                tiles3(("nkv", kv), h3, 3)

            def step_nnorm(i):
                pe.wait_ge(n_sq_ready, i + 1)
                n = 512 if i < 6 else 30
                mm(begin(("nnorm", i))[:, 0:n], half_ones, n_sq[:, i % 2, 0:n], True, True, job_done)

            def step_nv(i):
                hi, lo = split_chunk(("nv", i), 8)
                b = begin(("nv", i))
                for j in range(2):
                    t = slice(j * P, (j + 1) * P)
                    for k in range(KT):
                        mm3(b[:, j * T:(j + 1) * T], (H_HI[:, k, t], H_LO[:, k, t]), (hi[:, k, :], lo[:, k, :]), k == 0,
                            k == KT - 1, job_done if j == 1 and k == KT - 1 else None)
                owed[0] += 1

            def step_ngate():
                pe.wait_ge(wide_split, 1)
                b = begin(("ngate",))
                for t in range(2):
                    for k in range(KT):
                        mm3(b[:, t * 48:t * 48 + 48], [x[:, t * P:(t + 1) * P] for x in h3(k)],
                            (wide_hi[:, k, :], wide_lo[:, k, :]), k == 0, k == KT - 1,
                            job_done if t == 1 and k == KT - 1 else None)

            cmp_bank = [None]

            def step_cmp(kv, part):
                ck = chunk(("cmp", kv, part))
                if part == 0:
                    pe.wait_ge(flat_ready, kv + 1)
                    cmp_bank[0] = begin(("cmp", kv))
                for ht in range(2):
                    for j in range(8):
                        f = flat[kv][:, 8 * part + j, :, :]
                        mm(cmp_bank[0][:, ht * 60:ht * 60 + 60], ck[:, j, ht * P:(ht + 1) * P], f,
                           part == 0 and ht == 0 and j == 0, part == 1 and j == 7,
                           job_done if part == 1 and ht == 1 and j == 7 else None, grouped=True)
                owed[0] += 1

            def step_cmp_k():
                pe.wait_ge(w2_landed, 16)
                in_sbuf(("cmp", 0))
                b = begin(("cmp_k",))
                for par in range(2):
                    for ht in range(2):
                        v = hid_c[:, 0, ht, :].rearrange("p (g c) -> p g c", g=4)[:, par::2, :]
                        mm(b[64 * par:64 * par + 64, 0:30], w2c[:, 0, ht, :], v, ht == 0, ht == 1,
                           job_done if par and ht else None)

            def step_cmp_v():
                in_sbuf(("cmp", 1))
                b = begin(("cmp_v",))
                for g in range(4):
                    for ht in range(2):
                        mm(b[0:N_CMP, g * 64:g * 64 + 64], hid_c[:, 1, ht, g * N_CMP:(g + 1) * N_CMP], w2c[:, 1, ht, :],
                           ht == 0, ht == 1, job_done if g == 3 and ht else None)

            def step_cmp_s():
                pe.wait_ge(n_normed, 7)
                for half in range(2):
                    b = begin(("cmp_s", half))
                    rows = slice(64 * half, 64 * half + 64)
                    for qt in range(2):
                        for qi in range(8):
                            gp, at = qi // 4, (qt * 8 + qi) * N_CMP
                            mm(b[:, at:at + N_CMP], qk[rows, 1024 + qi * T + qt * P:1024 + qi * T + (qt + 1) * P],
                               qk[rows, 3072 + gp * N_CMP:3072 + (gp + 1) * N_CMP], True, True,
                               job_done if qt == 1 and qi == 7 else None)

            def step_nsa_s(u):
                h, qt = u // 2, u % 2
                qi, half, gp = nsa_head(h)
                rows = slice(64 * half, 64 * half + 64)
                nk = P * (qt + 1)
                b = begin(("nsa_s", u))
                for br in range(2):
                    mm(b[:, br * nk:(br + 1) * nk], qk[rows, 1024 + qi * T + qt * P:1024 + qi * T + (qt + 1) * P],
                       qk[rows, br * 512 + gp * T:br * 512 + gp * T + nk], True, True, job_done if br else None)

            def step_nsa_t(u):
                h, qt = u // 2, u % 2
                pe.wait_ge(n_ready, u + 1)
                if u == 0:
                    pe.wait_ge(cmp_ready, 1)
                nk = P * (qt + 1)
                b = begin(("nsa_t", u))
                if qt == 0:
                    for q in range(2):
                        tr(b[0:N_CMP, 256 + q * P:256 + (q + 1) * P], cmp_p[:, q, h, :])
                for kt in range(qt + 1):
                    for br in range(2):
                        at = (2 * kt + br) * P
                        tr(b[:, at:at + P], n_p[:, u % BUFS, br * nk + kt * P:br * nk + (kt + 1) * P],
                           job_done if kt == qt and br else None)

            def step_nsa_o(h):
                qi, half, gp = nsa_head(h)
                g = h // 4
                in_sbuf(("nsa_t", 2 * h + 1))
                b = begin(("nsa_o", h))[64 * half:64 * half + 64, 0:T]
                pt = n_pt[h % 2]
                mm(b, v_c[:, g, :], cmp_pt[h % 2], True, False)
                for br in range(2):
                    mm(b, v_s[br][:, 0, g * 64:g * 64 + 64], pt[:, 0, br, :], False, False)
                for br in range(2):
                    mm(b[:, P:T], v_s[br][:, 1, g * 64:g * 64 + 64], pt[:, 1, br, P:T], False, br == 1,
                       job_done if br else None)

            def step_nsa_out(c):
                if c == 0:
                    in_sbuf(("nsa_o", NSA_HEADS - 1))
                tiles3(("nsa_out", c), lambda k: (o_n[:, k, :], o_lo[:, k, :]))

            def step_ffn_in(l, i):
                tiles3(("ffn_in", l, i), h3, 4 + 2 * l)

            def rows_out(key, j, n_k, act, adds):
                hi, lo = split_chunk(key, 2)
                if j == 0:
                    for p in range(4):
                        begin(adds[p])
                for kk in range(2):
                    k = 2 * j + kk
                    if k == n_k:
                        break
                    for n in range(KT):
                        o = bank[4 + n // 2][:, n % 2 * T:n % 2 * T + T]
                        at = slice(n * P, (n + 1) * P)
                        mm3(o, (hi[:, kk, at], lo[:, kk, at]), act(k), k == 0 and n % 2 == 0, k == n_k - 1,
                            job_done if k == n_k - 1 and n % 2 else None, grouped=True)
                owed[0] += 1

            def step_ffn_out(l, j):
                in_sbuf(("ffn_in", l, 2 * j + 1))
                rows_out(("ffn_out", l, j), j, FFN_T, lambda k: (ffn_h[:, k, :], ffn_lo[:, k, :]),
                         [("ffn_add", l, p) for p in range(4)])

            def step_rnn_in(i):
                tiles3(("rnn_in", i), h3, 5)

            seen = [-1]

            def step_rnn_gate(n):
                pe.wait_ge(conv_ready, min(n + 2, RNN_T))
                b = begin(("rnn_gate", n))
                mine = [(i, x) for i, x in enumerate(GATE_TILES) if x[0] == n]
                for i, (_, wh, k) in mine:
                    if i // 16 != seen[0]:
                        if seen[0] >= 0:
                            owed[0] += 1
                        seen[0] = i // 16
                    ck = chunk(("gates", i // 16)).rearrange("p k n -> p (k n)")
                    ks = [x[2] for _, x in mine if x[1] == wh]
                    mm(b[:, wh * T:(wh + 1) * T], ck[:, i % 16 * P:(i % 16 + 1) * P], u_c[:, k, :], k == ks[0],
                       k == ks[-1], job_done if (i, (n, wh, k)) == mine[-1] else None)
                if n == RNN_T - 1:
                    owed[0] += 1

            def step_rnn_out(j):
                pe.wait_ge(rnn_ready, min(2 * j + 2, RNN_T))
                rows_out(("rnn_out", j), j, RNN_T, lambda k: (gelu_g[:, k, :], u_c[:, k, :]),
                         [("rnn_add", p) for p in range(4)])

            def whole(name):
                return lambda *a: tiles((name,) + a, T, hx)

            parts = {"sum_sq": step_sum_sq, "mod": step_mod, "mod_out": step_mod_out, "kr": step_kr, "rot": step_rot, "qr": whole("qr"),
                     "vr": step_vr, "gr": whole("gr"), "kvw": step_kvw, "qw": whole("qw"),
                     "kn": lambda c: key_tiles(("kn", c)), "vn": step_vn, "qn": whole("qn"), "gate": whole("gate"),
                     "ret_s": step_ret_s, "ret_o": step_ret_o, "ret_mean": step_ret_mean, "ret_var": step_ret_var,
                     "att_s": step_att_s, "att_t": step_att_t, "att_o": step_att_o, "branch": step_branch,
                     "mix_out": step_mix_out, "tok_major": step_tok_major, "router": step_router,
                     "affinity": step_affinity, "pick": step_pick, "gather": step_gather, "pick_t": step_pick_t,
                     "experts": step_experts, "combine": step_combine, "nkv": step_nkv,
                     "nqk": lambda i: tiles3(("nqk", i), h3), "nnorm": step_nnorm, "nv": step_nv, "ngate": step_ngate, "cmp": step_cmp,
                     "cmp_k": step_cmp_k, "cmp_v": step_cmp_v, "cmp_s": step_cmp_s, "nsa_s": step_nsa_s,
                     "nsa_t": step_nsa_t, "nsa_o": step_nsa_o, "nsa_out": step_nsa_out, "ffn_in": step_ffn_in,
                     "ffn_out": step_ffn_out, "rnn_in": step_rnn_in, "rnn_gate": step_rnn_gate,
                     "rnn_out": step_rnn_out}
            for name, *args in STEPS:
                if name in parts:
                    parts[name](*args)

        @block.scalar
        def _(act):
            f = nc.scalar.activation

            def job(name):
                act.wait_ge(job_done, JOBS[name].no)
                return bank[JOBS[name].bank]

            def takes(i, name):
                assert JOBS[name].engine == "act"
                i.then_inc(emptied["act"], 1)

            def two(b, n=T):
                return b[:, 0:2 * n].rearrange("p (a b) -> p a b", a=2)

            act.dma_start(X[:, :, :], small["x"]).then_inc(x_landed, 16)
            act.dma_start(ctx_in, small["ctx"]).then_inc(ctx_landed, 16)

            def step_sum_sq(ni):
                if ni == 0:
                    act.wait_ge(cols_landed, 16)
                    f(silu_c[:, 0:24], cols[:, 0:24], ACT.Silu).then_inc(silu_ready, 1)
                    act.wait_ge(x_landed, 16)
                    f(sq_0[:, :, 0:T], X[:, :, :], ACT.Square).then_inc(sq_x, 1)
                else:
                    for p in range(4):
                        if ni in X_JOBS:
                            act.wait_ge(emptied["dve"], JOBS[X_JOBS[ni][p]].emptied)
                        else:
                            act.wait_ge(x_final, 2 * p + 2)
                        f(SQ[:, 2 * p:2 * p + 2, :], X[:, 2 * p:2 * p + 2, :], ACT.Square).then_inc(sq_ready, 1)
                n = 2 * T if ni == 0 else T
                act.wait_ge(emptied["dve"], JOBS[("sum_sq", ni)].emptied)
                f(norm_t[:, 1, 0:n], norm_t[:, 0, 0:n], ACT.Sqrt).then_inc(std_ready, 1)

            def step_apply(ni):
                if ni == 2:
                    return
                done = H_COUNT[ni] - (16 if ni == 0 else 8)
                for k in range(KT):
                    act.wait_ge(h_scaled, done + (2 * k + 1 if ni == 0 else k + 1))
                    if ni >= 3:
                        f(r(H_HI[:, k, :]), H[:, k, 0:T], ACT.Identity, bias=shift_of(ni, k)).then_inc(h_ready, 1)
                        continue
                    f(H[:, k, 0:T], H[:, k, 0:T], ACT.Identity, bias=shift_of(ni, k)).then_inc(h_ready, 1)
                    if ni == 0:
                        act.wait_ge(h_scaled, 2 * k + 2)
                        f(H[:, k, T:2 * T], H[:, k, T:2 * T], ACT.Identity, bias=mod[:, k, 1:2]).then_inc(h_ready, 1)

            def step_split(key):
                c, n = CHUNK_NO[key], SPLIT_NO[key]
                act.wait_ge(landed[slot_of(c)], 16 * landed_count(c))
                if n >= SPLITS:
                    act.wait_ge(chunk_used, CHUNK_NO[SPLIT_USES[n - SPLITS]] + 1)
                else:
                    act.wait_ge(chunk_used, FIRST_SECOND)
                hi, lo = split_slots(key)
                f(r(hi), lo, ACT.Copy).then_inc(hi_ready, 1)

            def step_decay():
                act.wait_ge(sp_arg, 1)
                f(sp[:, 1, :], sp[:, 0, :], ACT.Exp, scale=-1.0).then_inc(sp_exp, 1)
                act.wait_ge(decay_landed, 16)
                for h in range(R_HEADS):
                    act.wait_ge(decay_arg, h + 1)
                    f(decay_m[:, h, 0:2, :], decay_m[:, h, 0:2, :], ACT.Exp, scale=-1.0)
                    f(decay_m[:, h, 2:4, :], decay_in[:, 1024:1536].rearrange("p (a b) -> p a b", a=2), ACT.Exp,
                      scale=sp[:, 7, h:h + 1])
                    if h >= 2:
                        act.wait_ge(decay_ready, h - 1)
                    f(ret_p[h % 2][:, 0:2, :], decay_in[:, 1536:2048].rearrange("p (a b) -> p a b", a=2), ACT.Exp,
                      scale=sp[:, 7, 4 + h:5 + h]).then_inc(decay_exp, 1)

            def step_kr(c):
                for j in range(2):
                    takes(f(k_r[:, 2 * c + j, :], job(("kr", c, j))[:, :], ACT.Copy), ("kr", c, j))

            def evac(name, dst, func=ACT.Copy, scale=1.0):
                def run(c):
                    takes(f(dst[:, 2 * c:2 * c + 2, :], two(job((name, c))), func, scale=scale), (name, c))
                return run

            def step_kvw():
                takes(f(k_w, job(("kvw", "k"))[:, :], ACT.Copy), ("kvw", "k"))

            def step_ret_o(h):
                takes(f(y_r[:, h, :], job(("ret_o", h))[:, 0:T], ACT.Copy), ("ret_o", h))

            def step_ret_mean(p):
                act.wait_ge(emptied["dve"], JOBS[("ret_mean", p)].emptied)
                f(ret_sq[:, 2 * p:2 * p + 2, :], y_r[:, 2 * p:2 * p + 2, :], ACT.Square).then_inc(ret_sq_ready, 1)

            def step_ret_var(p):
                act.wait_ge(emptied["dve"], JOBS[("ret_var", p)].emptied)
                f(rope_b if p else rope_a, rope_b if p else rope_a, ACT.Sqrt).then_inc(ret_std, 1)

            def step_att_s(u):
                na, hd, _ = att_unit(u)
                b = job(("att_s", u))
                act.wait_ge(max_ready, u + 1)
                if u >= BUFS:
                    act.wait_ge(job_done, JOBS[("att_t", u - BUFS)].no)
                s = 8 * (u % 4)
                i = f(probs[:, u % BUFS, :], b[:, :], ACT.Exp, bias=stat[:, s:s + 1], accum_out=stat[:, s + 1:s + 2])
                takes(i, ("att_s", u))
                if not na:
                    f(stat[:, s + 2:s + 3], col("sink", hd), ACT.Exp, bias=stat[:, s:s + 1]).then_inc(sink_ready, 1)

            def step_att_t(u):
                b = job(("att_t", u))
                i, qt = u // 2, u % 2
                if i >= 2:
                    act.wait_ge(job_done, JOBS[("att_o", i - 2)].no)
                takes(f(probs_t[i % 2][:, :, qt * P:(qt + 1) * P], b[:, :].rearrange("p (a b) -> p a b", a=4),
                        ACT.Copy), ("att_t", u))

            def step_tok_major(t, kq):
                if kq == 0:
                    takes(f(h_tok[:, t, 0:512], job(("tok_major", t, kq))[:, :], ACT.Copy), ("tok_major", t, kq))

            def step_router():
                b = job(("router",))
                act.wait_ge(aff_max, 1)
                for t in range(2):
                    i = f(aff[:, t, :], b[:, t * 16:t * 16 + 16], ACT.Exp, bias=stat[:, t:t + 1],
                          accum_out=stat[:, 2 + t:3 + t])
                takes(i, ("router",))

            def step_pick():
                takes(f(gate_b, job(("pick", "gate"))[:, :], ACT.Copy), ("pick", "gate"))

            def step_gather(k):
                if k % 2:
                    takes(f(x_e[:, k, 0:EXPERTS * CAP], job(("gather", k))[:, :], ACT.Copy), ("gather", k))

            def step_pick_t(t):
                takes(f(hot_t[:, :, t * P:(t + 1) * P], job(("pick_t", t))[:, :].rearrange("p (a b) -> p a b", a=4),
                        ACT.Copy), ("pick_t", t))

            def step_mod_row(blk):
                act.wait_ge(mod_done, blk + 1)
                if blk >= 3:
                    act.wait_ge(job_done, JOBS[("mod_out", blk - 2)].no)
                takes(f(mod_rows(blk), mods[:, :], ACT.Copy), ("mod_row", blk))

            def step_experts():
                with act.Fori(0, EXPERTS) as e:
                    act.wait_ge(gate_up_done, e + 1)
                    f(silu_g[64:P, :], bank[0][0:64, :], ACT.Silu).then_inc(silu_g_ready, 1)
                    act.wait_ge(hid_turned, e + 1)
                    f(hid_t.rearrange("p c n -> p (c n)"), bank[1][:, 0:256], ACT.Copy).then_inc(hid_t_ready, 1)

            def step_nkv(kv):
                b = two(job(("nkv", kv)))
                v = win_f[kv].rearrange("p (gp par) t -> p gp par t", par=2)
                f(v[0:64, :, 0, :], b[0:64, :, :], ACT.Copy)
                f(v[0:64, :, 1, :], b[64:128, :, :], ACT.Copy)
                f(v[64:128, :, 0, 0:T - 1], b[0:64, :, 1:T], ACT.Copy)
                takes(f(v[64:128, :, 1, 0:T - 1], b[64:128, :, 1:T], ACT.Copy), ("nkv", kv))

            def square_part(i, n):
                f(n_sq[:, i % 2, 0:n], qk[:, i * 512:i * 512 + n], ACT.Square).then_inc(n_sq_ready, 1)

            def step_nqk(i):
                act.wait_ge(emptied["dve"], JOBS[("nqk", i)].emptied)
                square_part(i, 512)

            def step_nnorm(i):
                n = 512 if i < 6 else 30
                if i == 4:
                    pass
                if i == 6:
                    act.wait_ge(emptied["dve"], JOBS[("cmp_k",)].emptied)
                    square_part(6, 30)
                act.wait_ge(emptied["dve"], JOBS[("nnorm", i)].emptied)
                f(n_rs[:, i % 2, 0:n], n_rs[:, i % 2, 0:n], ACT.Sqrt).then_inc(n_std, 1)

            def step_ngate():
                takes(f(n_gate.rearrange("p t n -> p (t n)"), job(("ngate",))[:, 0:96], ACT.Sigmoid), ("ngate",))

            def step_cmp(kv, part):
                if part == 1:
                    takes(f(hid_c[:, kv, :, :], job(("cmp", kv))[:, 0:120].rearrange("p (a b) -> p a b", a=2),
                            ACT.Silu), ("cmp", kv))

            def step_cmp_s():
                act.wait_ge(cmp_arg, 1)
                v = cmp_p.rearrange("p t h c -> p (t h c)")
                f(v, v, ACT.Exp).then_inc(cmp_exp, 1)

            def step_nsa_s(u):
                qt = u % 2
                nk = P * (qt + 1)
                b = job(("nsa_s", u))
                act.wait_ge(n_max, u + 1)
                if u >= BUFS:
                    act.wait_ge(job_done, JOBS[("nsa_t", u - BUFS)].no)
                s = 8 * (u % 4)
                for br in range(2):
                    i = f(n_p[:, u % BUFS, br * nk:(br + 1) * nk], b[:, br * nk:(br + 1) * nk], ACT.Exp,
                          bias=stat[:, s + br:s + br + 1], accum_out=stat[:, s + 2 + br:s + 3 + br])
                takes(i, ("nsa_s", u))

            def step_nsa_t(u):
                h, qt = u // 2, u % 2
                b = job(("nsa_t", u))
                if h >= 2:
                    act.wait_ge(job_done, JOBS[("nsa_o", h - 2)].no)
                pt = n_pt[h % 2]
                if qt == 0:
                    f(cmp_pt[h % 2], b[0:N_CMP, 256:512], ACT.Copy)
                    i = f(pt[:, 0, :, 0:P], b[:, 0:256].rearrange("p (a b) -> p a b", a=2), ACT.Copy)
                else:
                    i = f(pt[:, :, :, P:T], b[:, :].rearrange("p (k a b) -> p k a b", k=2, a=2), ACT.Copy)
                takes(i, ("nsa_t", u))

            def step_ffn_in(l, i):
                b = job(("ffn_in", l, i))
                if i >= 2:
                    act.wait_ge(emptied["dve"], JOBS[("ffn_in", l, i - 2)].emptied)
                f(ffn_g[:, i % 2, :], b[:, 0:T], ACT.Silu).then_inc(ffn_silu, 1)

            def step_rnn_in(i):
                b = job(("rnn_in", i))
                f(gelu_g[:, i, :], b[:, 0:T], ACT.Gelu_apprx_tanh)
                takes(f(u_in[:, i, 3:T + 3], b[:, T:2 * T], ACT.Copy), ("rnn_in", i))

            own = [0]

            def step_rnn_gate(n):
                b = job(("rnn_gate", n))
                f(rec[:, n, :], b[:, 0:T], ACT.Sigmoid, bias=col("b_a", n)).then_inc(act_step, 1)
                own[0] += 1
                takes(f(inp[:, n, :], b[:, T:2 * T], ACT.Sigmoid, bias=col("b_x", n)), ("rnn_gate", n))

            def step_rnn_decay(g):
                tiles, at = RNN_GROUPS[g], own[0]
                act.wait_ge(act_step, at)
                act.wait_ge(conv_ready, tiles[-1] + 1)
                for i in tiles:
                    f(thr[:, i, :], rec[:, i, :], ACT.Tanh, scale=sp[:, 6, 8 + i:9 + i]).then_inc(act_step, 1)
                    own[0] += 1
                for n, i in enumerate(tiles):
                    act.wait_ge(act_step, at + n + 1)
                    f(rec[:, i, :], rec[:, i, :], ACT.Exp, scale=sp[:, 7, 8 + i:9 + i]).then_inc(rnn_tanh, 1)

            def step_rnn_scan(g):
                for i in RNN_GROUPS[g]:
                    act.wait_ge(rnn_sqrt_in, i + 1)
                    f(thr[:, i, :], thr[:, i, :], ACT.Sqrt).then_inc(rnn_sqrt, 1)

            parts = {"sum_sq": step_sum_sq, "apply": step_apply, "split": step_split, "decay": step_decay, "kr": step_kr,
                     "qr": evac("qr", q_r), "gr": evac("gr", g_r, ACT.Silu), "kvw": step_kvw,
                     "qw": evac("qw", q_w, scale=0.125), "qn": evac("qn", q_n, scale=0.125),
                     "gate": evac("gate", gates, ACT.Sigmoid), "ret_o": step_ret_o, "ret_mean": step_ret_mean,
                     "ret_var": step_ret_var, "att_s": step_att_s, "att_t": step_att_t, "tok_major": step_tok_major,
                     "router": step_router, "pick": step_pick, "gather": step_gather, "pick_t": step_pick_t,
                     "experts": step_experts, "mod_row": step_mod_row, "nkv": step_nkv, "nqk": step_nqk,
                     "nnorm": step_nnorm, "ngate": step_ngate, "cmp": step_cmp, "cmp_s": step_cmp_s,
                     "nsa_s": step_nsa_s, "nsa_t": step_nsa_t, "ffn_in": step_ffn_in, "rnn_in": step_rnn_in,
                     "rnn_gate": step_rnn_gate, "rnn_decay": step_rnn_decay, "rnn_scan": step_rnn_scan}
            for name, *args in STEPS:
                if name in parts:
                    parts[name](*args)

        @block.vector
        def _(dve):
            v = nc.vector
            steps = [0]

            def link(i):
                steps[0] += 1
                i.then_inc(dve_step, 1)
                dve.wait_ge(dve_step, steps[0])

            def job(name):
                dve.wait_ge(job_done, JOBS[name].no)
                return bank[JOBS[name].bank]

            def takes(i, name):
                assert JOBS[name].engine == "dve"
                i.then_inc(emptied["dve"], 1)

            def taken(name):
                dve.wait_ge(emptied[JOBS[name].engine], JOBS[name].emptied)

            def two(b, n=T):
                return b[:, 0:2 * n].rearrange("p (a b) -> p a b", a=2)

            def over(a, n):
                return a.unsqueeze(1).to_broadcast([a.shape[0], n, a.shape[1]])

            def each(a, n):
                return a.unsqueeze(2).to_broadcast([a.shape[0], a.shape[1], n])

            def step_sum_sq(ni):
                if ni == 0:
                    dve.wait_ge(ctx_landed, 16)
                    v.tensor_tensor(sq_0[:, :, T:2 * T], ctx_in, ctx_in, ALU.mult).then_inc(sq_ctx, 1)
                n = 2 * T if ni == 0 else T
                b = job(("sum_sq", ni))
                takes(v.tensor_scalar(norm_t[:, 0, 0:n], b[:, 0:n], 1.0 / D, EPS, ALU.mult, ALU.add), ("sum_sq", ni))
                if ni:
                    finish_std(ni)

            def finish_std(ni):
                n = 2 * T if ni == 0 else T
                dve.wait_ge(std_ready, ni + 1)
                link(v.reciprocal(norm_t[:, 0, 0:n], norm_t[:, 1, 0:n]))

            def step_apply(ni):
                if ni == 0:
                    finish_std(0)
                for k in range(KT):
                    if ni == 2:
                        v.scalar_tensor_tensor(X[:, k, :], X[:, k, :], col("g_final", k), norm_t[:, 0, 0:T], ALU.mult,
                                               ALU.mult).then_inc(x_final, 1)
                        continue
                    v.scalar_tensor_tensor(H[:, k, 0:T], X[:, k, :], mod_a[:, ni, k:k + 1], norm_t[:, 0, 0:T], ALU.mult,
                                           ALU.mult).then_inc(h_scaled, 1)
                    if ni == 0:
                        v.scalar_tensor_tensor(H[:, k, T:2 * T], ctx_in[:, k, :], mod_a[:, 2, k:k + 1],
                                               norm_t[:, 0, T:2 * T], ALU.mult, ALU.mult).then_inc(h_scaled, 1)
                if ni == 2:
                    dve.wait_ge(x_final, 8)
                if ni >= 3:
                    for k in range(KT):
                        dve.wait_ge(h_ready, H_COUNT[ni] - 7 + k)
                        v.scalar_tensor_tensor(r(H_LO[:, k, :]), H[:, k, 0:T], shift_of(ni, k), r(H_HI[:, k, :]), ALU.add,
                                               ALU.subtract).then_inc(h_split, 1)

            def step_split(key):
                dve.wait_ge(hi_ready, SPLIT_NO[key] + 1)
                hi, lo = split_slots(key)
                v.tensor_tensor(r(lo), lo, r(hi), ALU.subtract).then_inc(lo_ready, 1)

            def step_decay():
                dve.wait_ge(cols_landed, 16)
                a = cols[:, COLS["decays"][0]:COLS["decays"][0] + 19]
                link(v.tensor_scalar(sp[:, 2, :], a, -1.0, None, ALU.mult))
                v.tensor_tensor(sp[:, 0, :], a, sp[:, 2, :], ALU.max).then_inc(sp_arg, 1)
                dve.wait_ge(sp_exp, 1)
                link(v.tensor_scalar(sp[:, 3, :], sp[:, 1, :], 2.0, None, ALU.add))
                link(v.reciprocal(sp[:, 3, :], sp[:, 3, :]))
                link(v.tensor_tensor(sp[:, 3, :], sp[:, 3, :], sp[:, 1, :], ALU.mult))
                link(v.tensor_tensor(sp[:, 4, :], sp[:, 3, :], sp[:, 3, :], ALU.mult))
                link(v.tensor_scalar(sp[:, 5, :], sp[:, 4, :], 1.0 / 17, None, ALU.mult))
                for odd in (15, 13, 11, 9, 7, 5, 3):
                    link(v.scalar_tensor_tensor(sp[:, 5, :], sp[:, 5, :], 1.0 / odd, sp[:, 4, :], ALU.add, ALU.mult))
                link(v.scalar_tensor_tensor(sp[:, 5, :], sp[:, 5, :], 1.0, sp[:, 3, :], ALU.add, ALU.mult))
                link(v.tensor_scalar(sp[:, 2, :], sp[:, 2, :], 0.0, None, ALU.max))
                link(v.scalar_tensor_tensor(sp[:, 6, :], sp[:, 5, :], 2.0, sp[:, 2, :], ALU.mult, ALU.add))
                link(v.tensor_scalar(sp[:, 6, 8:19], sp[:, 6, 8:19], 8.0, None, ALU.mult))
                link(v.tensor_scalar(sp[:, 7, :], sp[:, 6, :], -1.0, None, ALU.mult))
                dve.wait_ge(decay_landed, 16)
                for h in range(R_HEADS):
                    d = decay_m[:, h, 0:2, :].rearrange("p a b -> p (a b)")
                    link(v.tensor_scalar(d, decay_in[:, 0:512], sp[:, 6, h:h + 1], None, ALU.mult))
                    v.scalar_tensor_tensor(d, decay_in[:, 512:1024], sp[:, 6, 4 + h:5 + h], d, ALU.mult,
                                           ALU.add).then_inc(decay_arg, 1)
                for h in range(R_HEADS):
                    dve.wait_ge(decay_exp, h + 1)
                    v.tensor_tensor(decay_m[:, h, 2:4, :], decay_m[:, h, 2:4, :], ret_p[h % 2][:, 0:2, :],
                                    ALU.add).then_inc(decay_ready, 1)

            def gain_of(ni):
                name, at = NORM_GAIN[ni]
                return col(name, at, 8)

            def step_mod_out(blk):
                b = job(("mod_out", blk))[:, :].rearrange("p (i j r) -> p j i r", i=4, j=4)
                if blk < 3:
                    dst = mod[:, 16 * blk:16 * blk + 16, :].rearrange("p (j i) m -> p j i m", j=4)
                    bias = col("b_mod", 16 * blk, 16).rearrange("p (j i) -> p j i", j=4)
                    for m in range(2):
                        o = v.tensor_tensor(dst[:, :, :, m], b[:, :, :, m], bias, ALU.add)
                else:
                    at = 16 * (blk - 3)
                    o = v.tensor_tensor(mod2[:, at:at + 16].rearrange("p (j i) -> p j i", j=4), b[:, :, :, 0],
                                        col("ada_b", at, 16).rearrange("p (j i) -> p j i", j=4), ALU.add)
                takes(o, ("mod_out", blk))
                taken(("mod_out", blk))
                if blk == 0:
                    link(v.scalar_tensor_tensor(mod_a[:, 0, :], mod[:, 8:16, 0], 1.0, gain_of(0), ALU.add, ALU.mult))
                    link(v.scalar_tensor_tensor(mod_a[:, 2, :], mod[:, 8:16, 1], 1.0, gain_of(0), ALU.add, ALU.mult))
                elif blk == 2:
                    link(v.scalar_tensor_tensor(mod_a[:, 1, :], mod[:, 32:40, 0], 1.0, gain_of(1), ALU.add, ALU.mult))
                elif blk == MOD_BLOCKS - 1:
                    for ni in (3, 4, 5, 6):
                        at = SHIFT2[ni] + 8
                        link(v.scalar_tensor_tensor(mod_a[:, ni, :], mod2[:, at:at + 8], 1.0, gain_of(ni), ALU.add,
                                                    ALU.mult))

            def rope(name, dst, n, size):
                b = job(name)
                cos, sin = const(f"cos{size}"), const(f"sin{size}")
                if n == 1:
                    c, s, ps = cos, sin, b[:, 0:T]
                    ta, tb = rope_a[:, 0, :], rope_b[:, 0, :]
                else:
                    c, s, ps = over(cos, 2), over(sin, 2), two(b)
                    ta, tb = rope_a, rope_b
                takes(v.tensor_tensor(tb, ps, s, ALU.mult), name)
                link(v.tensor_tensor(ta, dst, c, ALU.mult))
                taken(name)
                v.tensor_tensor(dst, ta, tb, ALU.add).then_inc(roped, 1)
                rope_no[0] += 1
                dve.wait_ge(roped, rope_no[0])

            rope_no = [0]

            def step_rot(what, p):
                dst, n, size = {"kr": (k_r[:, 2 * p:2 * p + 2, 0:T], 2, 128), "qr": (q_r[:, 2 * p:2 * p + 2, :], 2, 128),
                                "kw": (k_w[:, 0:T], 1, 64), "qw": (q_w[:, 2 * p:2 * p + 2, :], 2, 64)}[what]
                if what == "kr" and p == 0:
                    dve.wait_ge(consts_landed, 16)
                rope(("rot", what, p), dst, n, size)

            def values(name, dst):
                def run(c):
                    for i in range(2):
                        takes(v.tensor_copy(dst[:, 2 * i:2 * i + 2, c * T:(c + 1) * T], two(job((name, c, i)))),
                              (name, c, i))
                return run

            def step_kvw():
                takes(v.tensor_copy(v_w, job(("kvw", "v"))[:, :].rearrange("p (a b) -> p a b", a=4)), ("kvw", "v"))

            def step_kn(c):
                for j in range(2):
                    takes(v.tensor_copy(k_n[:, 2 * c + j, :], job(("kn", c, j))[:, :]), ("kn", c, j))

            def step_ret_s(h, kp):
                b = job(("ret_s", h, kp))
                if h >= 2 and kp == 0:
                    dve.wait_ge(job_done, JOBS[("ret_o", h - 2)].no)
                takes(v.scalar_tensor_tensor(ret_p[h % 2][:, 2 * kp:2 * kp + 2, :], two(b), float(P) ** -0.5,
                                             decay_m[:, h, 2 * kp:2 * kp + 2, :], ALU.mult, ALU.mult), ("ret_s", h, kp))

            def step_ret_mean(p):
                y = y_r[:, 2 * p:2 * p + 2, :]
                takes(v.scalar_tensor_tensor(y, two(job(("ret_mean", p))), -1.0 / P, y, ALU.mult, ALU.add),
                      ("ret_mean", p))

            def step_ret_var(p):
                t = rope_b if p else rope_a
                b = job(("ret_var", p))
                takes(v.tensor_scalar(t, two(b), 1.0 / P, EPS, ALU.mult, ALU.add), ("ret_var", p))
                dve.wait_ge(ret_std, p + 1)
                link(v.reciprocal(t, t))
                y = y_r[:, 2 * p:2 * p + 2, :]
                link(v.tensor_tensor(y, y, t, ALU.mult))
                for h in (2 * p, 2 * p + 1):
                    i = v.scalar_tensor_tensor(y_r[:, h, :], y_r[:, h, :], col("ret_gn", h), g_r[:, h, :], ALU.mult,
                                               ALU.mult)
                i.then_inc(ret_ready, 1)

            def step_att_s(u):
                na, hd, qt = att_unit(u)
                b = job(("att_s", u))
                if u == 16:
                    dve.wait_ge(bias_ready, 1)
                if na:
                    m = bias_n[:, hd, qt, :]
                else:
                    m = const("win_mask")[:, qt * T:(qt + 1) * T]
                link(v.tensor_tensor(b[:, 0:T], b[:, 0:T], m, ALU.add))
                s = 8 * (u % 4)
                if na:
                    v.tensor_reduce(stat[:, s:s + 1], b[:, :], AX, ALU.max, negate=True).then_inc(max_ready, 1)
                else:
                    link(v.tensor_reduce(stat[:, s + 3:s + 4], b[:, :], AX, ALU.max))
                    v.tensor_scalar(stat[:, s:s + 1], stat[:, s + 3:s + 4], col("sink", hd), -1.0, ALU.max,
                                    ALU.mult).then_inc(max_ready, 1)

            def step_att_n(u):
                na = att_unit(u)[0]
                s = 8 * (u % 4)
                taken(("att_s", u))
                if not na:
                    dve.wait_ge(sink_ready, u + 1)
                    link(v.tensor_tensor(stat[:, s + 1:s + 2], stat[:, s + 1:s + 2], stat[:, s + 2:s + 3], ALU.add))
                link(v.reciprocal(stat[:, s + 4:s + 5], stat[:, s + 1:s + 2]))
                v.tensor_scalar(probs[:, u % BUFS, :], probs[:, u % BUFS, :], stat[:, s + 4:s + 5], None,
                                ALU.mult).then_inc(probs_ready, 1)

            def step_att_o(i):
                na, hd, _ = att_unit(2 * i)
                t, half = att_head(na, hd)
                rows = slice(64 * half, 64 * half + 64)
                takes(v.tensor_copy((y_n if na else y_w)[rows, t, :], job(("att_o", i))[rows, 0:T]), ("att_o", i))

            def step_branch(ch, br):
                if ch == 0 and br == 0:
                    taken(("gate", 11))
                for p in range(2):
                    name = ("branch", ch, br, p)
                    at = 4 * ch + 2 * p
                    g = gates[:, 8 * br + at:8 * br + at + 2, :]
                    takes(v.tensor_tensor(g, g, two(job(name)), ALU.mult), name)
                if br == 2:
                    taken(name)
                    for p in range(2):
                        at = 4 * ch + 2 * p
                        m = merged[:, at:at + 2, :]
                        link(v.tensor_tensor(m, gates[:, at:at + 2, :], gates[:, 8 + at:10 + at, :], ALU.add))
                        v.tensor_tensor(m, m, gates[:, 16 + at:18 + at, :], ALU.add).then_inc(merged_ready, 1)

            def add_to_x(name, gain, at):
                b = job(name)
                for j in range(2):
                    i = v.scalar_tensor_tensor(X[:, at + j, :], b[:, j * T:(j + 1) * T], gain(at + j), X[:, at + j, :],
                                               ALU.mult, ALU.add)
                takes(i, name)
                taken(name)

            def step_mix_out(c):
                add_to_x(("mix_out", c), lambda n: mod[:, 16 + n, 0:1], 2 * c)

            def step_tok_major(t, kq):
                if kq == 1:
                    takes(v.tensor_copy(h_tok[:, t, 512:1024], job(("tok_major", t, kq))[:, :]), ("tok_major", t, kq))

            def step_router():
                b = job(("router",))
                v.tensor_reduce(stat[:, 0:2], b[:, 0:32].rearrange("p (t e) -> p t e", t=2), AX, ALU.max,
                                negate=True).then_inc(aff_max, 1)
                taken(("router",))
                link(v.reciprocal(stat[:, 4:6], stat[:, 2:4]))
                v.tensor_tensor(aff, aff, each(stat[:, 4:6], 16), ALU.mult).then_inc(aff_ready, 1)

            def step_affinity():
                takes(v.tensor_copy(aff_t, job(("affinity",))[0:16, 0:T]), ("affinity",))
                taken(("affinity",))
                for r in range(4):
                    link(v.max(top_v[:, 8 * r:8 * r + 8], aff_t))
                    link(v.max_index(top_i[:, 8 * r:8 * r + 8], top_v[:, 8 * r:8 * r + 8], aff_t))
                    if r < 3:
                        link(v.match_replace(aff_t, top_v[:, 8 * r:8 * r + 8], aff_t, -1.0))
                link(v.tensor_copy(top_f, top_i[:, :]))
                own = const("own", 16).rearrange("p (e c) -> p e c", e=16)
                link(v.tensor_tensor(spread_i, own, over(top_f, 16), ALU.mult))
                v.tensor_tensor(spread_g, own, over(top_v, 16), ALU.mult).then_inc(spread_ready, 1)

            def step_pick():
                b = job(("pick", "idx"))
                for t in range(2):
                    i = v.tensor_scalar(hot[:, t, :], b[:, :], const("token")[:, t:t + 1], None, ALU.is_equal)
                takes(i, ("pick", "idx"))

            def step_gather(k):
                if k % 2 == 0:
                    takes(v.tensor_copy(x_e[:, k, 0:EXPERTS * CAP], job(("gather", k))[:, :]), ("gather", k))

            def step_experts():
                taken(("gather", 7))
                taken(("gather", 6))
                xe = x_e.rearrange("p k (e c) -> p k e c", c=CAP)
                link(v.memset(xe[:, :, EXPERTS, :], 0.0))
                v.tensor_copy(x_cur, xe[:, :, 0, :]).then_inc(x_cur_ready, 1)
                dve.sem_inc(ye_taken, 1)
                with dve.Fori(0, EXPERTS // 4) as i:
                    for u in range(4):
                        dve.wait_ge(silu_g_ready, i * 4 + (u + 1))
                        v.tensor_tensor(hid[64:P, :], silu_g[64:P, :], bank[0][64:P, :], ALU.mult).then_inc(hid_ready, 1)
                        nxt = xe[:, :, 0:16, :].rearrange("p k (i u) c -> p k i u c", u=4)[:, :, i, u + 1, :] if u < 3 else \
                            xe[:, :, 1:17, :].rearrange("p k (i u) c -> p k i u c", u=4)[:, :, i, 3, :]
                        v.tensor_copy(x_cur, nxt).then_inc(x_cur_ready, 1)
                        dve.wait_ge(down_done, i * 4 + (u + 1))
                        for j in range(4):
                            o = v.tensor_copy(y_tok[32 * u:32 * u + 32, i, j * T:(j + 1) * T],
                                              bank[2][32 * j:32 * j + 32, 0:T])
                        o.then_inc(ye_taken, 1)

            def step_pick_t(t):
                if t == 0:
                    taken(("pick", "gate"))
                    taken(("pick", "idx"))
                    v.tensor_tensor(hot_g, hot, over(gate_b, 2), ALU.mult).then_inc(hot_g_ready, 1)

            def step_combine(p):
                add_to_x(("combine", p), lambda n: mod[:, 40 + n, 0:1], 2 * p)

            def step_nkv(kv):
                taken(("nkv", kv))
                f4 = win_f[kv]
                for half in range(2):
                    rows = slice(64 * half, 64 * half + 64)
                    for g in range(4):
                        src = f4[rows, g, 0:240].rearrange("p (c j l) -> p j c l", c=15, l=2)[:, :, :, 0]
                        pos = col("pos", 16 * kv, 16)[rows]
                        i = v.tensor_tensor(flat[kv][rows, 0:8, g, :], src, each(pos[:, 0:8], 15), ALU.add)
                        src = f4[rows, g, 16:256].rearrange("p (c j l) -> p j c l", c=15, l=2)[:, :, :, 0]
                        i = v.tensor_tensor(flat[kv][rows, 8:16, g, :], src, each(pos[:, 8:16], 15), ALU.add)
                i.then_inc(flat_ready, 1)

            def step_nqk(i):
                takes(v.tensor_copy(qk[:, i * 512:(i + 1) * 512], job(("nqk", i))[:, :]), ("nqk", i))

            def step_nnorm(i):
                n = 512 if i < 6 else 30
                b = job(("nnorm", i))
                rs = n_rs[:, i % 2, 0:n]
                takes(v.tensor_scalar(rs, b[:, 0:n], 1.0 / 64, EPS, ALU.mult, ALU.add), ("nnorm", i))
                dve.wait_ge(n_std, i + 1)
                link(v.reciprocal(rs, rs))
                gain = (col("k_gain", 1), col("k_gain", 2))[i] if i < 2 else (
                    stat[:, 40:41] if i < 6 else col("k_gain", 0))
                if i == 2:
                    link(v.tensor_scalar(stat[:, 40:41], col("q_gain"), 0.125, None, ALU.mult))
                z = qk[:, i * 512:i * 512 + n]
                v.scalar_tensor_tensor(z, z, gain, rs, ALU.mult, ALU.mult).then_inc(n_normed, 1)

            def step_ngate():
                link(v.tensor_copy(r(wide_hi), wide[:, :, 16:64]))
                v.tensor_tensor(r(wide_lo), wide[:, :, 16:64], r(wide_hi), ALU.subtract).then_inc(wide_split, 1)

            def step_nv(i):
                takes(v.tensor_copy(v_s[i], two(job(("nv", i)))), ("nv", i))

            def step_cmp_k():
                takes(v.tensor_copy(qk[:, 3072:3102], job(("cmp_k",))[:, 0:30]), ("cmp_k",))

            def step_cmp_v():
                takes(v.tensor_copy(v_c, job(("cmp_v",))[0:N_CMP, 0:256].rearrange("p (a b) -> p a b", a=4)), ("cmp_v",))

            def step_cmp_s():
                add = const("cmp_add").rearrange("p (t c) -> p t c", t=2)
                keep = const("cmp_keep").rearrange("p (t c) -> p t c", t=2)
                for half in range(2):
                    ps = job(("cmp_s", half))[:, 0:240].rearrange("p (t q c) -> p t q c", t=2, q=8)
                    for t in range(2):
                        for gp in range(2):
                            h = 4 * (2 * gp + half)
                            i = v.tensor_tensor(cmp_p[:, t, h:h + 4, :], ps[:, t, 4 * gp:4 * gp + 4, :],
                                                over(add[:, t, :], 4), ALU.add)
                    takes(i, ("cmp_s", half))
                taken(("cmp_s", 1))
                link(v.tensor_reduce(cmp_m, cmp_p, AX, ALU.max))
                for t in range(2):
                    i = v.tensor_tensor(cmp_p[:, t, :, :], cmp_p[:, t, :, :], each(cmp_m[:, t, :], 15), ALU.subtract)
                i.then_inc(cmp_arg, 1)
                dve.wait_ge(cmp_exp, 1)
                for t in range(2):
                    link(v.tensor_tensor(cmp_p[:, t, :, :], cmp_p[:, t, :, :], over(keep[:, t, :], 16), ALU.mult))
                link(v.tensor_reduce(cmp_m, cmp_p, AX, ALU.add))
                link(v.tensor_scalar(cmp_m, cmp_m, TINY, None, ALU.max))
                link(v.reciprocal(cmp_m, cmp_m))
                taken(("ngate",))
                g = n_gate.rearrange("p t (h b) -> p t h b", b=3)
                link(v.tensor_tensor(cmp_m, cmp_m, g[:, :, :, 0], ALU.mult))
                for t in range(2):
                    i = v.tensor_tensor(cmp_p[:, t, :, :], cmp_p[:, t, :, :], each(cmp_m[:, t, :], 15), ALU.mult)
                i.then_inc(cmp_ready, 1)

            def step_nsa_s(u):
                qt = u % 2
                nk = P * (qt + 1)
                b = two(job(("nsa_s", u)), nk)
                diag = b[:, :, qt * P:(qt + 1) * P]
                link(v.tensor_tensor(diag, diag, over(const("causal"), 2), ALU.add))
                s = 8 * (u % 4)
                v.tensor_reduce(stat[:, s:s + 2], b, AX, ALU.max, negate=True).then_inc(n_max, 1)

            def step_nsa_n(u):
                h, qt = u // 2, u % 2
                nk = P * (qt + 1)
                s = 8 * (u % 4)
                taken(("nsa_s", u))
                link(v.reciprocal(stat[:, s + 4:s + 6], stat[:, s + 2:s + 4]))
                link(v.tensor_tensor(stat[:, s + 4:s + 6], stat[:, s + 4:s + 6], n_gate[:, qt, 3 * h + 1:3 * h + 3],
                                     ALU.mult))
                z = n_p[:, u % BUFS, 0:2 * nk].rearrange("p (a b) -> p a b", a=2)
                v.tensor_tensor(z, z, each(stat[:, s + 4:s + 6], nk), ALU.mult).then_inc(n_ready, 1)

            def step_nsa_o(h):
                qi, half, _ = nsa_head(h)
                rows = slice(64 * half, 64 * half + 64)
                b = job(("nsa_o", h))[rows, 0:T]
                link(v.tensor_copy(r(o_n[rows, qi, :]), b))
                takes(v.tensor_tensor(r(o_lo[rows, qi, :]), b, r(o_n[rows, qi, :]), ALU.subtract), ("nsa_o", h))

            def step_nsa_out(c):
                add_to_x(("nsa_out", c), lambda n: mod2[:, 16 + n:17 + n], 2 * c)

            def step_ffn_in(l, i):
                b = job(("ffn_in", l, i))
                dve.wait_ge(ffn_silu, FFN_T * l + i + 1)
                p = ffn_p[:, i % 2, :]
                link(v.tensor_tensor(p, ffn_g[:, i % 2, :], b[:, T:2 * T], ALU.mult))
                link(v.tensor_copy(r(ffn_h[:, i, :]), p))
                takes(v.tensor_tensor(r(ffn_lo[:, i, :]), p, r(ffn_h[:, i, :]), ALU.subtract), ("ffn_in", l, i))

            def step_ffn_add(l):
                for p in range(4):
                    add_to_x(("ffn_add", l, p), lambda n: mod2[:, 48 * l + 40 + n:48 * l + 41 + n], 2 * p)

            def step_rnn_in(i):
                if i == 0:
                    link(v.memset(u_in[:, :, 0:3], 0.0))
                taken(("rnn_in", i))
                link(v.tensor_scalar(u_c[:, i, :], u_in[:, i, 0:T], col("conv_w", i), col("conv_b", i), ALU.mult,
                                     ALU.add))
                for k in range(1, 4):
                    j = v.scalar_tensor_tensor(u_c[:, i, :], u_in[:, i, k:k + T], col("conv_w", 11 * k + i), u_c[:, i, :],
                                               ALU.mult, ALU.add)
                    if k < 3:
                        link(j)
                j.then_inc(conv_ready, 1)

            def step_rnn_decay(g):
                for i in RNN_GROUPS[g]:
                    dve.wait_ge(rnn_tanh, i + 1)
                    link(v.tensor_tensor(rnn_d[:, i % 2, :], rec[:, i, :], rec[:, i, :], ALU.mult))
                    v.scalar_tensor_tensor(thr[:, i, :], rnn_d[:, i % 2, :], 1.0, thr[:, i, :], ALU.add,
                                           ALU.mult).then_inc(rnn_sqrt_in, 1)
                    link(v.tensor_tensor(inp[:, i, :], inp[:, i, :], u_c[:, i, :], ALU.mult))

            def step_rnn_scan(g):
                for i in RNN_GROUPS[g]:
                    dve.wait_ge(rnn_sqrt, i + 1)
                    link(v.tensor_tensor(inp[:, i, :], inp[:, i, :], thr[:, i, :], ALU.mult))
                    dve.wait_ge(job_done, JOBS[("rnn_gate", min(i + 1, RNN_T - 1))].no)
                    link(v.tensor_tensor_scan(u_c[:, i, :], rec[:, i, :], inp[:, i, :], 0.0, ALU.mult, ALU.add))
                    link(v.tensor_tensor(u_c[:, i, :], gelu_g[:, i, :], u_c[:, i, :], ALU.mult))
                    link(v.tensor_copy(r(gelu_g[:, i, :]), u_c[:, i, :]))
                    v.tensor_tensor(r(u_c[:, i, :]), u_c[:, i, :], r(gelu_g[:, i, :]), ALU.subtract).then_inc(rnn_ready, 1)

            def step_rnn_add():
                for p in range(4):
                    add_to_x(("rnn_add", p), lambda n: mod2[:, 48 + 16 + n:48 + 17 + n], 2 * p)

            parts = {"sum_sq": step_sum_sq, "apply": step_apply, "split": step_split, "decay": step_decay,
                     "mod_out": step_mod_out,
                     "rot": step_rot, "vr": values("vr", v_r), "vn": values("vn", v_n), "kvw": step_kvw, "kn": step_kn,
                     "ret_s": step_ret_s, "ret_mean": step_ret_mean, "ret_var": step_ret_var, "att_s": step_att_s,
                     "att_n": step_att_n, "att_o": step_att_o, "branch": step_branch, "mix_out": step_mix_out,
                     "tok_major": step_tok_major, "router": step_router, "affinity": step_affinity, "pick": step_pick,
                     "gather": step_gather, "pick_t": step_pick_t, "experts": step_experts, "combine": step_combine,
                     "nkv": step_nkv, "nqk": step_nqk, "nnorm": step_nnorm, "nv": step_nv, "ngate": step_ngate,
                     "cmp_k": step_cmp_k,
                     "cmp_v": step_cmp_v, "cmp_s": step_cmp_s, "nsa_s": step_nsa_s, "nsa_n": step_nsa_n,
                     "nsa_o": step_nsa_o, "nsa_out": step_nsa_out, "ffn_in": step_ffn_in, "ffn_add": step_ffn_add,
                     "rnn_in": step_rnn_in, "rnn_decay": step_rnn_decay, "rnn_scan": step_rnn_scan,
                     "rnn_add": step_rnn_add}
            for name, *args in STEPS:
                if name in parts:
                    parts[name](*args)


W_IN = {"qr": 0, "kr": 512, "vr": 1024, "gr": 1536, "qw": 2048, "kw": 2560, "vw": 2688, "qn": 2816, "kn": 3328,
        "vn": 3840, "gate": 4352}
WIN_ORDER = [0, 4, 1, 5, 2, 6, 3, 7]
NSA_ORDER = [4 * (2 * gp + half) + t for gp in range(2) for t in range(4) for half in range(2)]


def weight_stream(np, i):
    w = np.zeros((len(CHUNKS), P, CHUNK), np.float32)
    head = [h * 64 + d for h in WIN_ORDER for d in range(64)]
    nsa_head = [h * 64 + d for h in NSA_ORDER for d in range(64)]
    w_in, nsa_in = i["w_in"][0], i["nsa_w_in_2"][0]
    rg = np.zeros((2, RNN_T * P, RNN_T * P), np.float32)
    for g, name in enumerate(("rg_w_a_2", "rg_w_x_2")):
        for b in range(16):
            rg[g, 88 * b:88 * b + 88, 88 * b:88 * b + 88] = i[name][0][b]

    def cut(m, k):
        return m.reshape(k, P, -1).transpose(1, 0, 2).reshape(P, -1)

    for c, (name, *a) in enumerate(CHUNKS):
        if name == "mod":
            m = i["w_mod"][0] if a[0] < 3 else i["ada_w_2"][a[0] // 3 - 1]
            w[c] = m[P * a[1]:P * a[1] + P, a[0] % 3 * CHUNK:a[0] % 3 * CHUNK + CHUNK]
        elif name == "kvw":
            w[c] = cut(w_in[:, W_IN["kw"]:W_IN["kw"] + 256], 8)
        elif name == "qw":
            w[c] = cut(w_in[:, W_IN["qw"]:W_IN["qw"] + 512][:, head][:, 256 * a[0]:256 * a[0] + 256], 8)
        elif name in W_IN:
            n = W_IN[name] + 256 * a[0]
            w[c] = cut(w_in[:, n:n + 256], 8)
        elif name == "branch":
            m = (i["w_ret"][0], i["w_win"][0][head], i["w_na"][0])[a[1]]
            w[c] = cut(m[:, 512 * a[0]:512 * a[0] + 512], 4)
        elif name == "mix_out":
            w[c] = cut(i["w_out"][0][:, 256 * a[0]:256 * a[0] + 256], 8)
        elif name == "expert":
            e, n = a
            if n < 8:
                w[c, :, 0:D] = i["w_exp_gate"][0][e][P * n:P * n + P]
                w[c, :, D:] = i["w_exp_up"][0][e][P * n:P * n + P]
            else:
                w[c] = cut(i["w_exp_down"][0][e][256 * (n - 8):256 * (n - 7)], 2)
        elif name == "nkv":
            w[c] = cut(nsa_in[:, 1024 + 256 * a[0]:1280 + 256 * a[0]], 8)
        elif name == "nqk":
            m = nsa_in[:, 0:1024][:, nsa_head]
            cols = (nsa_in[:, 1536:1792], nsa_in[:, 2048:2304])[a[0]] if a[0] < 2 else \
                m[:, 256 * (a[0] - 2):256 * (a[0] - 1)]
            w[c] = cut(cols, 8)
        elif name == "nv":
            w[c] = cut(nsa_in[:, 1792 + 512 * a[0]:2048 + 512 * a[0]], 8)
        elif name == "cmp":
            w[c] = cut(i["nsa_cmp_w1_2"][0][a[0]][1024 * a[1]:1024 * a[1] + 1024], 8)
        elif name == "nsa_out":
            w[c] = cut(i["nsa_w_out_2"][0][nsa_head][:, 256 * a[0]:256 * a[0] + 256], 8)
        elif name in ("ffn_in", "rnn_in"):
            m = i["ffn_w_in_2"][a[0]] if name == "ffn_in" else i["rg_w_in_2"][0]
            half, n = m.shape[1] // 2, P * a[-1]
            w[c] = cut(np.concatenate([m[:, n:n + P], m[:, half + n:half + n + P]], axis=1), 8)
        elif name == "ffn_out":
            w[c] = cut(i["ffn_w_out_2"][a[0]][256 * a[1]:256 * a[1] + 256], 2)
        elif name == "rnn_out":
            m = i["rg_w_out_2"][0][256 * a[0]:256 * a[0] + 256]
            w[c, :, 0:m.shape[0] // P * D] = cut(m, m.shape[0] // P)
        elif name == "gates":
            for j, (n, g, k) in enumerate(GATE_TILES[16 * a[0]:16 * a[0] + 16]):
                w[c, :, j * P:(j + 1) * P] = rg[g, k * P:(k + 1) * P, n * P:(n + 1) * P]
    return w


def column_pack(np, i):
    def tiles(x):
        return x.reshape(-1, P).T

    def every(x):
        return np.broadcast_to(x.reshape(1, -1), (P, x.size))

    def twice(x):
        return np.concatenate([x, x], axis=-1).reshape(-1, P).T

    both = np.stack([i["c"][0].reshape(8, P), i["c_ctx"].reshape(8, P)], axis=1).reshape(16, P).T
    parts = {"c_both": both, "c_2": tiles(i["c_2"][0]), "b_mod": tiles(i["b_mod"][0]),
             "ada_b": tiles(i["ada_b_2"].reshape(-1)), "g_mix": tiles(i["g_mix"][0]), "g_ffn": tiles(i["g_ffn"][0]),
             "g_final": tiles(i["g_final"]), "norm1": tiles(i["norm1_g_2"].reshape(-1)),
             "norm2": tiles(i["norm2_g_2"].reshape(-1)), "ret_gn": tiles(i["ret_gn"][0]),
             "decays": every(i["ret_decay_logit"][0].reshape(-1)), "lam": tiles(i["rg_lam_2"][0]),
             "sink": every(i["win_sink"][0][WIN_ORDER]), "q_gain": twice(i["nsa_q_gain_2"][0]),
             "k_gain": twice(i["nsa_k_gain_2"][0]), "pos": tiles(i["nsa_cmp_pos_2"][0].reshape(-1)),
             "conv_w": tiles(i["rg_conv_w_2"][0].reshape(-1)), "conv_b": tiles(i["rg_conv_b_2"][0]),
             "b_a": tiles(i["rg_b_a_2"][0].reshape(-1)), "b_x": tiles(i["rg_b_x_2"][0].reshape(-1))}
    return np.ascontiguousarray(np.concatenate([parts[k] for k in COLS], axis=1))


def constant_pack(np):
    f = np.float32
    p, t = np.arange(P), np.arange(T)

    def rope(size):
        nf = size // 4
        inv = f(10000.0) ** (-np.arange(nf, dtype=f) / f(nf))
        ang = np.concatenate([(t // 64).astype(f)[:, None] * inv, (t % 64).astype(f)[:, None] * inv], axis=1)
        a = np.tile(ang.T, (P // (size // 2), 1))
        m = np.zeros((P, P), f)
        for base in range(0, P, size):
            for d in range(size // 2):
                m[base + d + size // 2, base + d] = -1
                m[base + d, base + d + size // 2] = 1
        return m, np.cos(a).astype(f), np.sin(a).astype(f)

    rot128, cos128, sin128 = rope(128)
    rot64, cos64, sin64 = rope(64)
    q2 = p[:, None, None] + P * np.arange(2)[None, :, None]
    k = t[None, None, :]
    win = np.where(np.abs(k - q2) <= 128, 0, NEG).reshape(P, -1)
    cq, ck = p % 64, t % 64
    start = np.clip(cq - 8, 0, 48)
    na = np.where((ck[None] >= start[:, None]) & (ck[None] < start[:, None] + 16), 0, NEG)
    ends = np.arange(N_CMP) * 16 + 31
    seen = ends[None, None, :] <= q2
    parts = {"ident": np.eye(P), "ones": np.ones((P, P)), "half_ones": np.kron(np.eye(2), np.ones((64, 64))),
             "rot128": rot128, "rot64": rot64, "cos128": cos128, "sin128": sin128, "cos64": cos64, "sin64": sin64,
             "win_mask": win, "na_mask": na, "causal": np.where(p[None] <= p[:, None], 0, NEG),
             "cmp_add": np.where(seen, 0, NEG).reshape(P, -1), "cmp_keep": seen.reshape(P, -1),
             "own": np.kron(np.eye(P)[:, 0:16], np.ones((1, 32))), "token": p[:, None] + P * np.arange(2)[None]}
    consts = np.concatenate([parts[n].astype(f) for n in CONSTS], axis=1)
    key = (p[:, None, None] + P * np.arange(2)[None, :, None])
    decay = np.concatenate([x.reshape(P, -1) for x in (np.maximum(k - key, 0), np.maximum(key - k, 0), k + T - key,
                                                       T - k + key)], axis=1)
    return consts, decay.astype(f)


def kernel(**inputs):
    import numpy as np
    import concourse.bacc as bacc
    from concourse.bass_utils import run_bass_kernel_spmd

    i = {k: np.asarray(x) for k, x in inputs.items()}
    consts, decay = constant_pack(np)

    def feature_major(x):
        return np.ascontiguousarray(x.T.reshape(8, P, T).transpose(1, 0, 2))

    rows = np.arange(4)
    ri = rows[None, :] - rows[:, None] + 7
    cc = np.arange(64)
    ci = np.clip(cc[None, :] - cc[:, None], -15, 15) + 15
    bias = i["na_rpb"][0][:, ri[:, None, :, None], ci[None, :, None, :]].reshape(8, 2, P, T)
    wide = np.concatenate([i["w_router"][0], i["nsa_w_in_2"][0][:, 2560:2608]], axis=1)
    arrays = {
        "w": weight_stream(np, i), "cols": column_pack(np, i), "consts": consts, "decay": decay,
        "x": feature_major(i["x"][0]), "ctx": feature_major(i["ctx"][0]),
        "bias": np.ascontiguousarray(bias.transpose(2, 0, 1, 3).reshape(P, -1)),
        "wide": np.ascontiguousarray(wide.reshape(8, P, 64).transpose(1, 0, 2)),
        "w2c": np.ascontiguousarray(i["nsa_cmp_w2_2"][0].reshape(2, 2, P, 64).transpose(2, 0, 1, 3)),
    }
    nc = bacc.Bacc("TRN2", target_bir_lowering=False, num_devices=1)
    aps = {n: nc.dram_tensor(f"in_{n}", a.shape, F32, kind="ExternalInput").ap() for n, a in arrays.items()}
    out = nc.dram_tensor("out_t", (P, KT, T), F32, kind="ExternalOutput").ap()
    build(nc, aps["w"], aps, out)
    r = run_bass_kernel_spmd(nc, [{f"in_{n}": a for n, a in arrays.items()}], core_ids=[0])
    y = r.results[0]["out_t"]
    return np.ascontiguousarray(y.transpose(2, 1, 0).reshape(1, T, D))
```

```python
from contextlib import ExitStack

import concourse.bass as bass
from concourse import mybir

F32 = mybir.dt.float32
F32R = mybir.dt.float32r
U32 = mybir.dt.uint32
ALU = mybir.AluOpType
ACT = mybir.ActivationFunctionType
AX = mybir.AxisListType.X

P = 128
D = 1024
T = 256
KT = D // P
EPS = 1e-6
NEG = -1e30
TINY = 1.1754944e-38
N_MOD = 6
EXPERTS, CAP = 16, 32
R_HEADS = 4
FFN_T = 22
RNN_T = 11
N_CMP = 15
NSA_HEADS = 16
CHUNK = 2048
SLOTS = 12
MOD_BLOCKS, LAST_BLOCKS = 9, 6
LAG = 3
RNN_GROUPS = [range(0, 4), range(4, 8), range(8, RNN_T)]
BUFS = LAG + 1
FILL_START, FILL_LONG, FILL_SHORT, GATE_EVERY = 7, 2, 1, 2

COLS = {}
CONSTS = {}
DECAY = {}


def lay(table, items):
    at = 0
    for name, width in items:
        table[name] = (at, width)
        at += width
    return at


N_COLS = lay(COLS, [("c_both", 16), ("c_2", 8), ("b_mod", 48), ("ada_b", 96), ("g_mix", 8), ("g_ffn", 8),
                    ("g_final", 8), ("norm1", 16), ("norm2", 16), ("ret_gn", 4), ("decays", 8), ("lam", 11),
                    ("sink", 8), ("q_gain", 1), ("k_gain", 3), ("pos", 32), ("conv_w", 44), ("conv_b", 11),
                    ("b_a", 11), ("b_x", 11)])
N_CONSTS = lay(CONSTS, [("ident", 128), ("ones", 128), ("half_ones", 128), ("rot128", 128), ("rot64", 128),
                        ("cos128", 256), ("sin128", 256), ("cos64", 256), ("sin64", 256), ("win_mask", 512),
                        ("na_mask", 256), ("causal", 128), ("cmp_add", 30), ("cmp_keep", 30), ("own", 512),
                        ("token", 2)])
N_DECAY = lay(DECAY, [("ahead", 512), ("behind", 512), ("ctx_f", 512), ("ctx_b", 512)])


def plan_steps():
    s = [("decay",)] + [("mod", 0, k) for k in range(5)] + [("sum_sq", 0)]
    s += [("mod", 0, k) for k in range(5, KT)] + [("mod_row", 0), ("mod_out", 0)]
    def blocks(first, end):
        x = []
        for b in range(first, end):
            x += [("mod", b, k) for k in range(2)] + ([("mod_out", b - 1)] if b > first else [])
            x += [("mod", b, k) for k in range(2, KT)] + [("mod_row", b)]
        return x + [("mod_out", end - 1)]

    fill = blocks(1, LAST_BLOCKS)

    def take(n):
        for _ in range(min(n, len(fill))):
            s.append(fill.pop(0))

    s.append(("apply", 0))
    take(FILL_START)
    for x in [("kr", 0), ("kr", 1), ("qr", 0), ("qr", 1), ("vr", 0), ("rot", "kr", 0), ("vr", 1), ("rot", "kr", 1),
              ("gr", 0), ("rot", "qr", 0), ("gr", 1), ("rot", "qr", 1), ("kvw",), ("qw", 0), ("qw", 1),
              ("rot", "kw", 0), ("kn", 0), ("rot", "qw", 0), ("kn", 1), ("rot", "qw", 1),
              ("ret_s", 0, 0), ("ret_s", 0, 1), ("vn", 0), ("ret_s", 1, 0), ("ret_s", 1, 1), ("ret_o", 0), ("vn", 1),
              ("ret_s", 2, 0), ("ret_s", 2, 1), ("ret_o", 1), ("qn", 0), ("ret_s", 3, 0), ("ret_s", 3, 1),
              ("ret_o", 2), ("qn", 1), ("ret_o", 3), ("na_bias",), ("gate", 0), ("ret_mean", 0), ("ret_mean", 1),
              ("gate", 1), ("ret_var", 0), ("gate", 2), ("ret_var", 1)]:
        s.append(x)
        if x[0] in ("kr", "vr", "kvw", "kn", "vn"):
            take(FILL_LONG)
        elif x[0] in ("qr", "gr", "qw", "qn", "gate"):
            take(FILL_SHORT)
    gates = [("gate", i) for i in range(3, 12)]
    units = 32
    for i in range(units + LAG + 2):
        if i < units:
            s.append(("att_s", i))
        if gates and i % GATE_EVERY == 0:
            s.append(gates.pop(0))
        take(1)
        if 0 <= i - LAG + 1 < units:
            s.append(("att_n", i - LAG + 1))
        if 0 <= i - LAG < units:
            s.append(("att_t", i - LAG))
        if 0 <= i - LAG - 1 < units and (i - LAG - 1) % 2:
            s.append(("att_o", (i - LAG - 1) // 2))
    s += gates
    take(len(fill))
    s += [("branch", ch, b) for ch in range(2) for b in range(3)]
    s += [("mix_out", c) for c in range(4)]
    s += [("sum_sq", 1), ("apply", 1)]
    s += [("router",), ("tok_major", 0, 0), ("affinity",)]
    s += [("tok_major", t, kq) for t, kq in ((0, 1), (1, 0), (1, 1))] + [("pick",)]
    s += [("gather", k) for k in range(KT)] + [("pick_t", t) for t in range(2)]
    s += [("experts",)]
    s += [("combine", p) for p in range(4)]
    s += [("sum_sq", 2), ("apply", 2), ("sum_sq", 3), ("apply", 3)]
    s += [("nkv", 0), ("nkv", 1), ("nqk", 0), ("nqk", 1), ("cmp", 0, 0), ("cmp", 0, 1), ("cmp", 1, 0),
          ("cmp", 1, 1), ("cmp_k",), ("cmp_v",), ("nnorm", 0), ("nnorm", 1)]
    s += [("nqk", 2), ("nqk", 3), ("nnorm", 2), ("nqk", 4), ("nnorm", 3), ("nqk", 5), ("nnorm", 4), ("nsa_parts",),
          ("nv", 0), ("nnorm", 5), ("nv", 1), ("nnorm", 6), ("ngate",), ("cmp_s",)]
    units = 2 * NSA_HEADS
    fill += blocks(LAST_BLOCKS, MOD_BLOCKS)
    for i in range(units + LAG + 2):
        if i < units:
            s.append(("nsa_s", i))
        take(1)
        if 0 <= i - LAG + 1 < units:
            s.append(("nsa_n", i - LAG + 1))
        if 0 <= i - LAG < units:
            s.append(("nsa_t", i - LAG))
        if 0 <= i - LAG - 1 < units and (i - LAG - 1) % 2:
            s.append(("nsa_o", (i - LAG - 1) // 2))
    take(len(fill))
    s += [("nsa_out", c) for c in range(4)]
    s += [("sum_sq", 4), ("apply", 4)]
    s += [("ffn_in", 0, i) for i in range(FFN_T)] + [("ffn_out", 0, j) for j in range(FFN_T // 2)]
    s += [("ffn_add", 0)]
    s += [("sum_sq", 5), ("apply", 5)]
    s += [("rnn_in", i) for i in range(RNN_T)]
    for g, tiles in enumerate(RNN_GROUPS):
        s += [("rnn_gate", i) for i in tiles] + [("rnn_decay", g)]
        s += [("rnn_out", 0)] if g == len(RNN_GROUPS) - 1 else []
        s.append(("rnn_scan", g))
    s += [("rnn_out", j) for j in range(1, (RNN_T + 1) // 2)] + [("rnn_add",)]
    s += [("sum_sq", 6), ("apply", 6)]
    s += [("ffn_in", 1, i) for i in range(FFN_T)] + [("ffn_out", 1, j) for j in range(FFN_T // 2)]
    s += [("ffn_add", 1)]
    return s


def gate_tiles():
    return [(n, w, k) for n in range(RNN_T) for w in range(2) for k in range(max(0, n - 1), min(RNN_T, n + 2))]


SPLIT_STEPS = {"kr", "qr", "vr", "gr", "kvw", "qw", "kn", "vn", "qn", "gate", "branch", "mix_out",
               "nkv", "nqk", "nv", "nsa_out", "ffn_in", "ffn_out", "rnn_in", "rnn_out"}
ONE_CHUNK = SPLIT_STEPS | {"mod", "cmp"}
GATE_TILES = gate_tiles()


def chunk_keys(steps):
    keys, seen = [], 0
    for x in steps:
        if x[0] in ONE_CHUNK:
            keys.append(x)
        if x[0] == "experts":
            keys += [("expert", e, c) for e in range(EXPERTS) for c in range(12)]
        if x[0] == "rnn_gate":
            last = max(i for i, g in enumerate(GATE_TILES) if g[0] == x[1]) // 16
            while seen <= last:
                keys.append(("gates", seen))
                seen += 1
    return keys


CHUNKS = chunk_keys(plan_steps())
CHUNK_NO = {k: i for i, k in enumerate(CHUNKS)}
FIRST_GATE, FIRST_EXPERT = CHUNK_NO[("gate", 0)], CHUNK_NO[("expert", 0, 0)]
FIRST_SECOND = FIRST_EXPERT + 12 * EXPERTS
RING_USE = [(0, (0, 1, 2, 3, 6, 8), (4, 5)), (FIRST_GATE, (0, 1, 2, 3), (4, 5)), (FIRST_EXPERT, tuple(range(SLOTS)), ()),
            (FIRST_SECOND, tuple(range(9)), (9, 10, 11)), (len(CHUNKS), (), ())]


def plan_ring():
    places, last, fills = [], {}, {}
    for (first, slots, _), (end, _, _) in zip(RING_USE, RING_USE[1:]):
        for c in range(first, end):
            s = slots[(c - first) % len(slots)]
            fills[s] = fills.get(s, 0) + 1
            places.append((s, fills[s], last.get(s)))
            last[s] = c
    return places


RING = plan_ring()


def slot_of(c):
    return RING[c][0]


def landed_count(c):
    return RING[c][1]


def with_splits(steps):
    place, before, uses = {}, {}, [x for x in steps if x[0] in SPLIT_STEPS]
    for u in uses:
        c = CHUNK_NO[u]
        upper = [x[2] for x in RING_USE if x[0] <= c][-1]
        mine = [x for x in place if (CHUNK_NO[x] < FIRST_SECOND) == (c < FIRST_SECOND)]
        n = len(upper)
        place[u] = upper[len(mine) % n], mine[-n] if len(mine) >= n else None
        x = mine[1 - n] if len(mine) >= n - 1 else ("apply", 0) if c < FIRST_SECOND else ("sum_sq", 2)
        free = CHUNKS[min(RING[c][2] + (1 if c < FIRST_SECOND else 3), c - 1)] if RING[c][2] is not None else x
        if free in steps and steps.index(free) > steps.index(x):
            x = free
        before.setdefault(x, []).append(("split", u))
    return [y for x in steps for y in before.get(x, []) + [x]], place


STEPS, SPLIT_PLACE = with_splits(plan_steps())
SPLIT_NO = {u: i for i, u in enumerate(SPLIT_PLACE)}
N_GATE_CHUNKS = -(-len(GATE_TILES) // 16)


class Job:
    pass


def plan_jobs():
    jobs, last, emptied = {}, {}, {"act": 0, "dve": 0}
    turn = [0]

    def add(name, engine, bank=None, counted=True):
        j = Job()
        j.counted = counted
        if bank is None:
            bank = turn[0] % 7
            turn[0] += 1
        j.bank, j.engine = bank, engine
        emptied[engine] += 1
        j.emptied = emptied[engine]
        j.before = last.get(bank)
        last[bank] = j
        jobs[name] = j

    ffn_turn = [0]
    for x in STEPS:
        k = x[0]
        if k == "mod_row":
            add(x, "act", 7, counted=False)
        if k == "mod_out":
            add(x, "dve")
        if k == "sum_sq":
            add(x, "dve")
        elif k in ("kr", "kn"):
            for i in range(2):
                add(x + (i,), "act" if k == "kr" else "dve")
        elif k in ("qr", "gr", "qw", "qn", "gate"):
            add(x, "act")
        elif k in ("vr", "vn"):
            for i in range(2):
                add(x + (i,), "dve")
        elif k == "kvw":
            add(("kvw", "k"), "act")
            add(("kvw", "v"), "dve")
        elif k in ("rot", "ret_s", "ret_mean", "ret_var", "mix_out", "combine", "nqk", "nnorm", "nv", "cmp_k",
                   "cmp_v", "nsa_out", "affinity"):
            add(x, "dve")
        elif k in ("ret_o", "att_s", "att_t", "router", "nkv", "ngate", "nsa_s", "nsa_t"):
            add(x, "act")
        elif k in ("att_o", "nsa_o"):
            add(x, "dve")
        elif k == "branch":
            for i in range(2):
                add(x + (i,), "dve")
        elif k == "tok_major":
            add(x, "dve")
        elif k == "gather":
            add(x, "act" if x[1] % 2 else "dve")
        elif k == "pick":
            add(("pick", "idx"), "dve")
            add(("pick", "gate"), "act")
        elif k == "pick_t":
            add(x, "act")
        elif k == "cmp_s":
            for half in range(2):
                add(("cmp_s", half), "dve")
        elif k == "cmp":
            if x[2] == 1:
                add(("cmp", x[1]), "act")
        elif k == "experts":
            jobs["experts"] = {b: last.get(b) for b in range(3)}
            for b in range(3):
                last[b] = None
        elif k in ("ffn_in", "rnn_in"):
            add(x, "dve" if k == "ffn_in" else "act", ffn_turn[0] % 4)
            ffn_turn[0] += 1
        elif k == "rnn_gate":
            add(x, "act", ffn_turn[0] % 4)
            ffn_turn[0] += 1
        elif k in ("ffn_add", "rnn_add"):
            for p in range(4):
                add(x + (p,), "dve", 4 + p)
    return jobs


def build(nc, w, small, out):
    JOBS = {}
    n = 0
    for name, j in plan_jobs().items():
        JOBS[name] = j
        if isinstance(j, Job) and j.counted:
            n += 1
            j.no = n

    ctx = ExitStack()
    with ctx:
        def sb(name, shape, dt=F32):
            return ctx.enter_context(nc.sbuf_tensor(name, shape, dt))

        def sem(name):
            return ctx.enter_context(nc.semaphore(name))

        twins = {}

        def sb_twin(name, shape):
            at = -(-nc.sbuf_base // 32) * 32
            t = sb(name, shape)
            twins[t.name] = nc.alloc_sbuf_tensor_at(name + "_r", shape, F32R, offset=at)
            return t

        def r(ap):
            return bass.AP(twins[ap.tensor.name], ap.offset, ap.ap)

        ring = sb_twin("ring", [P, SLOTS, CHUNK])
        H = sb_twin("H", [P, KT, 2 * T])
        arena = sb_twin("arena", [P, 16896])
        X = sb("X", [P, KT, T])
        SQ = H[:, :, T:2 * T]
        H_HI, H_LO = H[:, :, T:2 * T], H[:, :, 0:T]
        cols = sb("cols", [P, N_COLS])
        consts = sb("consts", [P, N_CONSTS])
        wide = sb("wide", [P, KT, 64])
        silu_c = sb("silu_c", [P, 48])
        mod = sb("mod", [P, 48, 2])
        mod2 = sb("mod2", [P, 96])
        mod_a = sb("mod_a", [P, 7, 8])
        norm_t = sb("norm_t", [P, 2, 2 * T])
        sp = sb("sp", [P, 8, 19])
        stat = sb("stat", [P, 64])

        def col(name, i=0, width=1):
            return cols[:, COLS[name][0] + i:COLS[name][0] + i + width]

        def const(name, rows=P):
            return consts[0:rows, CONSTS[name][0]:CONSTS[name][0] + CONSTS[name][1]]

        def room(at, *shape, rows=P):
            size = 1
            for k in shape:
                size *= k
            v = arena[0:rows, at:at + size]
            if len(shape) == 2:
                v = v.rearrange("p (a b) -> p a b", a=shape[0])
            if len(shape) == 3:
                v = v.rearrange("p (a b c) -> p a b c", a=shape[0], b=shape[1])
            return v

        ident, ones, half_ones = const("ident"), const("ones"), const("half_ones")
        q_r, k_r, v_r, g_r = room(0, 4, T), room(1024, 4, 2 * T), room(3072, 4, 512), room(5120, 4, T)
        q_w, k_w, v_w = room(6144, 4, T), room(7168, 512), room(7680, 4, 128)
        q_n, k_n, v_n = room(8192, 4, T), room(9216, 4, 512), room(11264, 4, 512)
        hx_hi = room(13312, KT, T)
        probs_t = [room(1024 + 1024 * i, 4, T) for i in range(2)]
        decay_in = room(9216, N_DECAY)
        rope_a, rope_b = room(15872, 2, T), room(16384, 2, T)
        y_r, y_w, y_n = q_r, q_w, q_n
        y_r_hi, y_w_lo, y_n_lo = room(3072, 4, T), room(4096, 4, T), room(5120, 4, T)
        merged, merged_hi = room(1024, KT, T), room(9216, KT, T)
        ctx_in = room(1024, KT, T)
        gates = ring[:, 6:9, :].rearrange("p a b -> p (a b)").rearrange("p (a b) -> p a b", b=T)
        hc_hi = ring[:, 7, :].rearrange("p (a b) -> p a b", b=T)
        sq_0 = room(3072, KT, 2 * T)
        decay_m = ring[:, 9:11, :].rearrange("p a b -> p (a b)").rearrange("p (h k q) -> p h k q", h=4, k=4)
        bias_n = ring[:, 9:11, :].rearrange("p a b -> p (a b)").rearrange("p (h k q) -> p h k q", h=8, k=2)
        ret_p = [ring[:, 11, 1024 * i:1024 * i + 1024].rearrange("p (k q) -> p k q", k=4) for i in range(2)]
        ret_sq = ret_p[0]
        probs = ring[:, 11, :].rearrange("p (a b) -> p a b", a=BUFS)
        h_tok, h_tok_lo, x_e, y_tok = room(0, 2, D), room(6400, 2, D), room(2048, KT, (EXPERTS + 1) * CAP), room(6400, 4, D)
        hot, hot_t = room(10496, 2, 512), room(11520, 4, T)
        gate_b = room(12544, 512)
        aff, aff_t = room(13056, 2, 16), room(13088, T, rows=16)
        top_v = room(13344, 32, rows=16)
        top_f = room(13376, 32, rows=16)
        top_i = ctx.enter_context(nc.sbuf_tensor("top_i", [16, 32], U32))
        spread_i, spread_g = room(13408, 16, 32, rows=16), room(13920, 16, 32, rows=16)
        hot_g = room(13408, 2, 512)
        x_cur, silu_g, hid, hid_t = room(14432, KT, CAP), room(14688, 512), room(15200, 512), room(15712, 4, 2 * CAP)
        qk = room(0, 3104)
        n_sq, n_rs = room(3104, 2, 512), room(4128, 2, 512)
        win_f = [room(5152 + 1024 * i, 4, T) for i in range(2)]
        flat = [room(7200 + 960 * i, 16, 4, 15) for i in range(2)]
        o_n, o_lo = room(5152, KT, T), room(7200, KT, T)
        hid_c = room(9120, 2, 2, 60)
        v_c = room(9360, 4, 64, rows=15)
        v_s = [room(9616 + 512 * i, 2, T) for i in range(2)]
        n_p = room(3104, BUFS, 512)
        n_pt = [room(12176 + 1024 * i, 2, 2, T) for i in range(2)]
        cmp_p = room(14224, 2, 16, 15)
        cmp_pt = [room(14704 + 256 * i, T, rows=15) for i in range(2)]
        n_gate = room(15216, 2, 48)
        wide_hi, wide_lo = room(15600, KT, 48), room(15984, KT, 48)
        ident_1, causal_1 = room(16368, P), room(16496, P)
        cmp_m = room(15312, 2, 16)
        w2c = room(15344, 4, 64).rearrange("p (a b) n -> p a b n", a=2)
        ffn_h, ffn_lo = room(0, FFN_T, T), room(5632, FFN_T, T)
        ffn_g, ffn_p = room(11264, 2, T), room(11776, 2, T)
        gelu_g, u_in, u_c = room(0, RNN_T, T), room(2816, RNN_T, T + 3), room(5665, RNN_T, T)
        rec, inp = room(8481, RNN_T, T), room(11297, RNN_T, T)
        thr, rnn_d = room(2816, RNN_T, T), room(14113, 2, T)

        bank = [ctx.enter_context(nc.psum_tensor(f"bank{i}", [P, 512], F32)) for i in range(8)]
        mods = bank[7]

        def mod_rows(b):
            return room(15872, 2 * T) if b == 0 else norm_t[:, b % 2, :]

        landed = [sem(f"landed{i}") for i in range(SLOTS)]
        chunk_used = sem("chunk_used")
        job_done = sem("job_done")
        emptied = {"act": sem("act_emptied"), "dve": sem("dve_emptied")}
        x_landed, ctx_landed, cols_landed = sem("x_landed"), sem("ctx_landed"), sem("cols_landed")
        consts_landed, decay_landed, wide_landed = sem("consts_landed"), sem("decay_landed"), sem("wide_landed")
        hi_ready, lo_ready, h_split, wide_split = sem("hi_ready"), sem("lo_ready"), sem("h_split"), sem("wide_split")
        mask_ready, tok_hi, rnn_gated = sem("mask_ready"), sem("tok_hi"), sem("rnn_gated")
        bias_landed, bias_ready, w2_landed = sem("bias_landed"), sem("bias_ready"), sem("w2_landed")
        dve_step, act_step = sem("dve_step"), sem("act_step")
        silu_ready, mod_done, sq_x, sq_ctx = sem("silu_ready"), sem("mod_done"), sem("sq_x"), sem("sq_ctx")
        sq_ready, std_ready, h_scaled, h_ready = sem("sq_ready"), sem("std_ready"), sem("h_scaled"), sem("h_ready")
        x_final = sem("x_final")
        sp_arg, sp_exp, sp_ready = sem("sp_arg"), sem("sp_exp"), sem("sp_ready")
        decay_arg, decay_exp, decay_ready = sem("decay_arg"), sem("decay_exp"), sem("decay_ready")
        roped = sem("roped")
        ret_sq_ready, ret_std, ret_ready = sem("ret_sq_ready"), sem("ret_std"), sem("ret_ready")
        max_ready, sink_ready, probs_ready = sem("max_ready"), sem("sink_ready"), sem("probs_ready")
        merged_ready = sem("merged_ready")
        aff_max, aff_ready, spread_ready = sem("aff_max"), sem("aff_ready"), sem("spread_ready")
        x_cur_ready, gate_up_done, silu_g_ready = sem("x_cur_ready"), sem("gate_up_done"), sem("silu_g_ready")
        hid_ready, hid_turned, hid_t_ready = sem("hid_ready"), sem("hid_turned"), sem("hid_t_ready")
        down_done, ye_taken, hot_g_ready = sem("down_done"), sem("ye_taken"), sem("hot_g_ready")
        flat_ready, n_sq_ready, n_std, n_normed = sem("flat_ready"), sem("n_sq_ready"), sem("n_std"), sem("n_normed")
        cmp_arg, cmp_exp, cmp_ready = sem("cmp_arg"), sem("cmp_exp"), sem("cmp_ready")
        n_max, n_ready = sem("n_max"), sem("n_ready")
        ffn_silu, conv_ready, rnn_tanh, rnn_sqrt_in, rnn_sqrt, rnn_ready = (
            sem("ffn_silu"), sem("conv_ready"), sem("rnn_tanh"), sem("rnn_sqrt_in"), sem("rnn_sqrt"),
            sem("rnn_ready"))
        out_landed = sem("out_landed")

        def att_unit(u):
            return u >= 16, u // 2 % 8, u % 2

        def att_head(kind, hd):
            return (hd // 2, hd % 2)

        def nsa_head(h):
            g = h // 4
            return g // 2 * 4 + h % 4, g % 2, g // 2

        X_JOBS = {1: [("mix_out", c) for c in range(4)], 2: [("combine", p) for p in range(4)],
                  4: [("nsa_out", c) for c in range(4)], 5: [("ffn_add", 0, p) for p in range(4)],
                  6: [("rnn_add", p) for p in range(4)]}
        NORM_GAIN = {0: ("g_mix", 0), 1: ("g_ffn", 0), 3: ("norm1", 0), 4: ("norm2", 0), 5: ("norm1", 8),
                     6: ("norm2", 8)}
        SHIFT2 = {3: 0, 4: 24, 5: 48, 6: 72}
        H_COUNT = {0: 16, 1: 24, 3: 32, 4: 40, 5: 48, 6: 56}

        def split_slots(key):
            return ring[:, SPLIT_PLACE[key][0], :], ring[:, slot_of(CHUNK_NO[key]), :]

        def shift_of(ni, k):
            if ni == 0:
                return mod[:, k, 0:1]
            if ni == 1:
                return mod[:, 24 + k, 0:1]
            return mod2[:, SHIFT2[ni] + k:SHIFT2[ni] + k + 1]

        block = ctx.enter_context(nc.Block())

        @block.sync
        def _(sp_eng):
            def load(s, source):
                sp_eng.dma_start(ring[:, s, :], source).then_inc(landed[s], 16)

            def rounds(stage):
                first, slots, _ = RING_USE[stage]
                n, end = len(slots), RING_USE[stage + 1][0]
                full = (end - first) // n
                source = w[first:first + full * n].rearrange("(r s) p f -> r s p f", s=n)
                with sp_eng.Fori(1, full) as r:
                    for i, s in enumerate(slots):
                        sp_eng.wait_ge(chunk_used, r * n + (first + i + 1 - n))
                        load(s, source[r, i])
                for c in range(first + full * n, end):
                    sp_eng.wait_ge(chunk_used, c - n + 1)
                    load(slot_of(c), w[c])

            for c, s in enumerate(RING_USE[0][1]):
                load(s, w[c])
            rounds(0)
            for i, s in enumerate(RING_USE[1][1]):
                c = FIRST_GATE + i
                sp_eng.wait_ge(chunk_used, RING[c][2] + 1)
                load(s, w[c])
            rounds(1)
            sp_eng.wait_ge(merged_ready, 4)
            for s in range(6, SLOTS):
                load(s, w[FIRST_EXPERT + s])
            for s in RING_USE[1][1]:
                sp_eng.wait_ge(chunk_used, RING[FIRST_EXPERT + s][2] + 1)
                load(s, w[FIRST_EXPERT + s])
            sp_eng.wait_ge(chunk_used, FIRST_EXPERT)
            for s in RING_USE[1][2]:
                load(s, w[FIRST_EXPERT + s])
            rounds(2)
            for i, s in enumerate(RING_USE[3][1]):
                sp_eng.wait_ge(chunk_used, RING[FIRST_SECOND + i][2] + 1)
                load(s, w[FIRST_SECOND + i])
            rounds(3)
            for p in range(4):
                sp_eng.wait_ge(emptied["dve"], JOBS[("ffn_add", 1, p)].emptied)
                sp_eng.dma_start(out[:, 2 * p:2 * p + 2, :], X[:, 2 * p:2 * p + 2, :]).then_inc(out_landed, 16)
            sp_eng.wait_ge(out_landed, 64)

        @block.gpsimd
        def _(eng):
            nc.gpsimd.memset(stat[:, 63:64], 1.0)
            nc.gpsimd.memset(silu_c[:, 24:48], 0.0).then_inc(silu_ready, 1)
            eng.dma_start(wide[:, :, :], small["wide"]).then_inc(wide_landed, 16)
            eng.wait_ge(emptied["dve"], JOBS[("ret_s", 3, 1)].emptied)
            eng.dma_start(bias_n.rearrange("p h k q -> p (h k q)"), small["bias"]).then_inc(bias_landed, 16)
            eng.wait_ge(bias_landed, 16)
            eng.wait_ge(consts_landed, 16)
            mask = const("na_mask").unsqueeze(1).to_broadcast([P, 16, T])
            flat_bias = bias_n.rearrange("p h k q -> p (h k) q")
            nc.gpsimd.tensor_tensor(flat_bias, flat_bias, mask, ALU.add).then_inc(bias_ready, 1)
            eng.wait_ge(emptied["dve"], JOBS[("combine", 3)].emptied)
            eng.dma_start(w2c, small["w2c"]).then_inc(w2_landed, 16)
            for n in range(RNN_T):
                eng.wait_ge(emptied["act"], JOBS[("rnn_gate", n)].emptied)
                eng.wait_ge(conv_ready, n + 1)
                nc.gpsimd.tensor_tensor(inp[:, n, :], inp[:, n, :], u_c[:, n, :], ALU.mult).then_inc(rnn_gated, 1)

        @block.tensor
        def _(pe):
            owed = [0]

            def mm(o, lhsT, rhs, start, stop, ends=None, grouped=False):
                i = nc.tensor.matmul(o, lhsT, rhs, start=start, stop=stop, skip_group_check=grouped)
                return settle(i, ends)

            def tr(o, in_, ends=None, rows=P):
                i = nc.tensor.transpose(o, in_, ident[0:rows, 0:rows])
                return settle(i, ends)

            def settle(i, ends):
                if ends is not None:
                    i.then_inc(ends, 1)
                elif owed[0]:
                    i.then_inc(chunk_used, owed[0])
                    owed[0] = 0
                return i

            def chunk(key):
                c = CHUNK_NO[key]
                pe.wait_ge(landed[slot_of(c)], 16 * landed_count(c))
                return ring[:, slot_of(c), :].rearrange("p (k n) -> p k n", k=8)

            def begin(name):
                j = JOBS[name]
                if j.before is not None:
                    pe.wait_ge(emptied[j.before.engine], j.before.emptied)
                return bank[j.bank]

            def in_sbuf(name):
                pe.wait_ge(emptied[JOBS[name].engine], JOBS[name].emptied)

            def h_is(ni, k=KT - 1):
                if ni >= 3:
                    pe.wait_ge(h_split, 16 + 8 * (ni - 3) + k + 1)
                else:
                    pe.wait_ge(h_ready, H_COUNT[ni])

            def split_chunk(key, n):
                pe.wait_ge(lo_ready, SPLIT_NO[key] + 1)
                return [x.rearrange("p (k n) -> p k n", k=n) for x in split_slots(key)]

            def mm3(o, a, b, start, stop, ends=None, grouped=False):
                a, b = [r(x) for x in a], [r(x) for x in b]
                mm(o, a[0], b[0], start, False, grouped=grouped)
                mm(o, a[0], b[1], False, False, grouped=grouped)
                return mm(o, a[1], b[0], False, stop, ends, grouped)

            def tiles3(x, act, ni=None):
                hi, lo = split_chunk(x, 8)
                b = begin(x)
                for j in range(2):
                    for k in range(KT):
                        if j == 0 and ni is not None:
                            h_is(ni, k)
                        n = slice(j * P, (j + 1) * P)
                        mm3(b[:, j * T:(j + 1) * T], (hi[:, k, n], lo[:, k, n]), act(k), k == 0, k == KT - 1,
                            job_done if j == 1 and k == KT - 1 else None)
                owed[0] += 1

            def h3(k):
                return H_HI[:, k, :], H_LO[:, k, :]

            H0 = ((hx_hi, H[:, :, 0:T]), (hc_hi, H[:, :, T:2 * T]))

            def hx(k):
                return [x[:, k, :] for x in H0[0]]

            def key_tile(x, b, n, ends, first=False):
                hi, lo = split_chunk(x, 8)
                for c in range(2):
                    for k in range(KT):
                        if first:
                            pe.wait_ge(h_split, 2 * k + 1 + c)
                        mm3(b[:, c * T:(c + 1) * T], (hi[:, k, n], lo[:, k, n]), [y[:, k, :] for y in H0[c]], k == 0,
                            k == KT - 1, ends if c and k == KT - 1 else None)

            def key_tiles(x):
                for j in range(2):
                    key_tile(x, begin(x + (j,)), slice(j * P, (j + 1) * P), job_done, x == ("kr", 0) and j == 0)
                owed[0] += 1

            def value_tile(x, o, t, n, ends):
                hi, lo = split_chunk(x, 8)
                at = slice(t % 2 * P, t % 2 * P + P)
                for k in range(KT):
                    mm3(o, [y[:, k, at] for y in H0[t // 2]], (hi[:, k, n], lo[:, k, n]), k == 0, k == KT - 1,
                        ends if k == KT - 1 else None)

            def value_tiles(x, names):
                for i, name in enumerate(names):
                    b = begin(name)
                    for j in range(2):
                        value_tile(x, b[:, j * T:(j + 1) * T], 2 * i + j, slice(0, T), job_done if j else None)
                owed[0] += 1

            def step_sum_sq(ni):
                if ni == 0:
                    pe.wait_ge(consts_landed, 16)
                    pe.wait_ge(sq_x, 1)
                    pe.wait_ge(sq_ctx, 1)
                b = begin(("sum_sq", ni))
                for k in range(KT):
                    if ni and k % 2 == 0:
                        pe.wait_ge(sq_ready, 4 * (ni - 1) + k // 2 + 1)
                    if ni == 0:
                        mm(b[:, :], ones, sq_0[:, k, :], k == 0, k == KT - 1, job_done if k == KT - 1 else None)
                    else:
                        mm(b[:, 0:T], ones, SQ[:, k, :], k == 0, k == KT - 1, job_done if k == KT - 1 else None)

            def step_mod(blk, k):
                ck = ring[:, slot_of(CHUNK_NO[("mod", blk, k)]), :]
                chunk(("mod", blk, k))
                if blk == 0 and k == 0:
                    pe.wait_ge(silu_ready, 2)
                if k == 0:
                    begin(("mod_row", blk))
                if blk < 3:
                    v = silu_c[:, 2 * k:2 * k + 32]
                else:
                    v = silu_c[:, 16 + k:17 + k].to_broadcast([P, 32])
                for j in range(4):
                    mm(mods[32 * j:32 * j + 32, :], v, ck[:, 512 * j:512 * j + 512], k == 0, k == KT - 1,
                       mod_done if j == 3 and k == KT - 1 else None)
                owed[0] += 1

            def step_mod_out(blk):
                in_sbuf(("mod_row", blk))
                b = begin(("mod_out", blk))
                for i in range(4):
                    tr(b[:, i * P:(i + 1) * P], mod_rows(blk)[:, i * P:(i + 1) * P], job_done if i == 3 else None)

            def step_kr(c):
                key_tiles(("kr", c))

            def step_rot(what, p):
                if what == "kr":
                    in_sbuf(("kr", p, 1))
                    m, v, n = const("rot128"), k_r[:, 2 * p:2 * p + 2, 0:T], 512
                elif what == "qr":
                    in_sbuf(("qr", p))
                    m, v, n = const("rot128"), q_r[:, 2 * p:2 * p + 2, :], 512
                elif what == "kw":
                    in_sbuf(("kvw", "k"))
                    m, v, n = const("rot64"), k_w[:, 0:T], 256
                else:
                    in_sbuf(("qw", p))
                    m, v, n = const("rot64"), q_w[:, 2 * p:2 * p + 2, :], 512
                mm(begin(("rot", what, p))[:, 0:n], m, v, True, True, job_done)

            def step_vr(c):
                value_tiles(("vr", c), [("vr", c, 0), ("vr", c, 1)])

            def step_vn(c):
                value_tiles(("vn", c), [("vn", c, 0), ("vn", c, 1)])

            def step_kvw():
                key_tile(("kvw",), begin(("kvw", "k")), slice(0, P), job_done)
                b = begin(("kvw", "v"))
                for t in range(4):
                    value_tile(("kvw",), b[:, t * P:(t + 1) * P], t, slice(P, 2 * P), job_done if t == 3 else None)
                owed[0] += 1

            def step_ret_s(h, kp):
                if h == 0 and kp == 0:
                    pe.wait_ge(roped, 4)
                b = begin(("ret_s", h, kp))
                for j in range(2):
                    mm(b[:, j * T:(j + 1) * T], k_r[:, h, (2 * kp + j) * P:(2 * kp + j + 1) * P], q_r[:, h, :], True,
                       True, job_done if j else None)

            def step_ret_o(h):
                in_sbuf(("ret_s", h, 1))
                b = begin(("ret_o", h))
                for kt in range(4):
                    mm(b[:, 0:T], v_r[:, kt, h * P:(h + 1) * P], ret_p[h % 2][:, kt, :], kt == 0, kt == 3,
                       job_done if kt == 3 else None)

            def step_ret_mean(p):
                in_sbuf(("ret_o", 2 * p + 1))
                mm(begin(("ret_mean", p))[:, :], ones, y_r[:, 2 * p:2 * p + 2, :], True, True, job_done)

            def step_ret_var(p):
                pe.wait_ge(ret_sq_ready, p + 1)
                mm(begin(("ret_var", p))[:, :], ones, ret_sq[:, 2 * p:2 * p + 2, :], True, True, job_done)

            def step_att_s(u):
                na, hd, qt = att_unit(u)
                if u == 0:
                    pe.wait_ge(roped, 7)
                if u == 16:
                    in_sbuf(("qn", 1))
                    in_sbuf(("kn", 1, 1))
                t, half = att_head(na, hd)
                rows = slice(64 * half, 64 * half + 64)
                q = (q_n if na else q_w)[rows, t, qt * P:(qt + 1) * P]
                keys = k_n[rows, t, :] if na else k_w[rows, :]
                mm(begin(("att_s", u))[:, :], q, keys, True, True, job_done)

            def step_att_t(u):
                pe.wait_ge(probs_ready, u + 1)
                b = begin(("att_t", u))
                for kt in range(4):
                    tr(b[:, kt * P:(kt + 1) * P], probs[:, u % BUFS, kt * P:(kt + 1) * P], job_done if kt == 3 else None)

            def step_att_o(i):
                na, hd, _ = att_unit(2 * i)
                in_sbuf(("att_t", 2 * i + 1))
                if i == 0:
                    in_sbuf(("kvw", "v"))
                if i == 8:
                    in_sbuf(("vn", 1, 1))
                t, half = att_head(na, hd)
                b = begin(("att_o", i))
                for kt in range(4):
                    v = v_n[:, kt, hd * 64:hd * 64 + 64] if na else v_w[:, kt, half * 64:half * 64 + 64]
                    mm(b[64 * half:64 * half + 64, 0:T], v, probs_t[i % 2][:, kt, :], kt == 0, kt == 3,
                       job_done if kt == 3 else None)

            def step_branch(ch, br):
                hi, lo = split_chunk(("branch", ch, br), 4)
                y = ((y_r_hi, y_r), (y_w, y_w_lo), (y_n, y_n_lo))[br]
                if br == 0:
                    pe.wait_ge(ret_ready, 2)
                else:
                    in_sbuf(("att_o", 7 if br == 1 else 15))
                for p in range(2):
                    b = begin(("branch", ch, br, p))
                    for j in range(2):
                        for k in range(4):
                            n = slice((2 * p + j) * P, (2 * p + j + 1) * P)
                            mm3(b[:, j * T:(j + 1) * T], (hi[:, k, n], lo[:, k, n]), [x[:, k, :] for x in y], k == 0,
                                k == 3, job_done if j == 1 and k == 3 else None)
                owed[0] += 1

            def step_mix_out(c):
                def act(k):
                    if c == 0:
                        pe.wait_ge(merged_ready, k // 2 + 1)
                    return merged_hi[:, k, :], merged[:, k, :]

                tiles3(("mix_out", c), act)

            def step_tok_major(t, kq):
                b = begin(("tok_major", t, kq))
                for j in range(4):
                    tr(b[:, j * P:(j + 1) * P], H[:, 4 * kq + j, t * P:(t + 1) * P], job_done if j == 3 else None)

            def step_router():
                h_is(1)
                pe.wait_ge(wide_landed, 16)
                b = begin(("router",))
                for t in range(2):
                    for k in range(KT):
                        mm(b[:, t * 16:t * 16 + 16], H[:, k, t * P:(t + 1) * P], wide[:, k, 0:16], k == 0, k == KT - 1,
                           job_done if t == 1 and k == KT - 1 else None)

            def step_affinity():
                pe.wait_ge(aff_ready, 1)
                b = begin(("affinity",))
                for t in range(2):
                    tr(b[0:16, t * P:(t + 1) * P], aff[:, t, :], job_done if t else None)

            def step_pick():
                pe.wait_ge(spread_ready, 1)
                mm(begin(("pick", "idx"))[:, :], ones[0:16, :], spread_i, True, True, job_done)
                mm(begin(("pick", "gate"))[:, :], ones[0:16, :], spread_g, True, True, job_done)

            def step_gather(k):
                if k == 0:
                    for t in range(2):
                        for kq in range(2):
                            in_sbuf(("tok_major", t, kq))
                    in_sbuf(("pick", "idx"))
                b = begin(("gather", k))
                for t in range(2):
                    for part in (h_tok, h_tok_lo):
                        mm(b[:, :], r(part[:, t, k * P:(k + 1) * P]), r(hot[:, t, :]), t == 0 and part is h_tok,
                           t == 1 and part is h_tok_lo, job_done if t == 1 and part is h_tok_lo else None)

            def step_pick_t(t):
                pe.wait_ge(hot_g_ready, 1)
                b = begin(("pick_t", t))
                for j in range(4):
                    tr(b[:, j * P:(j + 1) * P], hot_g[:, t, j * P:(j + 1) * P], job_done if j == 3 else None)

            def step_experts():
                for b in range(3):
                    j = JOBS["experts"][b]
                    pe.wait_ge(emptied[j.engine], j.emptied)
                if owed[0]:
                    pe.sem_inc(chunk_used, owed[0])
                    owed[0] = 0
                before = [landed_count(FIRST_EXPERT + s) - 1 for s in range(SLOTS)]
                mm = nc.tensor.matmul
                with pe.Fori(0, EXPERTS // 4) as i:
                    for u in range(4):
                        pe.wait_ge(x_cur_ready, i * 4 + (u + 1))
                        for k in range(KT):
                            pe.wait_ge(landed[k], i * 64 + 16 * (before[k] + u + 1))
                            for j in range(4):
                                last = mm(bank[0][32 * j:32 * j + 32, :], x_cur[:, k, :],
                                          ring[:, k, 512 * j:512 * j + 512], start=k == 0, stop=k == KT - 1)
                            last.then_inc(chunk_used if k < KT - 1 else gate_up_done, 1)
                        pe.wait_ge(hid_ready, i * 4 + (u + 1))
                        pe.sem_inc(chunk_used, 1)
                        for c in range(4):
                            last = nc.tensor.transpose(bank[1][:, c * 64:c * 64 + 64], hid[64:P, c * P:(c + 1) * P],
                                                       ident[64:P, 64:P])
                        last.then_inc(hid_turned, 1)
                        pe.wait_ge(hid_t_ready, i * 4 + (u + 1))
                        pe.wait_ge(ye_taken, i * 4 + (u + 1))
                        for c in range(4):
                            s = KT + c
                            pe.wait_ge(landed[s], i * 64 + 16 * (before[s] + u + 1))
                            ck = ring[:, s, :].rearrange("p (k n) -> p k n", k=2)
                            for kk in range(2):
                                k = 2 * c + kk
                                for j in range(4):
                                    last = mm(bank[2][32 * j:32 * j + 32, 0:T],
                                              hid_t[:, k % 4, k // 4 * CAP:k // 4 * CAP + CAP], ck[:, kk, j * T:j * T + T],
                                              start=k == 0, stop=k == KT - 1)
                                    if kk == 0 and j == 3 and c:
                                        last.then_inc(chunk_used, 1)
                        last.then_inc(down_done, 1)
                        pe.wait_ge(down_done, i * 4 + (u + 1))
                        pe.sem_inc(chunk_used, 1)
                pe.wait_ge(ye_taken, EXPERTS + 1)

            def step_combine(p):
                b = begin(("combine", p))
                if p == 0:
                    in_sbuf(("pick_t", 1))
                for i in range(2):
                    n = 2 * p + i
                    for j in range(4):
                        mm(b[:, i * T:(i + 1) * T], y_tok[:, j, n * P:(n + 1) * P], hot_t[:, j, :], j == 0, j == 3,
                           job_done if i == 1 and j == 3 else None)

            def step_nkv(kv):
                tiles3(("nkv", kv), h3, 3)

            def step_nnorm(i):
                pe.wait_ge(n_sq_ready, i + 1)
                n = 512 if i < 6 else 30
                mm(begin(("nnorm", i))[:, 0:n], half_ones, n_sq[:, i % 2, 0:n], True, True, job_done)

            def step_nv(i):
                hi, lo = split_chunk(("nv", i), 8)
                b = begin(("nv", i))
                for j in range(2):
                    t = slice(j * P, (j + 1) * P)
                    for k in range(KT):
                        mm3(b[:, j * T:(j + 1) * T], (H_HI[:, k, t], H_LO[:, k, t]), (hi[:, k, :], lo[:, k, :]), k == 0,
                            k == KT - 1, job_done if j == 1 and k == KT - 1 else None)
                owed[0] += 1

            def step_ngate():
                pe.wait_ge(wide_split, 1)
                b = begin(("ngate",))
                for t in range(2):
                    for k in range(KT):
                        mm3(b[:, t * 48:t * 48 + 48], [x[:, t * P:(t + 1) * P] for x in h3(k)],
                            (wide_hi[:, k, :], wide_lo[:, k, :]), k == 0, k == KT - 1,
                            job_done if t == 1 and k == KT - 1 else None)

            cmp_bank = [None]

            def step_cmp(kv, part):
                ck = chunk(("cmp", kv, part))
                if part == 0:
                    pe.wait_ge(flat_ready, kv + 1)
                    cmp_bank[0] = begin(("cmp", kv))
                for ht in range(2):
                    for j in range(8):
                        f = flat[kv][:, 8 * part + j, :, :]
                        mm(cmp_bank[0][:, ht * 60:ht * 60 + 60], ck[:, j, ht * P:(ht + 1) * P], f,
                           part == 0 and ht == 0 and j == 0, part == 1 and j == 7,
                           job_done if part == 1 and ht == 1 and j == 7 else None, grouped=True)
                owed[0] += 1

            def step_cmp_k():
                pe.wait_ge(w2_landed, 16)
                in_sbuf(("cmp", 0))
                b = begin(("cmp_k",))
                for par in range(2):
                    for ht in range(2):
                        v = hid_c[:, 0, ht, :].rearrange("p (g c) -> p g c", g=4)[:, par::2, :]
                        mm(b[64 * par:64 * par + 64, 0:30], w2c[:, 0, ht, :], v, ht == 0, ht == 1,
                           job_done if par and ht else None)

            def step_cmp_v():
                in_sbuf(("cmp", 1))
                b = begin(("cmp_v",))
                for g in range(4):
                    for ht in range(2):
                        mm(b[0:N_CMP, g * 64:g * 64 + 64], hid_c[:, 1, ht, g * N_CMP:(g + 1) * N_CMP], w2c[:, 1, ht, :],
                           ht == 0, ht == 1, job_done if g == 3 and ht else None)

            def step_cmp_s():
                pe.wait_ge(n_normed, 7)
                for half in range(2):
                    b = begin(("cmp_s", half))
                    rows = slice(64 * half, 64 * half + 64)
                    for qt in range(2):
                        for qi in range(8):
                            gp, at = qi // 4, (qt * 8 + qi) * N_CMP
                            mm(b[:, at:at + N_CMP], qk[rows, 1024 + qi * T + qt * P:1024 + qi * T + (qt + 1) * P],
                               qk[rows, 3072 + gp * N_CMP:3072 + (gp + 1) * N_CMP], True, True,
                               job_done if qt == 1 and qi == 7 else None)

            def step_nsa_s(u):
                h, qt = u // 2, u % 2
                qi, half, gp = nsa_head(h)
                rows = slice(64 * half, 64 * half + 64)
                nk = P * (qt + 1)
                b = begin(("nsa_s", u))
                for br in range(2):
                    mm(b[:, br * nk:(br + 1) * nk], qk[rows, 1024 + qi * T + qt * P:1024 + qi * T + (qt + 1) * P],
                       qk[rows, br * 512 + gp * T:br * 512 + gp * T + nk], br == 0, False, grouped=True)
                pe.wait_ge(mask_ready, 1)
                mm(b[:, 0:2 * nk].rearrange("p (a b) -> p a b", a=2)[:, :, qt * P:(qt + 1) * P], r(ident_1),
                   r(causal_1).unsqueeze(1).to_broadcast([P, 2, P]), False, True, job_done, grouped=True)

            def step_nsa_t(u):
                h, qt = u // 2, u % 2
                pe.wait_ge(n_ready, u + 1)
                if u == 0:
                    pe.wait_ge(cmp_ready, 1)
                nk = P * (qt + 1)
                b = begin(("nsa_t", u))
                if qt == 0:
                    for q in range(2):
                        tr(b[0:N_CMP, 256 + q * P:256 + (q + 1) * P], cmp_p[:, q, h, :])
                for kt in range(qt + 1):
                    for br in range(2):
                        at = (2 * kt + br) * P
                        tr(b[:, at:at + P], n_p[:, u % BUFS, br * nk + kt * P:br * nk + (kt + 1) * P],
                           job_done if kt == qt and br else None)

            def step_nsa_o(h):
                qi, half, gp = nsa_head(h)
                g = h // 4
                in_sbuf(("nsa_t", 2 * h + 1))
                b = begin(("nsa_o", h))[64 * half:64 * half + 64, 0:T]
                pt = n_pt[h % 2]
                mm(b, v_c[:, g, :], cmp_pt[h % 2], True, False)
                for br in range(2):
                    mm(b, v_s[br][:, 0, g * 64:g * 64 + 64], pt[:, 0, br, :], False, False)
                for br in range(2):
                    mm(b[:, P:T], v_s[br][:, 1, g * 64:g * 64 + 64], pt[:, 1, br, P:T], False, br == 1,
                       job_done if br else None)

            def step_nsa_out(c):
                if c == 0:
                    in_sbuf(("nsa_o", NSA_HEADS - 1))
                tiles3(("nsa_out", c), lambda k: (o_n[:, k, :], o_lo[:, k, :]))

            def step_ffn_in(l, i):
                tiles3(("ffn_in", l, i), h3, 4 + 2 * l)

            def rows_out(key, j, n_k, act, adds):
                hi, lo = split_chunk(key, 2)
                if j == 0:
                    for p in range(4):
                        begin(adds[p])
                for n in range(KT):
                    o = bank[4 + n // 2][:, n % 2 * T:n % 2 * T + T]
                    at = slice(n * P, (n + 1) * P)
                    for kk in range(min(2, n_k - 2 * j)):
                        k = 2 * j + kk
                        mm3(o, (hi[:, kk, at], lo[:, kk, at]), act(k), k == 0 and n % 2 == 0, k == n_k - 1,
                            job_done if k == n_k - 1 and n % 2 else None, grouped=True)
                owed[0] += 1

            def step_ffn_out(l, j):
                in_sbuf(("ffn_in", l, 2 * j + 1))
                rows_out(("ffn_out", l, j), j, FFN_T, lambda k: (ffn_h[:, k, :], ffn_lo[:, k, :]),
                         [("ffn_add", l, p) for p in range(4)])

            def step_rnn_in(i):
                tiles3(("rnn_in", i), h3, 5)

            seen = [-1]

            def step_rnn_gate(n):
                pe.wait_ge(conv_ready, min(n + 2, RNN_T))
                b = begin(("rnn_gate", n))
                mine = [(i, x) for i, x in enumerate(GATE_TILES) if x[0] == n]
                for i, (_, wh, k) in mine:
                    if i // 16 != seen[0]:
                        if seen[0] >= 0:
                            owed[0] += 1
                        seen[0] = i // 16
                    ck = chunk(("gates", i // 16)).rearrange("p k n -> p (k n)")
                    ks = [x[2] for _, x in mine if x[1] == wh]
                    mm(b[:, wh * T:(wh + 1) * T], ck[:, i % 16 * P:(i % 16 + 1) * P], u_c[:, k, :], k == ks[0],
                       k == ks[-1], job_done if (i, (n, wh, k)) == mine[-1] else None)
                if n == RNN_T - 1:
                    owed[0] += 1

            def step_rnn_out(j):
                pe.wait_ge(rnn_ready, min(2 * j + 2, RNN_T))
                rows_out(("rnn_out", j), j, RNN_T, lambda k: (gelu_g[:, k, :], u_c[:, k, :]),
                         [("rnn_add", p) for p in range(4)])

            def whole(name):
                return lambda *a: tiles3((name,) + a, hx)

            parts = {"sum_sq": step_sum_sq, "mod": step_mod, "mod_out": step_mod_out, "kr": step_kr, "rot": step_rot, "qr": whole("qr"),
                     "vr": step_vr, "gr": whole("gr"), "kvw": step_kvw, "qw": whole("qw"),
                     "kn": lambda c: key_tiles(("kn", c)), "vn": step_vn, "qn": whole("qn"), "gate": whole("gate"),
                     "ret_s": step_ret_s, "ret_o": step_ret_o, "ret_mean": step_ret_mean, "ret_var": step_ret_var,
                     "att_s": step_att_s, "att_t": step_att_t, "att_o": step_att_o, "branch": step_branch,
                     "mix_out": step_mix_out, "tok_major": step_tok_major, "router": step_router,
                     "affinity": step_affinity, "pick": step_pick, "gather": step_gather, "pick_t": step_pick_t,
                     "experts": step_experts, "combine": step_combine, "nkv": step_nkv,
                     "nqk": lambda i: tiles3(("nqk", i), h3), "nnorm": step_nnorm, "nv": step_nv, "ngate": step_ngate, "cmp": step_cmp,
                     "cmp_k": step_cmp_k, "cmp_v": step_cmp_v, "cmp_s": step_cmp_s, "nsa_s": step_nsa_s,
                     "nsa_t": step_nsa_t, "nsa_o": step_nsa_o, "nsa_out": step_nsa_out, "ffn_in": step_ffn_in,
                     "ffn_out": step_ffn_out, "rnn_in": step_rnn_in, "rnn_gate": step_rnn_gate,
                     "rnn_out": step_rnn_out}
            for name, *args in STEPS:
                if name in parts:
                    parts[name](*args)

        @block.scalar
        def _(act):
            f = nc.scalar.activation

            def job(name):
                act.wait_ge(job_done, JOBS[name].no)
                return bank[JOBS[name].bank]

            def takes(i, name):
                assert JOBS[name].engine == "act"
                i.then_inc(emptied["act"], 1)

            def two(b, n=T):
                return b[:, 0:2 * n].rearrange("p (a b) -> p a b", a=2)

            act.dma_start(cols[:, :], small["cols"]).then_inc(cols_landed, 16)
            act.dma_start(X[:, :, :], small["x"]).then_inc(x_landed, 16)
            act.dma_start(ctx_in, small["ctx"]).then_inc(ctx_landed, 16)
            act.dma_start(decay_in, small["decay"]).then_inc(decay_landed, 16)
            act.dma_start(consts[:, :], small["consts"]).then_inc(consts_landed, 16)
            spare = stat[:, 63:64]
            act.wait_ge(silu_ready, 1)
            act.wait_ge(cols_landed, 16)
            f(silu_c[:, 0:24], cols[:, 0:24], ACT.Silu).then_inc(silu_ready, 1)
            act.wait_ge(x_landed, 16)
            f(sq_0[:, :, 0:T], X[:, :, :], ACT.Square).then_inc(sq_x, 1)

            def step_sum_sq(ni):
                f(spare[:, 0:1], spare[:, 0:1], ACT.Sqrt)
                for p in range(4 if ni else 0):
                    if ni in X_JOBS:
                        act.wait_ge(emptied["dve"], JOBS[X_JOBS[ni][p]].emptied)
                    else:
                        act.wait_ge(x_final, 2 * p + 2)
                    f(SQ[:, 2 * p:2 * p + 2, :], X[:, 2 * p:2 * p + 2, :], ACT.Square).then_inc(sq_ready, 1)
                n = 2 * T if ni == 0 else T
                act.wait_ge(emptied["dve"], JOBS[("sum_sq", ni)].emptied)
                f(norm_t[:, 1, 0:n], norm_t[:, 0, 0:n], ACT.Sqrt).then_inc(std_ready, 1)

            def step_apply(ni):
                if ni == 2:
                    return
                done = H_COUNT[ni] - (16 if ni == 0 else 8)
                for k in range(KT):
                    act.wait_ge(h_scaled, done + (2 * k + 1 if ni == 0 else k + 1))
                    if ni >= 3:
                        f(r(H_HI[:, k, :]), H[:, k, 0:T], ACT.Identity, bias=shift_of(ni, k)).then_inc(h_ready, 1)
                        continue
                    if ni == 0:
                        f(r(hx_hi[:, k, :]), H[:, k, 0:T], ACT.Identity, bias=shift_of(ni, k)).then_inc(h_ready, 1)
                        act.wait_ge(h_scaled, 2 * k + 2)
                        f(r(hc_hi[:, k, :]), H[:, k, T:2 * T], ACT.Identity, bias=mod[:, k, 1:2]).then_inc(h_ready, 1)
                        continue
                    f(H[:, k, 0:T], H[:, k, 0:T], ACT.Identity, bias=shift_of(ni, k)).then_inc(h_ready, 1)

            def step_split(key):
                c, before = CHUNK_NO[key], SPLIT_PLACE[key][1]
                act.wait_ge(landed[slot_of(c)], 16 * landed_count(c))
                if before is not None:
                    act.wait_ge(chunk_used, CHUNK_NO[before] + 1)
                elif c >= FIRST_SECOND:
                    act.wait_ge(chunk_used, FIRST_SECOND)
                hi, lo = split_slots(key)
                f(r(hi), lo, ACT.Copy).then_inc(hi_ready, 1)

            def step_decay():
                act.wait_ge(sp_arg, 1)
                f(sp[:, 1, :], sp[:, 0, :], ACT.Exp, scale=-1.0).then_inc(sp_exp, 1)
                act.wait_ge(decay_landed, 16)
                for h in range(R_HEADS):
                    act.wait_ge(decay_arg, h + 1)
                    f(decay_m[:, h, 0:2, :], decay_m[:, h, 0:2, :], ACT.Exp, scale=-1.0)
                    f(decay_m[:, h, 2:4, :], decay_in[:, 1024:1536].rearrange("p (a b) -> p a b", a=2), ACT.Exp,
                      scale=sp[:, 7, h:h + 1])
                    if h >= 2:
                        act.wait_ge(decay_ready, h - 1)
                    f(ret_p[h % 2][:, 0:2, :], decay_in[:, 1536:2048].rearrange("p (a b) -> p a b", a=2), ACT.Exp,
                      scale=sp[:, 7, 4 + h:5 + h]).then_inc(decay_exp, 1)

            def step_kr(c):
                for j in range(2):
                    takes(f(k_r[:, 2 * c + j, :], job(("kr", c, j))[:, :], ACT.Copy), ("kr", c, j))

            def evac(name, dst, func=ACT.Copy, scale=1.0):
                def run(c):
                    takes(f(dst[:, 2 * c:2 * c + 2, :], two(job((name, c))), func, scale=scale), (name, c))
                return run

            def step_kvw():
                takes(f(k_w, job(("kvw", "k"))[:, :], ACT.Copy), ("kvw", "k"))

            def step_ret_o(h):
                takes(f(y_r[:, h, :], job(("ret_o", h))[:, 0:T], ACT.Copy), ("ret_o", h))

            def step_ret_mean(p):
                act.wait_ge(emptied["dve"], JOBS[("ret_mean", p)].emptied)
                f(ret_sq[:, 2 * p:2 * p + 2, :], y_r[:, 2 * p:2 * p + 2, :], ACT.Square).then_inc(ret_sq_ready, 1)

            def step_ret_var(p):
                act.wait_ge(emptied["dve"], JOBS[("ret_var", p)].emptied)
                f(rope_b if p else rope_a, rope_b if p else rope_a, ACT.Sqrt).then_inc(ret_std, 1)

            def step_att_s(u):
                na, hd, _ = att_unit(u)
                b = job(("att_s", u))
                act.wait_ge(max_ready, u + 1)
                if u >= BUFS:
                    act.wait_ge(job_done, JOBS[("att_t", u - BUFS)].no)
                s = 8 * (u % 4)
                i = f(probs[:, u % BUFS, :], b[:, :], ACT.Exp, bias=stat[:, s:s + 1], accum_out=stat[:, s + 1:s + 2])
                takes(i, ("att_s", u))
                if not na:
                    f(stat[:, s + 2:s + 3], col("sink", hd), ACT.Exp, bias=stat[:, s:s + 1]).then_inc(sink_ready, 1)

            def step_att_t(u):
                b = job(("att_t", u))
                i, qt = u // 2, u % 2
                if i >= 2:
                    act.wait_ge(job_done, JOBS[("att_o", i - 2)].no)
                takes(f(probs_t[i % 2][:, :, qt * P:(qt + 1) * P], b[:, :].rearrange("p (a b) -> p a b", a=4),
                        ACT.Copy), ("att_t", u))

            def step_tok_major(t, kq):
                f(r(h_tok[:, t, 512 * kq:512 * kq + 512]), job(("tok_major", t, kq))[:, :],
                  ACT.Copy).then_inc(tok_hi, 1)

            def step_router():
                b = job(("router",))
                act.wait_ge(aff_max, 1)
                for t in range(2):
                    i = f(aff[:, t, :], b[:, t * 16:t * 16 + 16], ACT.Exp, bias=stat[:, t:t + 1],
                          accum_out=stat[:, 2 + t:3 + t])
                takes(i, ("router",))

            def step_pick():
                takes(f(gate_b, job(("pick", "gate"))[:, :], ACT.Copy), ("pick", "gate"))

            def step_gather(k):
                if k % 2:
                    takes(f(x_e[:, k, 0:EXPERTS * CAP], job(("gather", k))[:, :], ACT.Copy), ("gather", k))

            def step_pick_t(t):
                takes(f(hot_t[:, :, t * P:(t + 1) * P], job(("pick_t", t))[:, :].rearrange("p (a b) -> p a b", a=4),
                        ACT.Copy), ("pick_t", t))

            def step_mod_row(blk):
                act.wait_ge(mod_done, blk + 1)
                if blk >= 3:
                    act.wait_ge(job_done, JOBS[("mod_out", blk - 2)].no)
                takes(f(mod_rows(blk), mods[:, :], ACT.Copy), ("mod_row", blk))

            def step_experts():
                with act.Fori(0, EXPERTS) as e:
                    act.wait_ge(gate_up_done, e + 1)
                    f(silu_g[64:P, :], bank[0][0:64, :], ACT.Silu).then_inc(silu_g_ready, 1)
                    act.wait_ge(hid_turned, e + 1)
                    f(hid_t.rearrange("p c n -> p (c n)"), bank[1][:, 0:256], ACT.Copy).then_inc(hid_t_ready, 1)

            def step_nkv(kv):
                b = two(job(("nkv", kv)))
                v = win_f[kv].rearrange("p (gp par) t -> p gp par t", par=2)
                f(v[0:64, :, 0, :], b[0:64, :, :], ACT.Copy)
                f(v[0:64, :, 1, :], b[64:128, :, :], ACT.Copy)
                f(v[64:128, :, 0, 0:T - 1], b[0:64, :, 1:T], ACT.Copy)
                takes(f(v[64:128, :, 1, 0:T - 1], b[64:128, :, 1:T], ACT.Copy), ("nkv", kv))

            def square_part(i, n):
                f(n_sq[:, i % 2, 0:n], qk[:, i * 512:i * 512 + n], ACT.Square).then_inc(n_sq_ready, 1)

            def step_nqk(i):
                act.wait_ge(emptied["dve"], JOBS[("nqk", i)].emptied)
                square_part(i, 512)

            def step_nnorm(i):
                n = 512 if i < 6 else 30
                if i == 6:
                    act.wait_ge(emptied["dve"], JOBS[("cmp_k",)].emptied)
                    square_part(6, 30)
                act.wait_ge(emptied["dve"], JOBS[("nnorm", i)].emptied)
                f(n_rs[:, i % 2, 0:n], n_rs[:, i % 2, 0:n], ACT.Sqrt).then_inc(n_std, 1)

            def step_ngate():
                takes(f(n_gate.rearrange("p t n -> p (t n)"), job(("ngate",))[:, 0:96], ACT.Sigmoid), ("ngate",))

            def step_cmp(kv, part):
                if part == 1:
                    takes(f(hid_c[:, kv, :, :], job(("cmp", kv))[:, 0:120].rearrange("p (a b) -> p a b", a=2),
                            ACT.Silu), ("cmp", kv))

            def step_cmp_s():
                act.wait_ge(cmp_arg, 1)
                v = cmp_p.rearrange("p t h c -> p (t h c)")
                f(v, v, ACT.Exp).then_inc(cmp_exp, 1)

            def step_nsa_s(u):
                qt = u % 2
                nk = P * (qt + 1)
                b = job(("nsa_s", u))
                act.wait_ge(n_max, u + 1)
                if u >= BUFS:
                    act.wait_ge(job_done, JOBS[("nsa_t", u - BUFS)].no)
                s = 8 * (u % 4)
                for br in range(2):
                    i = f(n_p[:, u % BUFS, br * nk:(br + 1) * nk], b[:, br * nk:(br + 1) * nk], ACT.Exp,
                          bias=stat[:, s + br:s + br + 1], accum_out=stat[:, s + 2 + br:s + 3 + br])
                takes(i, ("nsa_s", u))

            def step_nsa_t(u):
                h, qt = u // 2, u % 2
                b = job(("nsa_t", u))
                if h >= 2:
                    act.wait_ge(job_done, JOBS[("nsa_o", h - 2)].no)
                pt = n_pt[h % 2]
                if qt == 0:
                    f(cmp_pt[h % 2], b[0:N_CMP, 256:512], ACT.Copy)
                    i = f(pt[:, 0, :, 0:P], b[:, 0:256].rearrange("p (a b) -> p a b", a=2), ACT.Copy)
                else:
                    i = f(pt[:, :, :, P:T], b[:, :].rearrange("p (k a b) -> p k a b", k=2, a=2), ACT.Copy)
                takes(i, ("nsa_t", u))

            def step_ffn_in(l, i):
                b = job(("ffn_in", l, i))
                if i >= 2:
                    act.wait_ge(emptied["dve"], JOBS[("ffn_in", l, i - 2)].emptied)
                f(ffn_g[:, i % 2, :], b[:, 0:T], ACT.Silu).then_inc(ffn_silu, 1)

            def step_rnn_in(i):
                b = job(("rnn_in", i))
                f(gelu_g[:, i, :], b[:, 0:T], ACT.Gelu_apprx_tanh)
                takes(f(u_in[:, i, 3:T + 3], b[:, T:2 * T], ACT.Copy), ("rnn_in", i))

            own = [0]

            def step_rnn_gate(n):
                b = job(("rnn_gate", n))
                f(rec[:, n, :], b[:, 0:T], ACT.Sigmoid, bias=col("b_a", n)).then_inc(act_step, 1)
                own[0] += 1
                takes(f(inp[:, n, :], b[:, T:2 * T], ACT.Sigmoid, bias=col("b_x", n)), ("rnn_gate", n))

            def step_rnn_decay(g):
                tiles, at = RNN_GROUPS[g], own[0]
                act.wait_ge(act_step, at)
                act.wait_ge(conv_ready, tiles[-1] + 1)
                for i in tiles:
                    f(thr[:, i, :], rec[:, i, :], ACT.Tanh, scale=sp[:, 6, 8 + i:9 + i]).then_inc(act_step, 1)
                    own[0] += 1
                for n, i in enumerate(tiles):
                    act.wait_ge(act_step, at + n + 1)
                    f(rec[:, i, :], rec[:, i, :], ACT.Exp, scale=sp[:, 7, 8 + i:9 + i]).then_inc(rnn_tanh, 1)

            def step_rnn_scan(g):
                for i in RNN_GROUPS[g]:
                    act.wait_ge(rnn_sqrt_in, i + 1)
                    f(thr[:, i, :], thr[:, i, :], ACT.Sqrt).then_inc(rnn_sqrt, 1)

            parts = {"sum_sq": step_sum_sq, "apply": step_apply, "split": step_split, "decay": step_decay, "kr": step_kr,
                     "qr": evac("qr", q_r), "gr": evac("gr", g_r, ACT.Silu), "kvw": step_kvw,
                     "qw": evac("qw", q_w, scale=0.125), "qn": evac("qn", q_n, scale=0.125),
                     "gate": evac("gate", gates, ACT.Sigmoid), "ret_o": step_ret_o, "ret_mean": step_ret_mean,
                     "ret_var": step_ret_var, "att_s": step_att_s, "att_t": step_att_t, "tok_major": step_tok_major,
                     "router": step_router, "pick": step_pick, "gather": step_gather, "pick_t": step_pick_t,
                     "experts": step_experts, "mod_row": step_mod_row, "nkv": step_nkv, "nqk": step_nqk,
                     "nnorm": step_nnorm, "ngate": step_ngate, "cmp": step_cmp, "cmp_s": step_cmp_s,
                     "nsa_s": step_nsa_s, "nsa_t": step_nsa_t, "ffn_in": step_ffn_in, "rnn_in": step_rnn_in,
                     "rnn_gate": step_rnn_gate, "rnn_decay": step_rnn_decay, "rnn_scan": step_rnn_scan}
            for name, *args in STEPS:
                if name in parts:
                    parts[name](*args)

        @block.vector
        def _(dve):
            v = nc.vector
            steps = [0]

            def link(i):
                steps[0] += 1
                i.then_inc(dve_step, 1)
                dve.wait_ge(dve_step, steps[0])

            def job(name):
                dve.wait_ge(job_done, JOBS[name].no)
                return bank[JOBS[name].bank]

            def takes(i, name):
                assert JOBS[name].engine == "dve"
                i.then_inc(emptied["dve"], 1)

            def taken(name):
                dve.wait_ge(emptied[JOBS[name].engine], JOBS[name].emptied)

            def two(b, n=T):
                return b[:, 0:2 * n].rearrange("p (a b) -> p a b", a=2)

            def over(a, n):
                return a.unsqueeze(1).to_broadcast([a.shape[0], n, a.shape[1]])

            def each(a, n):
                return a.unsqueeze(2).to_broadcast([a.shape[0], a.shape[1], n])

            dve.wait_ge(ctx_landed, 16)
            v.tensor_tensor(sq_0[:, :, T:2 * T], ctx_in, ctx_in, ALU.mult).then_inc(sq_ctx, 1)

            def step_sum_sq(ni):
                n = 2 * T if ni == 0 else T
                b = job(("sum_sq", ni))
                takes(v.tensor_scalar(norm_t[:, 0, 0:n], b[:, 0:n], 1.0 / D, EPS, ALU.mult, ALU.add), ("sum_sq", ni))
                finish_std(ni)

            def finish_std(ni):
                n = 2 * T if ni == 0 else T
                dve.wait_ge(std_ready, ni + 1)
                link(v.reciprocal(norm_t[:, 0, 0:n], norm_t[:, 1, 0:n]))

            def step_apply(ni):
                if ni == 2:
                    for k in range(KT):
                        v.scalar_tensor_tensor(X[:, k, :], X[:, k, :], col("g_final", k), norm_t[:, 0, 0:T], ALU.mult,
                                               ALU.mult).then_inc(x_final, 1)
                    dve.wait_ge(x_final, 8)
                    return

                parts = [(X, mod_a[:, ni, :], norm_t[:, 0, 0:T], H[:, :, 0:T], lambda k: shift_of(ni, k),
                          H_HI if ni else hx_hi)]
                if ni == 0:
                    parts.append((ctx_in, mod_a[:, 2, :], norm_t[:, 0, T:2 * T], H[:, :, T:2 * T],
                                  lambda k: mod[:, k, 1:2], hc_hi))
                tiles = [(k,) + x for k in range(KT) for x in parts]

                def lower(i):
                    k, _, _, _, h, shift, hi = tiles[i]
                    dve.wait_ge(h_ready, H_COUNT[ni] - len(tiles) + 1 + i)
                    v.scalar_tensor_tensor(r(h[:, k, :]), h[:, k, :], shift(k), r(hi[:, k, :]), ALU.add,
                                           ALU.subtract).then_inc(h_split, 1)

                ahead = 2
                for i, (k, x, gain, rstd, h, _, _) in enumerate(tiles):
                    v.scalar_tensor_tensor(h[:, k, :], x[:, k, :], gain[:, k:k + 1], rstd, ALU.mult,
                                           ALU.mult).then_inc(h_scaled, 1)
                    if ni != 1 and i >= ahead:
                        lower(i - ahead)
                for i in range(len(tiles) - ahead, len(tiles) if ni != 1 else 0):
                    lower(i)

            def step_split(key):
                dve.wait_ge(hi_ready, SPLIT_NO[key] + 1)
                hi, lo = split_slots(key)
                v.tensor_tensor(r(lo), lo, r(hi), ALU.subtract).then_inc(lo_ready, 1)

            def step_decay():
                dve.wait_ge(cols_landed, 16)
                a = cols[:, COLS["decays"][0]:COLS["decays"][0] + 19]
                link(v.tensor_scalar(sp[:, 2, :], a, -1.0, None, ALU.mult))
                v.tensor_tensor(sp[:, 0, :], a, sp[:, 2, :], ALU.max).then_inc(sp_arg, 1)
                dve.wait_ge(sp_exp, 1)
                link(v.tensor_scalar(sp[:, 3, :], sp[:, 1, :], 2.0, None, ALU.add))
                link(v.reciprocal(sp[:, 3, :], sp[:, 3, :]))
                link(v.tensor_tensor(sp[:, 3, :], sp[:, 3, :], sp[:, 1, :], ALU.mult))
                link(v.tensor_tensor(sp[:, 4, :], sp[:, 3, :], sp[:, 3, :], ALU.mult))
                link(v.tensor_scalar(sp[:, 5, :], sp[:, 4, :], 1.0 / 17, None, ALU.mult))
                for odd in (15, 13, 11, 9, 7, 5, 3):
                    link(v.scalar_tensor_tensor(sp[:, 5, :], sp[:, 5, :], 1.0 / odd, sp[:, 4, :], ALU.add, ALU.mult))
                link(v.scalar_tensor_tensor(sp[:, 5, :], sp[:, 5, :], 1.0, sp[:, 3, :], ALU.add, ALU.mult))
                link(v.tensor_scalar(sp[:, 2, :], sp[:, 2, :], 0.0, None, ALU.max))
                link(v.scalar_tensor_tensor(sp[:, 6, :], sp[:, 5, :], 2.0, sp[:, 2, :], ALU.mult, ALU.add))
                link(v.tensor_scalar(sp[:, 6, 8:19], sp[:, 6, 8:19], 8.0, None, ALU.mult))
                link(v.tensor_scalar(sp[:, 7, :], sp[:, 6, :], -1.0, None, ALU.mult))
                dve.wait_ge(decay_landed, 16)
                for h in range(R_HEADS):
                    d = decay_m[:, h, 0:2, :].rearrange("p a b -> p (a b)")
                    link(v.tensor_scalar(d, decay_in[:, 0:512], sp[:, 6, h:h + 1], None, ALU.mult))
                    v.scalar_tensor_tensor(d, decay_in[:, 512:1024], sp[:, 6, 4 + h:5 + h], d, ALU.mult,
                                           ALU.add).then_inc(decay_arg, 1)
                for h in range(R_HEADS):
                    dve.wait_ge(decay_exp, h + 1)
                    v.tensor_tensor(decay_m[:, h, 2:4, :], decay_m[:, h, 2:4, :], ret_p[h % 2][:, 0:2, :],
                                    ALU.add).then_inc(decay_ready, 1)

            def gain_of(ni):
                name, at = NORM_GAIN[ni]
                return col(name, at, 8)

            def step_mod_out(blk):
                b = job(("mod_out", blk))[:, :].rearrange("p (i j r) -> p j i r", i=4, j=4)
                if blk < 3:
                    dst = mod[:, 16 * blk:16 * blk + 16, :].rearrange("p (j i) m -> p j i m", j=4)
                    bias = col("b_mod", 16 * blk, 16).rearrange("p (j i) -> p j i", j=4)
                    for m in range(2):
                        o = v.tensor_tensor(dst[:, :, :, m], b[:, :, :, m], bias, ALU.add)
                else:
                    at = 16 * (blk - 3)
                    o = v.tensor_tensor(mod2[:, at:at + 16].rearrange("p (j i) -> p j i", j=4), b[:, :, :, 0],
                                        col("ada_b", at, 16).rearrange("p (j i) -> p j i", j=4), ALU.add)
                takes(o, ("mod_out", blk))
                taken(("mod_out", blk))
                if blk == 0:
                    link(v.scalar_tensor_tensor(mod_a[:, 0, :], mod[:, 8:16, 0], 1.0, gain_of(0), ALU.add, ALU.mult))
                    link(v.scalar_tensor_tensor(mod_a[:, 2, :], mod[:, 8:16, 1], 1.0, gain_of(0), ALU.add, ALU.mult))
                elif blk == 2:
                    link(v.scalar_tensor_tensor(mod_a[:, 1, :], mod[:, 32:40, 0], 1.0, gain_of(1), ALU.add, ALU.mult))
                elif blk in (LAST_BLOCKS - 1, MOD_BLOCKS - 1):
                    for ni in (3, 4) if blk == LAST_BLOCKS - 1 else (5, 6):
                        at = SHIFT2[ni] + 8
                        link(v.scalar_tensor_tensor(mod_a[:, ni, :], mod2[:, at:at + 8], 1.0, gain_of(ni), ALU.add,
                                                    ALU.mult))

            def rope(name, dst, n, size):
                b = job(name)
                cos, sin = const(f"cos{size}"), const(f"sin{size}")
                if n == 1:
                    c, s, ps = cos, sin, b[:, 0:T]
                    ta, tb = rope_a[:, 0, :], rope_b[:, 0, :]
                else:
                    c, s, ps = over(cos, 2), over(sin, 2), two(b)
                    ta, tb = rope_a, rope_b
                takes(v.tensor_tensor(tb, ps, s, ALU.mult), name)
                link(v.tensor_tensor(ta, dst, c, ALU.mult))
                taken(name)
                v.tensor_tensor(dst, ta, tb, ALU.add).then_inc(roped, 1)
                rope_no[0] += 1
                dve.wait_ge(roped, rope_no[0])

            rope_no = [0]

            def step_rot(what, p):
                dst, n, size = {"kr": (k_r[:, 2 * p:2 * p + 2, 0:T], 2, 128), "qr": (q_r[:, 2 * p:2 * p + 2, :], 2, 128),
                                "kw": (k_w[:, 0:T], 1, 64), "qw": (q_w[:, 2 * p:2 * p + 2, :], 2, 64)}[what]
                if what == "kr" and p == 0:
                    dve.wait_ge(consts_landed, 16)
                rope(("rot", what, p), dst, n, size)

            def values(name, dst):
                def run(c):
                    for i in range(2):
                        takes(v.tensor_copy(dst[:, 2 * i:2 * i + 2, c * T:(c + 1) * T], two(job((name, c, i)))),
                              (name, c, i))
                return run

            def step_kvw():
                takes(v.tensor_copy(v_w, job(("kvw", "v"))[:, :].rearrange("p (a b) -> p a b", a=4)), ("kvw", "v"))

            def step_kn(c):
                for j in range(2):
                    takes(v.tensor_copy(k_n[:, 2 * c + j, :], job(("kn", c, j))[:, :]), ("kn", c, j))

            def step_ret_s(h, kp):
                b = job(("ret_s", h, kp))
                if h >= 2 and kp == 0:
                    dve.wait_ge(job_done, JOBS[("ret_o", h - 2)].no)
                takes(v.scalar_tensor_tensor(ret_p[h % 2][:, 2 * kp:2 * kp + 2, :], two(b), float(P) ** -0.5,
                                             decay_m[:, h, 2 * kp:2 * kp + 2, :], ALU.mult, ALU.mult), ("ret_s", h, kp))

            def step_ret_mean(p):
                y = y_r[:, 2 * p:2 * p + 2, :]
                takes(v.scalar_tensor_tensor(y, two(job(("ret_mean", p))), -1.0 / P, y, ALU.mult, ALU.add),
                      ("ret_mean", p))

            def step_ret_var(p):
                t = rope_b if p else rope_a
                b = job(("ret_var", p))
                takes(v.tensor_scalar(t, two(b), 1.0 / P, EPS, ALU.mult, ALU.add), ("ret_var", p))
                dve.wait_ge(ret_std, p + 1)
                link(v.reciprocal(t, t))
                y = y_r[:, 2 * p:2 * p + 2, :]
                link(v.tensor_tensor(y, y, t, ALU.mult))
                for h in (2 * p, 2 * p + 1):
                    link(v.scalar_tensor_tensor(y_r[:, h, :], y_r[:, h, :], col("ret_gn", h), g_r[:, h, :], ALU.mult,
                                                ALU.mult))
                hi = y_r_hi[:, 2 * p:2 * p + 2, :]
                link(v.tensor_copy(r(hi), y))
                v.tensor_tensor(r(y), y, r(hi), ALU.subtract).then_inc(ret_ready, 1)

            def step_att_s(u):
                na, hd, qt = att_unit(u)
                b = job(("att_s", u))
                if u == 16:
                    dve.wait_ge(bias_ready, 1)
                if na:
                    m = bias_n[:, hd, qt, :]
                else:
                    m = const("win_mask")[:, qt * T:(qt + 1) * T]
                link(v.tensor_tensor(b[:, 0:T], b[:, 0:T], m, ALU.add))
                s = 8 * (u % 4)
                if na:
                    v.tensor_reduce(stat[:, s:s + 1], b[:, :], AX, ALU.max, negate=True).then_inc(max_ready, 1)
                else:
                    link(v.tensor_reduce(stat[:, s + 3:s + 4], b[:, :], AX, ALU.max))
                    v.tensor_scalar(stat[:, s:s + 1], stat[:, s + 3:s + 4], col("sink", hd), -1.0, ALU.max,
                                    ALU.mult).then_inc(max_ready, 1)

            def step_att_n(u):
                na = att_unit(u)[0]
                s = 8 * (u % 4)
                taken(("att_s", u))
                if not na:
                    dve.wait_ge(sink_ready, u + 1)
                    link(v.tensor_tensor(stat[:, s + 1:s + 2], stat[:, s + 1:s + 2], stat[:, s + 2:s + 3], ALU.add))
                link(v.reciprocal(stat[:, s + 4:s + 5], stat[:, s + 1:s + 2]))
                v.tensor_scalar(probs[:, u % BUFS, :], probs[:, u % BUFS, :], stat[:, s + 4:s + 5], None,
                                ALU.mult).then_inc(probs_ready, 1)

            def step_att_o(i):
                na, hd, _ = att_unit(2 * i)
                t, half = att_head(na, hd)
                rows = slice(64 * half, 64 * half + 64)
                hi, lo = ((y_n, y_n_lo) if na else (y_w, y_w_lo))
                b = job(("att_o", i))[rows, 0:T]
                link(v.tensor_copy(r(hi[rows, t, :]), b))
                takes(v.tensor_tensor(r(lo[rows, t, :]), b, r(hi[rows, t, :]), ALU.subtract), ("att_o", i))

            def step_branch(ch, br):
                if ch == 0 and br == 0:
                    taken(("gate", 11))
                for p in range(2):
                    name = ("branch", ch, br, p)
                    at = 4 * ch + 2 * p
                    g = gates[:, 8 * br + at:8 * br + at + 2, :]
                    takes(v.tensor_tensor(g, g, two(job(name)), ALU.mult), name)
                taken(name)
                for p in range(2 if br else 0):
                    at = 4 * ch + 2 * p
                    m = merged[:, at:at + 2, :]
                    if br == 1:
                        link(v.tensor_tensor(m, gates[:, at:at + 2, :], gates[:, 8 + at:10 + at, :], ALU.add))
                    else:
                        link(v.tensor_tensor(m, m, gates[:, 16 + at:18 + at, :], ALU.add))
                        hi = merged_hi[:, at:at + 2, :]
                        link(v.tensor_copy(r(hi), m))
                        v.tensor_tensor(r(m), m, r(hi), ALU.subtract).then_inc(merged_ready, 1)

            def add_to_x(name, gain, at):
                b = job(name)
                for j in range(2):
                    i = v.scalar_tensor_tensor(X[:, at + j, :], b[:, j * T:(j + 1) * T], gain(at + j), X[:, at + j, :],
                                               ALU.mult, ALU.add)
                takes(i, name)
                taken(name)

            def step_mix_out(c):
                add_to_x(("mix_out", c), lambda n: mod[:, 16 + n, 0:1], 2 * c)

            def step_tok_major(t, kq):
                dve.wait_ge(tok_hi, 2 * t + kq + 1)
                at = slice(512 * kq, 512 * kq + 512)
                takes(v.tensor_tensor(r(h_tok_lo[:, t, at]), job(("tok_major", t, kq))[:, :], r(h_tok[:, t, at]),
                                      ALU.subtract), ("tok_major", t, kq))

            def step_router():
                b = job(("router",))
                v.tensor_reduce(stat[:, 0:2], b[:, 0:32].rearrange("p (t e) -> p t e", t=2), AX, ALU.max,
                                negate=True).then_inc(aff_max, 1)
                taken(("router",))
                link(v.reciprocal(stat[:, 4:6], stat[:, 2:4]))
                v.tensor_tensor(aff, aff, each(stat[:, 4:6], 16), ALU.mult).then_inc(aff_ready, 1)

            def step_affinity():
                takes(v.tensor_copy(aff_t, job(("affinity",))[0:16, 0:T]), ("affinity",))
                taken(("affinity",))
                for r in range(4):
                    link(v.max(top_v[:, 8 * r:8 * r + 8], aff_t))
                    link(v.max_index(top_i[:, 8 * r:8 * r + 8], top_v[:, 8 * r:8 * r + 8], aff_t))
                    if r < 3:
                        link(v.match_replace(aff_t, top_v[:, 8 * r:8 * r + 8], aff_t, -1.0))
                link(v.tensor_copy(top_f, top_i[:, :]))
                own = const("own", 16).rearrange("p (e c) -> p e c", e=16)
                link(v.tensor_tensor(spread_i, own, over(top_f, 16), ALU.mult))
                v.tensor_tensor(spread_g, own, over(top_v, 16), ALU.mult).then_inc(spread_ready, 1)

            def step_pick():
                b = job(("pick", "idx"))
                for t in range(2):
                    i = v.tensor_scalar(r(hot[:, t, :]), b[:, :], const("token")[:, t:t + 1], None, ALU.is_equal)
                takes(i, ("pick", "idx"))

            def step_gather(k):
                if k % 2 == 0:
                    takes(v.tensor_copy(x_e[:, k, 0:EXPERTS * CAP], job(("gather", k))[:, :]), ("gather", k))

            def step_experts():
                taken(("gather", 7))
                taken(("gather", 6))
                xe = x_e.rearrange("p k (e c) -> p k e c", c=CAP)
                link(v.memset(xe[:, :, EXPERTS, :], 0.0))
                v.tensor_copy(x_cur, xe[:, :, 0, :]).then_inc(x_cur_ready, 1)
                dve.sem_inc(ye_taken, 1)
                with dve.Fori(0, EXPERTS // 4) as i:
                    for u in range(4):
                        dve.wait_ge(silu_g_ready, i * 4 + (u + 1))
                        v.tensor_tensor(hid[64:P, :], silu_g[64:P, :], bank[0][64:P, :], ALU.mult).then_inc(hid_ready, 1)
                        nxt = xe[:, :, 0:16, :].rearrange("p k (i u) c -> p k i u c", u=4)[:, :, i, u + 1, :] if u < 3 else \
                            xe[:, :, 1:17, :].rearrange("p k (i u) c -> p k i u c", u=4)[:, :, i, 3, :]
                        v.tensor_copy(x_cur, nxt).then_inc(x_cur_ready, 1)
                        dve.wait_ge(down_done, i * 4 + (u + 1))
                        for j in range(4):
                            o = v.tensor_copy(y_tok[32 * u:32 * u + 32, i, j * T:(j + 1) * T],
                                              bank[2][32 * j:32 * j + 32, 0:T])
                        o.then_inc(ye_taken, 1)

            def step_pick_t(t):
                if t == 0:
                    taken(("pick", "gate"))
                    taken(("pick", "idx"))
                    v.tensor_tensor(hot_g, r(hot), over(gate_b, 2), ALU.mult).then_inc(hot_g_ready, 1)

            def step_combine(p):
                add_to_x(("combine", p), lambda n: mod[:, 40 + n, 0:1], 2 * p)

            def step_nkv(kv):
                taken(("nkv", kv))
                f4 = win_f[kv]
                for half in range(2):
                    rows = slice(64 * half, 64 * half + 64)
                    for g in range(4):
                        src = f4[rows, g, 0:240].rearrange("p (c j l) -> p j c l", c=15, l=2)[:, :, :, 0]
                        pos = col("pos", 16 * kv, 16)[rows]
                        i = v.tensor_tensor(flat[kv][rows, 0:8, g, :], src, each(pos[:, 0:8], 15), ALU.add)
                        src = f4[rows, g, 16:256].rearrange("p (c j l) -> p j c l", c=15, l=2)[:, :, :, 0]
                        i = v.tensor_tensor(flat[kv][rows, 8:16, g, :], src, each(pos[:, 8:16], 15), ALU.add)
                i.then_inc(flat_ready, 1)

            def step_nqk(i):
                takes(v.tensor_copy(qk[:, i * 512:(i + 1) * 512], job(("nqk", i))[:, :]), ("nqk", i))

            def step_nnorm(i):
                n = 512 if i < 6 else 30
                b = job(("nnorm", i))
                rs = n_rs[:, i % 2, 0:n]
                takes(v.tensor_scalar(rs, b[:, 0:n], 1.0 / 64, EPS, ALU.mult, ALU.add), ("nnorm", i))
                dve.wait_ge(n_std, i + 1)
                link(v.reciprocal(rs, rs))
                gain = (col("k_gain", 1), col("k_gain", 2))[i] if i < 2 else (
                    stat[:, 40:41] if i < 6 else col("k_gain", 0))
                if i == 2:
                    link(v.tensor_scalar(stat[:, 40:41], col("q_gain"), 0.125, None, ALU.mult))
                z = qk[:, i * 512:i * 512 + n]
                v.scalar_tensor_tensor(z, z, gain, rs, ALU.mult, ALU.mult).then_inc(n_normed, 1)

            def step_nsa_parts():
                v.tensor_copy(r(ident_1), ident)
                v.tensor_copy(r(causal_1), const("causal")).then_inc(mask_ready, 1)
                link(v.tensor_copy(r(wide_hi), wide[:, :, 16:64]))
                v.tensor_tensor(r(wide_lo), wide[:, :, 16:64], r(wide_hi), ALU.subtract).then_inc(wide_split, 1)

            def step_nv(i):
                takes(v.tensor_copy(v_s[i], two(job(("nv", i)))), ("nv", i))

            def step_cmp_k():
                takes(v.tensor_copy(qk[:, 3072:3102], job(("cmp_k",))[:, 0:30]), ("cmp_k",))

            def step_cmp_v():
                takes(v.tensor_copy(v_c, job(("cmp_v",))[0:N_CMP, 0:256].rearrange("p (a b) -> p a b", a=4)), ("cmp_v",))

            def step_cmp_s():
                add = const("cmp_add").rearrange("p (t c) -> p t c", t=2)
                keep = const("cmp_keep").rearrange("p (t c) -> p t c", t=2)
                for half in range(2):
                    ps = job(("cmp_s", half))[:, 0:240].rearrange("p (t q c) -> p t q c", t=2, q=8)
                    for t in range(2):
                        for gp in range(2):
                            h = 4 * (2 * gp + half)
                            i = v.tensor_tensor(cmp_p[:, t, h:h + 4, :], ps[:, t, 4 * gp:4 * gp + 4, :],
                                                over(add[:, t, :], 4), ALU.add)
                    takes(i, ("cmp_s", half))
                taken(("cmp_s", 1))
                link(v.tensor_reduce(cmp_m, cmp_p, AX, ALU.max))
                for t in range(2):
                    i = v.tensor_tensor(cmp_p[:, t, :, :], cmp_p[:, t, :, :], each(cmp_m[:, t, :], 15), ALU.subtract)
                i.then_inc(cmp_arg, 1)
                dve.wait_ge(cmp_exp, 1)
                for t in range(2):
                    link(v.tensor_tensor(cmp_p[:, t, :, :], cmp_p[:, t, :, :], over(keep[:, t, :], 16), ALU.mult))
                link(v.tensor_reduce(cmp_m, cmp_p, AX, ALU.add))
                link(v.tensor_scalar(cmp_m, cmp_m, TINY, None, ALU.max))
                link(v.reciprocal(cmp_m, cmp_m))
                taken(("ngate",))
                g = n_gate.rearrange("p t (h b) -> p t h b", b=3)
                link(v.tensor_tensor(cmp_m, cmp_m, g[:, :, :, 0], ALU.mult))
                for t in range(2):
                    i = v.tensor_tensor(cmp_p[:, t, :, :], cmp_p[:, t, :, :], each(cmp_m[:, t, :], 15), ALU.mult)
                i.then_inc(cmp_ready, 1)

            def step_nsa_s(u):
                qt = u % 2
                nk = P * (qt + 1)
                b = two(job(("nsa_s", u)), nk)
                s = 8 * (u % 4)
                v.tensor_reduce(stat[:, s:s + 2], b, AX, ALU.max, negate=True).then_inc(n_max, 1)

            def step_nsa_n(u):
                h, qt = u // 2, u % 2
                nk = P * (qt + 1)
                s = 8 * (u % 4)
                taken(("nsa_s", u))
                link(v.reciprocal(stat[:, s + 4:s + 6], stat[:, s + 2:s + 4]))
                link(v.tensor_tensor(stat[:, s + 4:s + 6], stat[:, s + 4:s + 6], n_gate[:, qt, 3 * h + 1:3 * h + 3],
                                     ALU.mult))
                z = n_p[:, u % BUFS, 0:2 * nk].rearrange("p (a b) -> p a b", a=2)
                v.tensor_tensor(z, z, each(stat[:, s + 4:s + 6], nk), ALU.mult).then_inc(n_ready, 1)

            def step_nsa_o(h):
                qi, half, _ = nsa_head(h)
                rows = slice(64 * half, 64 * half + 64)
                b = job(("nsa_o", h))[rows, 0:T]
                link(v.tensor_copy(r(o_n[rows, qi, :]), b))
                takes(v.tensor_tensor(r(o_lo[rows, qi, :]), b, r(o_n[rows, qi, :]), ALU.subtract), ("nsa_o", h))

            def step_nsa_out(c):
                add_to_x(("nsa_out", c), lambda n: mod2[:, 16 + n:17 + n], 2 * c)

            def step_ffn_in(l, i):
                b = job(("ffn_in", l, i))
                dve.wait_ge(ffn_silu, FFN_T * l + i + 1)
                p = ffn_p[:, i % 2, :]
                link(v.tensor_tensor(p, ffn_g[:, i % 2, :], b[:, T:2 * T], ALU.mult))
                link(v.tensor_copy(r(ffn_h[:, i, :]), p))
                takes(v.tensor_tensor(r(ffn_lo[:, i, :]), p, r(ffn_h[:, i, :]), ALU.subtract), ("ffn_in", l, i))

            def step_ffn_add(l):
                for p in range(4):
                    add_to_x(("ffn_add", l, p), lambda n: mod2[:, 48 * l + 40 + n:48 * l + 41 + n], 2 * p)

            def step_rnn_in(i):
                if i == 0:
                    link(v.memset(u_in[:, :, 0:3], 0.0))
                taken(("rnn_in", i))
                link(v.tensor_scalar(u_c[:, i, :], u_in[:, i, 0:T], col("conv_w", i), col("conv_b", i), ALU.mult,
                                     ALU.add))
                for k in range(1, 4):
                    j = v.scalar_tensor_tensor(u_c[:, i, :], u_in[:, i, k:k + T], col("conv_w", 11 * k + i), u_c[:, i, :],
                                               ALU.mult, ALU.add)
                    if k < 3:
                        link(j)
                j.then_inc(conv_ready, 1)

            def step_rnn_decay(g):
                for i in RNN_GROUPS[g]:
                    dve.wait_ge(rnn_tanh, i + 1)
                    link(v.tensor_tensor(rnn_d[:, i % 2, :], rec[:, i, :], rec[:, i, :], ALU.mult))
                    v.scalar_tensor_tensor(thr[:, i, :], rnn_d[:, i % 2, :], 1.0, thr[:, i, :], ALU.add,
                                           ALU.mult).then_inc(rnn_sqrt_in, 1)

            def step_rnn_scan(g):
                for i in RNN_GROUPS[g]:
                    dve.wait_ge(rnn_sqrt, i + 1)
                    dve.wait_ge(rnn_gated, i + 1)
                    link(v.tensor_tensor(inp[:, i, :], inp[:, i, :], thr[:, i, :], ALU.mult))
                    dve.wait_ge(job_done, JOBS[("rnn_gate", min(i + 1, RNN_T - 1))].no)
                    link(v.tensor_tensor_scan(u_c[:, i, :], rec[:, i, :], inp[:, i, :], 0.0, ALU.mult, ALU.add))
                    link(v.tensor_tensor(u_c[:, i, :], gelu_g[:, i, :], u_c[:, i, :], ALU.mult))
                    link(v.tensor_copy(r(gelu_g[:, i, :]), u_c[:, i, :]))
                    v.tensor_tensor(r(u_c[:, i, :]), u_c[:, i, :], r(gelu_g[:, i, :]), ALU.subtract).then_inc(rnn_ready, 1)

            def step_rnn_add():
                for p in range(4):
                    add_to_x(("rnn_add", p), lambda n: mod2[:, 48 + 16 + n:48 + 17 + n], 2 * p)

            parts = {"sum_sq": step_sum_sq, "apply": step_apply, "split": step_split, "decay": step_decay,
                     "mod_out": step_mod_out,
                     "rot": step_rot, "vr": values("vr", v_r), "vn": values("vn", v_n), "kvw": step_kvw, "kn": step_kn,
                     "ret_s": step_ret_s, "ret_mean": step_ret_mean, "ret_var": step_ret_var, "att_s": step_att_s,
                     "att_n": step_att_n, "att_o": step_att_o, "branch": step_branch, "mix_out": step_mix_out,
                     "tok_major": step_tok_major, "router": step_router, "affinity": step_affinity, "pick": step_pick,
                     "gather": step_gather, "pick_t": step_pick_t, "experts": step_experts, "combine": step_combine,
                     "nkv": step_nkv, "nqk": step_nqk, "nnorm": step_nnorm, "nv": step_nv, "nsa_parts": step_nsa_parts,
                     "cmp_k": step_cmp_k,
                     "cmp_v": step_cmp_v, "cmp_s": step_cmp_s, "nsa_s": step_nsa_s, "nsa_n": step_nsa_n,
                     "nsa_o": step_nsa_o, "nsa_out": step_nsa_out, "ffn_in": step_ffn_in, "ffn_add": step_ffn_add,
                     "rnn_in": step_rnn_in, "rnn_decay": step_rnn_decay, "rnn_scan": step_rnn_scan,
                     "rnn_add": step_rnn_add}
            for name, *args in STEPS:
                if name in parts:
                    parts[name](*args)


W_IN = {"qr": 0, "kr": 512, "vr": 1024, "gr": 1536, "qw": 2048, "kw": 2560, "vw": 2688, "qn": 2816, "kn": 3328,
        "vn": 3840, "gate": 4352}
WIN_ORDER = [0, 4, 1, 5, 2, 6, 3, 7]
NSA_ORDER = [4 * (2 * gp + half) + t for gp in range(2) for t in range(4) for half in range(2)]


def weight_stream(np, i):
    w = np.zeros((len(CHUNKS), P, CHUNK), np.float32)
    head = [h * 64 + d for h in WIN_ORDER for d in range(64)]
    nsa_head = [h * 64 + d for h in NSA_ORDER for d in range(64)]
    w_in, nsa_in = i["w_in"][0], i["nsa_w_in_2"][0]
    rg = np.zeros((2, RNN_T * P, RNN_T * P), np.float32)
    for g, name in enumerate(("rg_w_a_2", "rg_w_x_2")):
        for b in range(16):
            rg[g, 88 * b:88 * b + 88, 88 * b:88 * b + 88] = i[name][0][b]

    def cut(m, k):
        return m.reshape(k, P, -1).transpose(1, 0, 2).reshape(P, -1)

    for c, (name, *a) in enumerate(CHUNKS):
        if name == "mod":
            m = i["w_mod"][0] if a[0] < 3 else i["ada_w_2"][a[0] // 3 - 1]
            w[c] = m[P * a[1]:P * a[1] + P, a[0] % 3 * CHUNK:a[0] % 3 * CHUNK + CHUNK]
        elif name == "kvw":
            w[c] = cut(w_in[:, W_IN["kw"]:W_IN["kw"] + 256], 8)
        elif name == "qw":
            w[c] = cut(w_in[:, W_IN["qw"]:W_IN["qw"] + 512][:, head][:, 256 * a[0]:256 * a[0] + 256], 8)
        elif name in W_IN:
            n = W_IN[name] + 256 * a[0]
            w[c] = cut(w_in[:, n:n + 256], 8)
        elif name == "branch":
            m = (i["w_ret"][0], i["w_win"][0][head], i["w_na"][0])[a[1]]
            w[c] = cut(m[:, 512 * a[0]:512 * a[0] + 512], 4)
        elif name == "mix_out":
            w[c] = cut(i["w_out"][0][:, 256 * a[0]:256 * a[0] + 256], 8)
        elif name == "expert":
            e, n = a
            if n < 8:
                w[c, :, 0:D] = i["w_exp_gate"][0][e][P * n:P * n + P]
                w[c, :, D:] = i["w_exp_up"][0][e][P * n:P * n + P]
            else:
                w[c] = cut(i["w_exp_down"][0][e][256 * (n - 8):256 * (n - 7)], 2)
        elif name == "nkv":
            w[c] = cut(nsa_in[:, 1024 + 256 * a[0]:1280 + 256 * a[0]], 8)
        elif name == "nqk":
            m = nsa_in[:, 0:1024][:, nsa_head]
            cols = (nsa_in[:, 1536:1792], nsa_in[:, 2048:2304])[a[0]] if a[0] < 2 else \
                m[:, 256 * (a[0] - 2):256 * (a[0] - 1)]
            w[c] = cut(cols, 8)
        elif name == "nv":
            w[c] = cut(nsa_in[:, 1792 + 512 * a[0]:2048 + 512 * a[0]], 8)
        elif name == "cmp":
            w[c] = cut(i["nsa_cmp_w1_2"][0][a[0]][1024 * a[1]:1024 * a[1] + 1024], 8)
        elif name == "nsa_out":
            w[c] = cut(i["nsa_w_out_2"][0][nsa_head][:, 256 * a[0]:256 * a[0] + 256], 8)
        elif name in ("ffn_in", "rnn_in"):
            m = i["ffn_w_in_2"][a[0]] if name == "ffn_in" else i["rg_w_in_2"][0]
            half, n = m.shape[1] // 2, P * a[-1]
            w[c] = cut(np.concatenate([m[:, n:n + P], m[:, half + n:half + n + P]], axis=1), 8)
        elif name == "ffn_out":
            w[c] = cut(i["ffn_w_out_2"][a[0]][256 * a[1]:256 * a[1] + 256], 2)
        elif name == "rnn_out":
            m = i["rg_w_out_2"][0][256 * a[0]:256 * a[0] + 256]
            w[c, :, 0:m.shape[0] // P * D] = cut(m, m.shape[0] // P)
        elif name == "gates":
            for j, (n, g, k) in enumerate(GATE_TILES[16 * a[0]:16 * a[0] + 16]):
                w[c, :, j * P:(j + 1) * P] = rg[g, k * P:(k + 1) * P, n * P:(n + 1) * P]
    return w


def column_pack(np, i):
    def tiles(x):
        return x.reshape(-1, P).T

    def every(x):
        return np.broadcast_to(x.reshape(1, -1), (P, x.size))

    def twice(x):
        return np.concatenate([x, x], axis=-1).reshape(-1, P).T

    both = np.stack([i["c"][0].reshape(8, P), i["c_ctx"].reshape(8, P)], axis=1).reshape(16, P).T
    parts = {"c_both": both, "c_2": tiles(i["c_2"][0]), "b_mod": tiles(i["b_mod"][0]),
             "ada_b": tiles(i["ada_b_2"].reshape(-1)), "g_mix": tiles(i["g_mix"][0]), "g_ffn": tiles(i["g_ffn"][0]),
             "g_final": tiles(i["g_final"]), "norm1": tiles(i["norm1_g_2"].reshape(-1)),
             "norm2": tiles(i["norm2_g_2"].reshape(-1)), "ret_gn": tiles(i["ret_gn"][0]),
             "decays": every(i["ret_decay_logit"][0].reshape(-1)), "lam": tiles(i["rg_lam_2"][0]),
             "sink": every(i["win_sink"][0][WIN_ORDER]), "q_gain": twice(i["nsa_q_gain_2"][0]),
             "k_gain": twice(i["nsa_k_gain_2"][0]), "pos": tiles(i["nsa_cmp_pos_2"][0].reshape(-1)),
             "conv_w": tiles(i["rg_conv_w_2"][0].reshape(-1)), "conv_b": tiles(i["rg_conv_b_2"][0]),
             "b_a": tiles(i["rg_b_a_2"][0].reshape(-1)), "b_x": tiles(i["rg_b_x_2"][0].reshape(-1))}
    return np.ascontiguousarray(np.concatenate([parts[k] for k in COLS], axis=1))


def constant_pack(np):
    f = np.float32
    p, t = np.arange(P), np.arange(T)

    def rope(size):
        nf = size // 4
        inv = f(10000.0) ** (-np.arange(nf, dtype=f) / f(nf))
        ang = np.concatenate([(t // 64).astype(f)[:, None] * inv, (t % 64).astype(f)[:, None] * inv], axis=1)
        a = np.tile(ang.T, (P // (size // 2), 1))
        m = np.zeros((P, P), f)
        for base in range(0, P, size):
            for d in range(size // 2):
                m[base + d + size // 2, base + d] = -1
                m[base + d, base + d + size // 2] = 1
        return m, np.cos(a).astype(f), np.sin(a).astype(f)

    rot128, cos128, sin128 = rope(128)
    rot64, cos64, sin64 = rope(64)
    q2 = p[:, None, None] + P * np.arange(2)[None, :, None]
    k = t[None, None, :]
    win = np.where(np.abs(k - q2) <= 128, 0, NEG).reshape(P, -1)
    cq, ck = p % 64, t % 64
    start = np.clip(cq - 8, 0, 48)
    na = np.where((ck[None] >= start[:, None]) & (ck[None] < start[:, None] + 16), 0, NEG)
    ends = np.arange(N_CMP) * 16 + 31
    seen = ends[None, None, :] <= q2
    parts = {"ident": np.eye(P), "ones": np.ones((P, P)), "half_ones": np.kron(np.eye(2), np.ones((64, 64))),
             "rot128": rot128, "rot64": rot64, "cos128": cos128, "sin128": sin128, "cos64": cos64, "sin64": sin64,
             "win_mask": win, "na_mask": na, "causal": np.where(p[None] <= p[:, None], 0, NEG),
             "cmp_add": np.where(seen, 0, NEG).reshape(P, -1), "cmp_keep": seen.reshape(P, -1),
             "own": np.kron(np.eye(P)[:, 0:16], np.ones((1, 32))), "token": p[:, None] + P * np.arange(2)[None]}
    consts = np.concatenate([parts[n].astype(f) for n in CONSTS], axis=1)
    key = (p[:, None, None] + P * np.arange(2)[None, :, None])
    decay = np.concatenate([x.reshape(P, -1) for x in (np.maximum(k - key, 0), np.maximum(key - k, 0), k + T - key,
                                                       T - k + key)], axis=1)
    return consts, decay.astype(f)


def kernel(**inputs):
    import numpy as np
    import concourse.bacc as bacc
    from concourse.bass_utils import run_bass_kernel_spmd

    i = {k: np.asarray(x) for k, x in inputs.items()}
    consts, decay = constant_pack(np)

    def feature_major(x):
        return np.ascontiguousarray(x.T.reshape(8, P, T).transpose(1, 0, 2))

    rows = np.arange(4)
    ri = rows[None, :] - rows[:, None] + 7
    cc = np.arange(64)
    ci = np.clip(cc[None, :] - cc[:, None], -15, 15) + 15
    bias = i["na_rpb"][0][:, ri[:, None, :, None], ci[None, :, None, :]].reshape(8, 2, P, T)
    wide = np.concatenate([i["w_router"][0], i["nsa_w_in_2"][0][:, 2560:2608]], axis=1)
    arrays = {
        "w": weight_stream(np, i), "cols": column_pack(np, i), "consts": consts, "decay": decay,
        "x": feature_major(i["x"][0]), "ctx": feature_major(i["ctx"][0]),
        "bias": np.ascontiguousarray(bias.transpose(2, 0, 1, 3).reshape(P, -1)),
        "wide": np.ascontiguousarray(wide.reshape(8, P, 64).transpose(1, 0, 2)),
        "w2c": np.ascontiguousarray(i["nsa_cmp_w2_2"][0].reshape(2, 2, P, 64).transpose(2, 0, 1, 3)),
    }
    nc = bacc.Bacc("TRN2", target_bir_lowering=False, num_devices=1)
    aps = {n: nc.dram_tensor(f"in_{n}", a.shape, F32, kind="ExternalInput").ap() for n, a in arrays.items()}
    out = nc.dram_tensor("out_t", (P, KT, T), F32, kind="ExternalOutput").ap()
    build(nc, aps["w"], aps, out)
    r = run_bass_kernel_spmd(nc, [{f"in_{n}": a for n, a in arrays.items()}], core_ids=[0])
    y = r.results[0]["out_t"]
    return np.ascontiguousarray(y.transpose(2, 1, 0).reshape(1, T, D))
```
